# Optimizing a Trainium2 kernel written in Bass

```python
import math
import jax, jax.numpy as jnp
from jax import lax
import numpy as np

D_MODEL = 1024
BATCH = 1
SEQ = 256
DEPTH = 1

N_BRANCH = 4
BRANCH_W = D_MODEL // 2
DN_HEADS = 4
DN_DK = BRANCH_W // DN_HEADS
DN_DV = BRANCH_W // DN_HEADS
DN_CHUNK = 64
CONV_W = 4
GM_GROUPS = 4
GM_CH = BRANCH_W // GM_GROUPS
GM_CHUNK = 128
SW_HEADS = 8
SW_KV_HEADS = 2
SW_HD = BRANCH_W // SW_HEADS
SW_WINDOW = 128
SW_BLOCK = 128
MEM_LEN = 256
XM_HEADS = 4
XM_HD = BRANCH_W // XM_HEADS

EPS = 1e-6
NEG_INF = -1e30

IN_SPLITS = [
    3 * BRANCH_W,
    BRANCH_W,
    DN_HEADS,
    DN_HEADS,
    2 * BRANCH_W,
    BRANCH_W,
    SW_HEADS * SW_HD,
    SW_KV_HEADS * SW_HD,
    SW_KV_HEADS * SW_HD,
    BRANCH_W,
    XM_HEADS * XM_HD,
    BRANCH_W,
    N_BRANCH * D_MODEL,
]
D_IN = sum(IN_SPLITS)


def _rmsnorm(x, g):
    xf = x.astype(jnp.float32)
    y = xf * lax.rsqrt(jnp.mean(xf * xf, axis=-1, keepdims=True) + EPS)
    return (y * g.astype(jnp.float32)).astype(x.dtype)

def _l2norm(x):
    return x * lax.rsqrt(jnp.sum(x * x, axis=-1, keepdims=True) + EPS)

def _split_cols(cols):
    idx, acc = [], 0
    for s in IN_SPLITS[:-1]:
        acc += s
        idx.append(acc)
    return jnp.split(cols, idx, axis=-1)

def _causal_dwconv(x, w):
    c = x.shape[-1]
    return lax.conv_general_dilated(
        x, w[:, None, :].astype(x.dtype), window_strides=(1,),
        padding=[(CONV_W - 1, 0)], dimension_numbers=("NWC", "WIO", "NWC"),
        feature_group_count=c)

def _gated_delta_chunked(q, k, v, g, beta):
    B, T, H, dk = q.shape
    dv = v.shape[-1]
    C = DN_CHUNK
    n = T // C

    def blk(a):
        return jnp.moveaxis(a.reshape((B, n, C, H) + a.shape[3:]), 3, 1)

    q, k, v, g, beta = blk(q), blk(k), blk(v), blk(g), blk(beta)
    gc = jnp.cumsum(g, axis=-1)
    diff = gc[..., :, None] - gc[..., None, :]
    ii = jnp.arange(C)
    strict = ii[:, None] > ii[None, :]
    incl = ii[:, None] >= ii[None, :]
    kb = k * beta[..., None]
    L = jnp.where(strict, jnp.einsum("bhncd,bhnsd->bhncs", kb, k)
                  * jnp.exp(jnp.where(strict, diff, 0.0)), 0.0)
    eye = jnp.eye(C, dtype=q.dtype)
    rhs = jnp.concatenate([v * beta[..., None], kb * jnp.exp(gc)[..., None]], axis=-1)
    sol = lax.linalg.triangular_solve(eye + L, rhs, left_side=True, lower=True,
                                      unit_diagonal=True)
    u, w = sol[..., :dv], sol[..., dv:]
    a_qk = jnp.where(incl, jnp.einsum("bhncd,bhnsd->bhncs", q, k)
                     * jnp.exp(jnp.where(incl, diff, 0.0)), 0.0)
    g_last = gc[..., -1]
    qg = q * jnp.exp(gc)[..., None]
    kd = k * jnp.exp(g_last[..., None] - gc)[..., None]
    d_last = jnp.exp(g_last)
    xs = tuple(jnp.moveaxis(a, 2, 0) for a in (qg, kd, u, w, a_qk, d_last))

    def step(S, inp):
        qg_c, kd_c, u_c, w_c, a_c, d_c = inp
        v_new = u_c - jnp.einsum("bhck,bhkv->bhcv", w_c, S)
        o = (jnp.einsum("bhck,bhkv->bhcv", qg_c, S)
             + jnp.einsum("bhcs,bhsv->bhcv", a_c, v_new))
        S = S * d_c[..., None, None] + jnp.einsum("bhck,bhcv->bhkv", kd_c, v_new)
        return S, o

    S0 = jnp.zeros((B, H, dk, dv), jnp.float32)
    _, o = lax.scan(step, S0, xs)
    o = jnp.moveaxis(o, 0, 2)
    return jnp.moveaxis(o, 1, 3).reshape(B, T, H, dv)

def _deltanet_branch(qkv, z, b_logit, a_logit, conv_w, a_log, dt_bias, o_norm):
    B, T, _ = qkv.shape
    qkv = jax.nn.silu(_causal_dwconv(qkv, conv_w)).astype(jnp.float32)
    q, k, v = jnp.split(qkv, 3, axis=-1)
    q = _l2norm(q.reshape(B, T, DN_HEADS, DN_DK)) * (DN_DK ** -0.5)
    k = _l2norm(k.reshape(B, T, DN_HEADS, DN_DK))
    v = v.reshape(B, T, DN_HEADS, DN_DV)
    beta = jax.nn.sigmoid(b_logit.astype(jnp.float32))
    g = -jnp.exp(a_log.astype(jnp.float32)) * jax.nn.softplus(
        a_logit.astype(jnp.float32) + dt_bias.astype(jnp.float32))
    o = _gated_delta_chunked(q, k, v, g, beta)
    o = _rmsnorm(o, o_norm) * jax.nn.silu(z.astype(jnp.float32).reshape(B, T, DN_HEADS, DN_DV))
    return o.reshape(B, T, BRANCH_W).astype(z.dtype)

def _spatial_gating_branch(uv, z, v_gain, w_s, b_s):
    B, T, _ = uv.shape
    u, v = jnp.split(jax.nn.gelu(uv), 2, axis=-1)
    v = _rmsnorm(v, v_gain)
    n = T // GM_CHUNK
    vb = v.reshape(B, n, GM_CHUNK, GM_GROUPS, GM_CH)
    causal = jnp.tril(jnp.ones((GM_CHUNK, GM_CHUNK), dtype=bool))
    ws = jnp.where(causal, w_s, 0.0).astype(v.dtype)
    s = jnp.einsum("gpq,bnqgc->bnpgc", ws, vb) + b_s.T.astype(v.dtype)[None, None, :, :, None]
    return u * s.reshape(B, T, BRANCH_W) * jax.nn.silu(z)

def _sliding_window_branch(q, k, v, z, sinks):
    B, T, _ = q.shape
    P = SW_BLOCK
    n = T // P
    G = SW_HEADS // SW_KV_HEADS
    q = q.reshape(B, n, P, SW_KV_HEADS, G, SW_HD)
    k = k.reshape(B, n, P, SW_KV_HEADS, SW_HD)
    v = v.reshape(B, n, P, SW_KV_HEADS, SW_HD)
    pad = jnp.zeros_like(k[:, :1])
    kb = jnp.concatenate([jnp.concatenate([pad, k[:, :-1]], axis=1), k], axis=2)
    vb = jnp.concatenate([jnp.concatenate([pad, v[:, :-1]], axis=1), v], axis=2)
    s = jnp.einsum("bnqkgd,bnskd->bnkgqs", q, kb).astype(jnp.float32) * (SW_HD ** -0.5)
    qi = jnp.arange(P)[:, None]
    kj = jnp.arange(2 * P)[None, :]
    dist = qi + P - kj
    blk = jnp.arange(n)[:, None, None]
    valid = (dist >= 0) & (dist < SW_WINDOW) & (blk * P - P + kj >= 0)
    s = jnp.where(valid[None, :, None, None], s, NEG_INF)
    sink = jnp.broadcast_to(
        sinks.astype(jnp.float32).reshape(SW_KV_HEADS, G)[None, None, :, :, None, None],
        s.shape[:-1] + (1,))
    p = jax.nn.softmax(jnp.concatenate([s, sink], axis=-1), axis=-1)[..., :-1]
    o = jnp.einsum("bnkgqs,bnskd->bnqkgd", p.astype(vb.dtype), vb).reshape(B, T, BRANCH_W)
    return o * jax.nn.silu(z)

def _memory_branch(q, z, mem_kv):
    B, T, _ = q.shape
    q = q.reshape(B, T, XM_HEADS, XM_HD)
    mk, mv = jnp.split(mem_kv, 2, axis=-1)
    mk = mk.reshape(B, -1, XM_HEADS, XM_HD)
    mv = mv.reshape(B, -1, XM_HEADS, XM_HD)
    s = jnp.einsum("bthd,bmhd->bhtm", q, mk).astype(jnp.float32) * (XM_HD ** -0.5)
    p = jax.nn.softmax(s, axis=-1)
    o = jnp.einsum("bhtm,bmhd->bthd", p.astype(mv.dtype), mv).reshape(B, T, BRANCH_W)
    return o * jax.nn.silu(z)

def _layer(x, mem, norm_pre, norm_post, norm_mem, w_in, conv_w, a_log, dt_bias, dn_norm,
           gm_norm, spatial_w, spatial_b, sinks, w_mem_kv, w_up, w_out):
    B, T, D = x.shape
    h = _rmsnorm(x, norm_pre)
    cols = h @ w_in
    (dn_qkv, dn_z, dn_b, dn_a, gm_uv, gm_z, sw_q, sw_k, sw_v, sw_z,
     xm_q, xm_z, gate_logits) = _split_cols(cols)
    mem_kv = _rmsnorm(mem, norm_mem) @ w_mem_kv
    y_a = _deltanet_branch(dn_qkv, dn_z, dn_b, dn_a, conv_w, a_log, dt_bias, dn_norm)
    y_b = _spatial_gating_branch(gm_uv, gm_z, gm_norm, spatial_w, spatial_b)
    y_c = _sliding_window_branch(sw_q, sw_k, sw_v, sw_z, sinks)
    y_m = _memory_branch(xm_q, xm_z, mem_kv)
    ys = jnp.stack([y_a, y_b, y_c, y_m], axis=2)
    proj = jnp.einsum("btnc,ncd->btnd", ys, w_up)
    gates = jax.nn.sigmoid(gate_logits.reshape(B, T, N_BRANCH, D))
    merged = jnp.sum(gates * proj, axis=2)
    out = merged @ w_out
    return x + _rmsnorm(out, norm_post)

def first_inputs(seed: int = 0) -> dict:
    key = jax.random.key(seed)
    ks = jax.random.split(key, 20)
    f32 = jnp.float32
    nrm = lambda k, shape, scale: jax.random.normal(k, shape, f32) * scale
    dt = jnp.exp(jax.random.uniform(ks[8], (DEPTH, DN_HEADS), f32,
                                    math.log(1e-3), math.log(1e-1)))
    return {
        "x": nrm(ks[0], (BATCH, SEQ, D_MODEL), 1.0),
        "mem": nrm(ks[1], (BATCH, MEM_LEN, D_MODEL), 1.0),
        "norm_pre": 1.0 + nrm(ks[2], (DEPTH, D_MODEL), 0.1),
        "norm_post": 1.0 + nrm(ks[3], (DEPTH, D_MODEL), 0.1),
        "norm_mem": 1.0 + nrm(ks[4], (DEPTH, D_MODEL), 0.1),
        "w_in": nrm(ks[5], (DEPTH, D_MODEL, D_IN), D_MODEL ** -0.5),
        "conv_w": nrm(ks[6], (DEPTH, CONV_W, 3 * BRANCH_W), CONV_W ** -0.5),
        "a_log": jnp.log(jax.random.uniform(ks[7], (DEPTH, DN_HEADS), f32, 1.0, 16.0)),
        "dt_bias": dt + jnp.log(-jnp.expm1(-dt)),
        "dn_norm": 1.0 + nrm(ks[9], (DEPTH, DN_DV), 0.1),
        "gm_norm": 1.0 + nrm(ks[10], (DEPTH, BRANCH_W), 0.1),
        "spatial_w": nrm(ks[11], (DEPTH, GM_GROUPS, GM_CHUNK, GM_CHUNK), GM_CHUNK ** -0.5),
        "spatial_b": 1.0 + nrm(ks[12], (DEPTH, GM_GROUPS, GM_CHUNK), 0.1),
        "sinks": nrm(ks[13], (DEPTH, SW_HEADS), 1.0),
        "w_mem_kv": nrm(ks[14], (DEPTH, D_MODEL, 2 * BRANCH_W), D_MODEL ** -0.5),
        "w_up": nrm(ks[15], (DEPTH, N_BRANCH, BRANCH_W, D_MODEL), BRANCH_W ** -0.5),
        "w_out": nrm(ks[16], (DEPTH, D_MODEL, D_MODEL), D_MODEL ** -0.5),
    }

def first_block(x, mem, norm_pre, norm_post, norm_mem, w_in, conv_w, a_log, dt_bias, dn_norm,
              gm_norm, spatial_w, spatial_b, sinks, w_mem_kv, w_up, w_out):
    for l in range(DEPTH):
        x = _layer(x, mem, norm_pre[l], norm_post[l], norm_mem[l], w_in[l], conv_w[l],
                   a_log[l], dt_bias[l], dn_norm[l], gm_norm[l], spatial_w[l], spatial_b[l],
                   sinks[l], w_mem_kv[l], w_up[l], w_out[l])
    return x


DEPTH_2 = 2

N_MIXERS = 2
RMS_EPS = 1e-6
FFN_HIDDEN = 2816
Q_BLOCK = 128
NEG = -1e30
MLA_HEADS = 16
MLA_Q_LORA = 384
MLA_KV_LORA = 256
MLA_NOPE = 64
MLA_ROPE = 32
MLA_V = 64
ROPE_THETA = 10000.0
NSA_HEADS = 16
NSA_GROUPS = 4
NSA_QK = 64
NSA_V = 64
CMP_BLOCK = 32
CMP_STRIDE = 16
CMP_HIDDEN = 128
SEL_BLOCK = 64
SEL_TOP_N = 16
WINDOW = 512
SEL_Q_CHUNK = 16
REL_BUCKETS = 32
REL_MAX_DIST = 128


def rmsnorm(x, g):
    x32 = x.astype(jnp.float32)
    y = x32 * lax.rsqrt(jnp.mean(x32 * x32, axis=-1, keepdims=True) + RMS_EPS)
    return y.astype(x.dtype) * g

def swiglu(x, w_gate, w_up, w_down):
    return (jax.nn.silu(x @ w_gate) * (x @ w_up)) @ w_down

def rope_angles(S):
    half = MLA_ROPE // 2
    inv = ROPE_THETA ** (-jnp.arange(half, dtype=jnp.float32) * 2.0 / MLA_ROPE)
    ang = jnp.arange(S, dtype=jnp.float32)[:, None] * inv[None, :]
    return jnp.cos(ang), jnp.sin(ang)

def apply_rotary(x, cos, sin):
    half = x.shape[-1] // 2
    cos = cos.astype(x.dtype)
    sin = sin.astype(x.dtype)
    x1, x2 = x[..., :half], x[..., half:]
    return jnp.concatenate([x1 * cos - x2 * sin, x1 * sin + x2 * cos], axis=-1)

def t5_bucket(dist):
    n = jnp.maximum(dist, 0)
    max_exact = REL_BUCKETS // 2
    nf = jnp.maximum(n, 1).astype(jnp.float32)
    large = max_exact + (jnp.log(nf / max_exact) / math.log(REL_MAX_DIST / max_exact)
                         * (REL_BUCKETS - max_exact)).astype(jnp.int32)
    large = jnp.minimum(large, REL_BUCKETS - 1)
    return jnp.where(n < max_exact, n, large)

def mla_mixer(h, w_in, q_norm, kv_norm, w_uq, w_ukv, w_o):
    B, S, _ = h.shape
    H = MLA_HEADS
    proj = h @ w_in
    c_q = proj[..., :MLA_Q_LORA]
    c_kv = proj[..., MLA_Q_LORA:MLA_Q_LORA + MLA_KV_LORA]
    k_rope = proj[..., MLA_Q_LORA + MLA_KV_LORA:]
    q = (rmsnorm(c_q, q_norm) @ w_uq).reshape(B, S, H, MLA_NOPE + MLA_ROPE)
    kv = (rmsnorm(c_kv, kv_norm) @ w_ukv).reshape(B, S, H, MLA_NOPE + MLA_V)
    cos, sin = rope_angles(S)
    q_nope = q[..., :MLA_NOPE]
    q_rope = apply_rotary(q[..., MLA_NOPE:], cos[:, None, :], sin[:, None, :])
    k_rope = apply_rotary(k_rope, cos, sin)
    k_nope = kv[..., :MLA_NOPE]
    v = kv[..., MLA_NOPE:]
    scale = (MLA_NOPE + MLA_ROPE) ** -0.5
    n_blk = S // Q_BLOCK
    qn_b = q_nope.reshape(B, n_blk, Q_BLOCK, H, MLA_NOPE).swapaxes(0, 1)
    qr_b = q_rope.reshape(B, n_blk, Q_BLOCK, H, MLA_ROPE).swapaxes(0, 1)
    starts = jnp.arange(n_blk) * Q_BLOCK
    kpos = jnp.arange(S)

    def block(args):
        qn, qr, s0 = args
        s = (jnp.einsum('bqhd,bkhd->bhqk', qn, k_nope)
             + jnp.einsum('bqhd,bkd->bhqk', qr, k_rope)).astype(jnp.float32) * scale
        qpos = s0 + jnp.arange(Q_BLOCK)
        p = jax.nn.softmax(jnp.where(kpos[None, :] <= qpos[:, None], s, NEG), axis=-1)
        return jnp.einsum('bhqk,bkhd->bqhd', p.astype(v.dtype), v)

    o = lax.map(block, (qn_b, qr_b, starts)).swapaxes(0, 1).reshape(B, S, H * MLA_V)
    return o @ w_o

def compress_blocks(x, blk_idx, pos_emb, w1, w2):
    B = x.shape[0]
    n_cmp, L = blk_idx.shape
    blocks = x[:, blk_idx] + pos_emb[None, None, :, None, :]
    flat = jnp.moveaxis(blocks, 3, 2).reshape(B, n_cmp, x.shape[2], L * x.shape[3])
    return jax.nn.gelu(flat @ w1) @ w2

def selection_overlap(n_cmp, n_sel):
    cs = np.arange(n_cmp) * CMP_STRIDE
    ce = cs + CMP_BLOCK
    ss = np.arange(n_sel) * SEL_BLOCK
    se = ss + SEL_BLOCK
    ov = np.minimum(ce[:, None], se[None, :]) - np.maximum(cs[:, None], ss[None, :])
    return (np.clip(ov, 0, None) / CMP_BLOCK).astype(np.float32)

def selected_attention(q, k, v, sel_idx, tbl, scale):
    B, S, G, R, dk = q.shape
    dv = v.shape[-1]
    n_sel = S // SEL_BLOCK
    n_top = sel_idx.shape[-1]
    kb = k.reshape(B, n_sel, SEL_BLOCK, G, dk).transpose(0, 3, 1, 2, 4)
    vb = v.reshape(B, n_sel, SEL_BLOCK, G, dv).transpose(0, 3, 1, 2, 4)
    C = SEL_Q_CHUNK
    n_ch = S // C
    q_ch = q.reshape(B, n_ch, C, G, R, dk).swapaxes(0, 1)
    idx_ch = sel_idx.reshape(B, G, n_ch, C, n_top).transpose(2, 0, 1, 3, 4)
    starts = jnp.arange(n_ch) * C
    gather = jax.vmap(jax.vmap(lambda blocks, ix: blocks[ix]))
    g_ar = jnp.arange(G)[None, :, None, None]
    K = n_top * SEL_BLOCK

    def chunk(args):
        q_i, ix, s0 = args
        kg = gather(kb, ix).reshape(B, G, C, K, dk)
        vg = gather(vb, ix).reshape(B, G, C, K, dv)
        kpos = (ix[..., None] * SEL_BLOCK + jnp.arange(SEL_BLOCK)).reshape(B, G, C, K)
        qpos = s0 + jnp.arange(C)
        dist = qpos[None, None, :, None] - kpos
        bias = tbl[t5_bucket(dist), g_ar]
        s = jnp.einsum('bcgrd,bgckd->bgcrk', q_i, kg).astype(jnp.float32) * scale \
            + jnp.moveaxis(bias, -1, 3).astype(jnp.float32)
        p = jax.nn.softmax(jnp.where((dist >= 0)[:, :, :, None, :], s, NEG), axis=-1)
        return jnp.einsum('bgcrk,bgckd->bcgrd', p.astype(vg.dtype), vg)

    out = lax.map(chunk, (q_ch, idx_ch, starts))
    return out.swapaxes(0, 1).reshape(B, S, G, R, dv)

def window_attention(q, k, v, tbl, scale):
    B, S, G, R, dk = q.shape
    n_blk = S // Q_BLOCK
    span = WINDOW + Q_BLOCK
    k_pad = jnp.pad(k, ((0, 0), (WINDOW, 0), (0, 0), (0, 0)))
    v_pad = jnp.pad(v, ((0, 0), (WINDOW, 0), (0, 0), (0, 0)))
    q_b = q.reshape(B, n_blk, Q_BLOCK, G, R, dk).swapaxes(0, 1)
    starts = jnp.arange(n_blk) * Q_BLOCK

    def block(args):
        q_i, s0 = args
        k_i = lax.dynamic_slice_in_dim(k_pad, s0, span, axis=1)
        v_i = lax.dynamic_slice_in_dim(v_pad, s0, span, axis=1)
        qpos = s0 + jnp.arange(Q_BLOCK)
        kpos = s0 - WINDOW + jnp.arange(span)
        dist = qpos[:, None] - kpos[None, :]
        mask = (dist >= 0) & (dist < WINDOW) & (kpos >= 0)[None, :]
        bias = tbl[t5_bucket(dist)].transpose(2, 3, 0, 1)
        s = jnp.einsum('bqgrd,bkgd->bgrqk', q_i, k_i).astype(jnp.float32) * scale + bias.astype(jnp.float32)
        p = jax.nn.softmax(jnp.where(mask, s, NEG), axis=-1)
        return jnp.einsum('bgrqk,bkgd->bqgrd', p.astype(v_i.dtype), v_i)

    out = lax.map(block, (q_b, starts))
    return out.swapaxes(0, 1).reshape(B, S, G, R, v.shape[-1])

def nsa_mixer(h, rel_bias, w_in, pos_k, w1_k, w2_k, pos_v, w1_v, w2_v, w_o):
    B, S, _ = h.shape
    H, G = NSA_HEADS, NSA_GROUPS
    R = H // G
    sizes = [H * NSA_QK, G * NSA_QK, G * NSA_V, G * NSA_QK, G * NSA_V, G * NSA_QK, G * NSA_V, H * 3]
    cuts = [int(c) for c in np.cumsum(sizes[:-1])]
    q, k_c, v_c, k_s, v_s, k_w, v_w, g = jnp.split(h @ w_in, cuts, axis=-1)
    q = q.reshape(B, S, G, R, NSA_QK)
    k_c, k_s, k_w = (t.reshape(B, S, G, NSA_QK) for t in (k_c, k_s, k_w))
    v_c, v_s, v_w = (t.reshape(B, S, G, NSA_V) for t in (v_c, v_s, v_w))
    gates = jax.nn.sigmoid(g.astype(jnp.float32)).astype(h.dtype).reshape(B, S, G, R, 3)
    tbl = rel_bias.reshape(REL_BUCKETS, G, R)
    scale = NSA_QK ** -0.5
    pos = jnp.arange(S)

    n_cmp = (S - CMP_BLOCK) // CMP_STRIDE + 1
    blk_idx = jnp.arange(n_cmp)[:, None] * CMP_STRIDE + jnp.arange(CMP_BLOCK)[None, :]
    kc = compress_blocks(k_c, blk_idx, pos_k, w1_k, w2_k)
    vc = compress_blocks(v_c, blk_idx, pos_v, w1_v, w2_v)
    cmp_end = jnp.arange(n_cmp) * CMP_STRIDE + CMP_BLOCK - 1
    dist = pos[:, None] - cmp_end[None, :]
    valid = dist >= 0
    bias = tbl[t5_bucket(dist)].transpose(2, 3, 0, 1)
    s = jnp.einsum('bsgrd,bngd->bgrsn', q, kc).astype(jnp.float32) * scale + bias.astype(jnp.float32)
    p_cmp = jax.nn.softmax(jnp.where(valid, s, NEG), axis=-1) * valid
    o_cmp = jnp.einsum('bgrsn,bngd->bsgrd', p_cmp.astype(vc.dtype), vc)

    n_sel = S // SEL_BLOCK
    overlap = jnp.asarray(selection_overlap(n_cmp, n_sel))
    imp = jnp.einsum('bgrsn,nj->bgsj', p_cmp, overlap)
    blk_t = (pos // SEL_BLOCK)[:, None]
    j = jnp.arange(n_sel)[None, :]
    forced = (j == 0) | (j == blk_t) | (j == blk_t - 1)
    score = jnp.where(forced, 1e6, jnp.where(j <= blk_t, imp, -1e6))
    n_top = min(SEL_TOP_N, n_sel)
    _, sel_idx = lax.top_k(score, n_top)
    o_sel = selected_attention(q, k_s, v_s, sel_idx, tbl, scale)

    o_win = window_attention(q, k_w, v_w, tbl, scale)

    o = gates[..., 0:1] * o_cmp + gates[..., 1:2] * o_sel + gates[..., 2:3] * o_win
    return o.reshape(B, S, H * NSA_V) @ w_o

def second_inputs(seed: int = 0) -> dict:
    key = jax.random.key(seed)
    ks = iter(jax.random.split(key, 32))
    n_mla = len(range(0, DEPTH_2, N_MIXERS))
    n_nsa = DEPTH_2 - n_mla

    def dense(shape, fan_in):
        return jax.random.normal(next(ks), shape, jnp.float32) * fan_in ** -0.5

    def gain(shape):
        return 1.0 + 0.01 * jax.random.normal(next(ks), shape, jnp.float32)

    def small(shape, s):
        return s * jax.random.normal(next(ks), shape, jnp.float32)

    mla_in = MLA_Q_LORA + MLA_KV_LORA + MLA_ROPE
    nsa_in = NSA_HEADS * NSA_QK + 3 * NSA_GROUPS * (NSA_QK + NSA_V) + 3 * NSA_HEADS
    return {
        "x": jax.random.normal(next(ks), (BATCH, SEQ, D_MODEL), jnp.float32),
        "ffn_norm_a": gain((DEPTH_2, D_MODEL)),
        "ffn_a_w_gate": dense((DEPTH_2, D_MODEL, FFN_HIDDEN), D_MODEL),
        "ffn_a_w_up": dense((DEPTH_2, D_MODEL, FFN_HIDDEN), D_MODEL),
        "ffn_a_w_down": dense((DEPTH_2, FFN_HIDDEN, D_MODEL), FFN_HIDDEN),
        "mix_norm": gain((DEPTH_2, D_MODEL)),
        "ffn_norm_b": gain((DEPTH_2, D_MODEL)),
        "ffn_b_w_gate": dense((DEPTH_2, D_MODEL, FFN_HIDDEN), D_MODEL),
        "ffn_b_w_up": dense((DEPTH_2, D_MODEL, FFN_HIDDEN), D_MODEL),
        "ffn_b_w_down": dense((DEPTH_2, FFN_HIDDEN, D_MODEL), FFN_HIDDEN),
        "final_norm": gain((D_MODEL,)),
        "rel_bias": small((REL_BUCKETS, NSA_HEADS), 0.5),
        "mla_w_in": dense((n_mla, D_MODEL, mla_in), D_MODEL),
        "mla_q_norm": gain((n_mla, MLA_Q_LORA)),
        "mla_kv_norm": gain((n_mla, MLA_KV_LORA)),
        "mla_w_uq": dense((n_mla, MLA_Q_LORA, MLA_HEADS * (MLA_NOPE + MLA_ROPE)), MLA_Q_LORA),
        "mla_w_ukv": dense((n_mla, MLA_KV_LORA, MLA_HEADS * (MLA_NOPE + MLA_V)), MLA_KV_LORA),
        "mla_w_o": dense((n_mla, MLA_HEADS * MLA_V, D_MODEL), MLA_HEADS * MLA_V),
        "nsa_w_in": dense((n_nsa, D_MODEL, nsa_in), D_MODEL),
        "nsa_cmp_pos_k": small((n_nsa, CMP_BLOCK, NSA_QK), 0.1),
        "nsa_cmp_w1_k": dense((n_nsa, CMP_BLOCK * NSA_QK, CMP_HIDDEN), CMP_BLOCK * NSA_QK),
        "nsa_cmp_w2_k": dense((n_nsa, CMP_HIDDEN, NSA_QK), CMP_HIDDEN),
        "nsa_cmp_pos_v": small((n_nsa, CMP_BLOCK, NSA_V), 0.1),
        "nsa_cmp_w1_v": dense((n_nsa, CMP_BLOCK * NSA_V, CMP_HIDDEN), CMP_BLOCK * NSA_V),
        "nsa_cmp_w2_v": dense((n_nsa, CMP_HIDDEN, NSA_V), CMP_HIDDEN),
        "nsa_w_o": dense((n_nsa, NSA_HEADS * NSA_V, D_MODEL), NSA_HEADS * NSA_V),
    }

def second_block(x, ffn_norm_a, ffn_a_w_gate, ffn_a_w_up, ffn_a_w_down, mix_norm, ffn_norm_b,
              ffn_b_w_gate, ffn_b_w_up, ffn_b_w_down, final_norm, rel_bias,
              mla_w_in, mla_q_norm, mla_kv_norm, mla_w_uq, mla_w_ukv, mla_w_o,
              nsa_w_in, nsa_cmp_pos_k, nsa_cmp_w1_k, nsa_cmp_w2_k,
              nsa_cmp_pos_v, nsa_cmp_w1_v, nsa_cmp_w2_v, nsa_w_o):
    h = x
    for i in range(DEPTH_2):
        h = h + 0.5 * swiglu(rmsnorm(h, ffn_norm_a[i]), ffn_a_w_gate[i], ffn_a_w_up[i], ffn_a_w_down[i])
        m = rmsnorm(h, mix_norm[i])
        j = i // N_MIXERS
        if i % N_MIXERS == 0:
            h = h + mla_mixer(m, mla_w_in[j], mla_q_norm[j], mla_kv_norm[j],
                              mla_w_uq[j], mla_w_ukv[j], mla_w_o[j])
        else:
            h = h + nsa_mixer(m, rel_bias, nsa_w_in[j], nsa_cmp_pos_k[j], nsa_cmp_w1_k[j], nsa_cmp_w2_k[j],
                              nsa_cmp_pos_v[j], nsa_cmp_w1_v[j], nsa_cmp_w2_v[j], nsa_w_o[j])
        h = h + 0.5 * swiglu(rmsnorm(h, ffn_norm_b[i]), ffn_b_w_gate[i], ffn_b_w_up[i], ffn_b_w_down[i])
    return rmsnorm(h, final_norm)


def setup_inputs(seed=0):
    out = dict(first_inputs(seed))
    for name, value in second_inputs(seed + 1).items():
        if name != "x":
            out[name + "_2"] = value
    return out


def reference(
    x, mem, norm_pre, norm_post, norm_mem, w_in, conv_w, a_log, dt_bias, dn_norm, gm_norm,
    spatial_w, spatial_b, sinks, w_mem_kv, w_up, w_out, ffn_norm_a_2, ffn_a_w_gate_2,
    ffn_a_w_up_2, ffn_a_w_down_2, mix_norm_2, ffn_norm_b_2, ffn_b_w_gate_2, ffn_b_w_up_2,
    ffn_b_w_down_2, final_norm_2, rel_bias_2, mla_w_in_2, mla_q_norm_2, mla_kv_norm_2,
    mla_w_uq_2, mla_w_ukv_2, mla_w_o_2, nsa_w_in_2, nsa_cmp_pos_k_2, nsa_cmp_w1_k_2,
    nsa_cmp_w2_k_2, nsa_cmp_pos_v_2, nsa_cmp_w1_v_2, nsa_cmp_w2_v_2, nsa_w_o_2,
):
    x = first_block(
        x, mem, norm_pre, norm_post, norm_mem, w_in, conv_w, a_log, dt_bias, dn_norm, gm_norm,
        spatial_w, spatial_b, sinks, w_mem_kv, w_up, w_out,
    )
    return second_block(
        x, ffn_norm_a_2, ffn_a_w_gate_2, ffn_a_w_up_2, ffn_a_w_down_2, mix_norm_2, ffn_norm_b_2,
        ffn_b_w_gate_2, ffn_b_w_up_2, ffn_b_w_down_2, final_norm_2, rel_bias_2, mla_w_in_2,
        mla_q_norm_2, mla_kv_norm_2, mla_w_uq_2, mla_w_ukv_2, mla_w_o_2, nsa_w_in_2,
        nsa_cmp_pos_k_2, nsa_cmp_w1_k_2, nsa_cmp_w2_k_2, nsa_cmp_pos_v_2, nsa_cmp_w1_v_2,
        nsa_cmp_w2_v_2, nsa_w_o_2,
    )


_drawn_inputs = setup_inputs


def setup_inputs(seed=0):
    import zlib

    import numpy as np

    out = dict(_drawn_inputs(seed))
    spreads = {}
    factors = {'norm_mem': 5.956,
     'sinks': 6.086,
     'ffn_norm_a_2': 8.0,
     'mix_norm_2': 8.0,
     'ffn_norm_b_2': 8.0,
     'final_norm_2': 32.648,
     'mla_q_norm_2': 8.0,
     'mla_kv_norm_2': 8.0,
     'nsa_cmp_pos_k_2': 22.44,
     'nsa_cmp_pos_v_2': 30.912,
     'rel_bias_2': 4.884}
    for name, (base, spread) in spreads.items():
        noise = np.random.default_rng([zlib.crc32(name.encode()), seed]).standard_normal(out[name].shape)
        drawn = base * np.exp(spread * noise) if base else spread * noise
        out[name] = __import__('jax').numpy.asarray(drawn.astype(out[name].dtype))
    for name, factor in factors.items():
        out[name] = (out[name] * factor).astype(out[name].dtype)
    return out
```

```python
import numpy as np
from contextlib import ExitStack

import concourse.bass as bass
from concourse import mybir

F32 = mybir.dt.float32
F32R = mybir.dt.float32r
ALU = mybir.AluOpType
ACT = mybir.ActivationFunctionType
AX = mybir.AxisListType

P = 128
S = 256
TT = S // P
D = 1024
KC = D // P
TW = 2048
CW = TW // KC
SLOTS = 3
EPS = 1e-6
NEG = -1e30
FFN = 2816
FT = FFN // CW
BW = 512
NBR = 4
DN_H = 4
SW_H, SW_KV, SW_D, SW_WIN = 8, 2, 64, 128
XM_H = 4
MLA_H, MLA_QL, MLA_KVL, MLA_N, MLA_R, MLA_V = 16, 384, 256, 64, 32, 64
NSA_H, NSA_G, NSA_D = 16, 4, 64
NSA_R = NSA_H // NSA_G
CMP_L, CMP_ST = 32, 16
NCMP = (S - CMP_L) // CMP_ST + 1
BUCKETS = 32
PAIRS = TT * DN_H


def plan():
    t = ["mk0", "mk1", "mv0", "mv1"]
    t += ["xmq0", "xmq1", "xmz0", "xmz1"]
    t += ["swq0", "swq1", "swkv", "swz0", "swz1"]
    t += ["gmu0", "gmu1", "gmz0", "gmz1", "gmv0", "gmv1"]
    t += ["ba"] + [f"dn{j}" for j in range(6)] + ["dnz0", "dnz1"]
    for n in range(NBR):
        for half in range(2):
            t += [f"gate{n}{half}0", f"gate{n}{half}1", f"up{n}{half}"]
    t += [f"out{j}" for j in range(4)]
    t += ffn_names(0)
    t += ["mlain0", "mlain1", "mlain2"] + [f"uq{j}" for j in range(4)] + ["uk", "uv"]
    t += [f"mlao{j}" for j in range(4)]
    t += ffn_names(1) + ffn_names(2)
    t += [f"nq{j}" for j in range(4)] + ["nkc", "nvc", "nks", "nvs", "nkw", "nvw", "ng"]
    t += [f"nsao{j}" for j in range(4)]
    t += ffn_names(3)
    return t + ["pad"]


def ffn_names(f):
    t = [f"f{f}g0", f"f{f}u0"]
    for i in range(1, FT):
        t += [f"f{f}g{i}", f"f{f}u{i}", f"f{f}d{i - 1}"]
    return t + [f"f{f}d{FT - 1}"]


PLAN = plan()
TILE = {n: i for i, n in enumerate(PLAN)}
NT = len(PLAN)
PLAIN = [n for n in PLAN if n[0] not in "fu" and n[:4] != "gate" and n != "pad"]
UNIT = {n: i for i, n in enumerate(PLAIN)}

VEC = {}
_at = 0
for _n, _w in (("pre", 8), ("mem", 8), ("fa0", 8), ("fa1", 8), ("mx0", 8), ("mx1", 8), ("fb0", 8),
               ("fb1", 8), ("qn", 3), ("kvn", 2), ("conv", 48)):
    VEC[_n] = _at
    _at += _w
NVEC = _at
ROW = {}
_at = 0
for _n, _w in (("onorm", 128), ("gmn", 512), ("bs", 512), ("dtb", 8), ("alog", 8), ("sink", 8)):
    ROW[_n] = _at
    _at += _w
NROW = _at
LEVELS = 7
CON = {}
_at = 0
for _n, _w in (("ident", 128), ("upto", 128), ("before", 128), ("ones", 128), ("causal", 256),
               ("window", 256), ("rowok", 2), ("cos", 256), ("sin", 256)):
    CON[_n] = _at
    _at += _w
NCON = _at


def constants():
    j = np.arange(P)[:, None]
    i = np.arange(P)[None, :]
    con = np.zeros((P, NCON), np.float32)

    def put(name, a):
        con[:, CON[name]:CON[name] + a.shape[1]] = a

    put("ident", (i == j) * 1.0)
    put("upto", (j <= i) * 1.0)
    put("before", (j < i) * 1.0)
    put("ones", np.ones((P, P)))
    dist = P + j - np.arange(2 * P)[None, :]
    put("causal", np.where(dist >= 0, 0.0, NEG))
    put("window", np.where((dist >= 0) & (dist < SW_WIN), 0.0, NEG))
    put("rowok", (j + P * np.arange(TT)[None, :] >= CMP_L - 1) * 1.0)
    half = MLA_R // 2
    inv = np.float32(10000.0) ** (-np.arange(half, dtype=np.float32) * np.float32(2.0) / MLA_R)
    ang = np.arange(S, dtype=np.float32)[None, :] * inv[:, None].astype(np.float32)
    rope = np.zeros((2, P, S), np.float32)
    rope[0, 64:96] = np.tile(np.cos(ang), (2, 1))
    rope[1, 64:80], rope[1, 80:96] = -np.sin(ang), np.sin(ang)
    put("cos", rope[0])
    put("sin", rope[1])
    level = np.zeros((P, LEVELS, P), np.float32)
    for n in range(LEVELS):
        s = 1 << n
        level[:, n] = (j // (2 * s) == i // (2 * s)) & (i % (2 * s) >= s) & (j % (2 * s) < s)
    dist = np.arange(2 * S) - S
    n = np.maximum(dist, 0)
    exact = BUCKETS // 2
    large = exact + (np.log(np.maximum(n, 1).astype(np.float32) / exact) / np.float32(np.log(128 / exact))
                     * (BUCKETS - exact)).astype(np.int32)
    bucket = np.where(n < exact, n, np.minimum(large, BUCKETS - 1))
    hot = np.zeros((BUCKETS + 1, 2 * S), np.float32)
    hot[bucket, np.arange(2 * S)] = 1.0
    hot[BUCKETS] = dist < 0
    return con, level.reshape(P, LEVELS * P), hot


def lay_out(a):
    def cols(w, c0, n=CW):
        k = w.shape[0] // P
        return w[:, c0:c0 + n].reshape(k, P, n).transpose(1, 0, 2).reshape(P, k * n)

    w_in = a["w_in"][0]
    mkv = a["w_mem_kv"][0]
    win_m, wuq, wukv = a["mla_w_in_2"][0], a["mla_w_uq_2"][0], a["mla_w_ukv_2"][0]
    win_n = a["nsa_w_in_2"][0]
    o_qkv, o_z, o_b = 0, 1536, 2048
    o_uv = o_b + 2 * DN_H
    o_gz = o_uv + 1024
    o_sq = o_gz + 512
    o_sk = o_sq + 512
    o_sz = o_sk + 256
    o_xq = o_sz + 512
    o_xz = o_xq + 512
    o_g = o_xz + 512
    stream = np.zeros((NT, P, TW), np.float32)

    def put(name, t):
        stream[TILE[name], :, :t.shape[1]] = t

    for j in range(2):
        put(f"mk{j}", cols(mkv, CW * j))
        put(f"mv{j}", cols(mkv, BW + CW * j))
        for name, o in (("xmq", o_xq), ("xmz", o_xz), ("swq", o_sq), ("swz", o_sz), ("gmu", o_uv),
                        ("gmv", o_uv + BW), ("gmz", o_gz), ("dnz", o_z)):
            put(f"{name}{j}", cols(w_in, o + CW * j))
    put("swkv", cols(w_in, o_sk))
    put("ba", cols(w_in, o_b, 8))
    for j in range(6):
        put(f"dn{j}", cols(w_in, o_qkv + CW * j))
    for n in range(NBR):
        for h in range(2):
            for g in range(2):
                put(f"gate{n}{h}{g}", cols(w_in, o_g + D * n + 512 * h + CW * g))
            put(f"up{n}{h}", cols(a["w_up"][0, n], 512 * h, 512))
    for j in range(4):
        put(f"out{j}", cols(a["w_out"][0], CW * j))
        put(f"mlao{j}", cols(a["mla_w_o_2"][0], CW * j))
        put(f"nsao{j}", cols(a["nsa_w_o_2"][0], CW * j))
        put(f"nq{j}", cols(win_n, CW * j))
    for f in range(4):
        ab, l = "ab"[f % 2], f // 2
        g, u, d = (a[f"ffn_{ab}_w_{x}_2"][l] for x in ("gate", "up", "down"))
        for i in range(FT):
            put(f"f{f}g{i}", cols(g, CW * i))
            put(f"f{f}u{i}", cols(u, CW * i))
            put(f"f{f}d{i}", cols(d[CW * i:CW * (i + 1)], 0, D))
    put("mlain0", cols(win_m, 0))
    put("mlain1", cols(win_m, CW))
    rope = win_m[:, 640:672]
    last = np.concatenate([win_m[:, 512:640], np.zeros((D, 64), np.float32), rope, rope[:, 16:],
                           rope[:, :16]], axis=1)
    put("mlain2", cols(last, 0))
    q = wuq.reshape(MLA_QL, MLA_H, MLA_N + MLA_R)
    q = np.concatenate([q, q[:, :, 80:96], q[:, :, 64:80]], axis=2).reshape(MLA_QL, MLA_H * P)
    for j in range(4):
        put(f"uq{j}", cols(q, 512 * j, 512))
    kv = wukv.reshape(MLA_KVL, MLA_H, 2, 64)
    put("uk", cols(np.ascontiguousarray(kv[:, :, 0]).reshape(MLA_KVL, D), 0, D))
    put("uv", cols(np.ascontiguousarray(kv[:, :, 1]).reshape(MLA_KVL, D), 0, D))
    for n, name in enumerate(("nkc", "nvc", "nks", "nvs", "nkw", "nvw")):
        put(name, cols(win_n, D + CW * n))
    put("ng", cols(win_n, 2560, 48))

    vec = np.zeros((P, NVEC), np.float32)
    for name, v in (("pre", a["norm_pre"][0]), ("mem", a["norm_mem"][0]), ("fa0", a["ffn_norm_a_2"][0]),
                    ("fa1", a["ffn_norm_a_2"][1]), ("mx0", a["mix_norm_2"][0]), ("mx1", a["mix_norm_2"][1]),
                    ("fb0", a["ffn_norm_b_2"][0]), ("fb1", a["ffn_norm_b_2"][1]),
                    ("qn", a["mla_q_norm_2"][0]), ("kvn", a["mla_kv_norm_2"][0]),
                    ("conv", a["conv_w"][0])):
        v = v.reshape(-1, P).T
        vec[:, VEC[name]:VEC[name] + v.shape[1]] = v
    row = np.zeros((P, NROW), np.float32)
    for name, v in (("onorm", a["dn_norm"][0]), ("gmn", a["gm_norm"][0]), ("bs", a["spatial_b"][0].reshape(-1)),
                    ("dtb", np.tile(a["dt_bias"][0], TT)), ("alog", np.tile(a["a_log"][0], TT)),
                    ("sink", a["sinks"][0])):
        row[:, ROW[name]:ROW[name] + v.shape[0]] = v[None, :]
    con, level, hot = constants()
    tok = lambda v: v[0].reshape(TT, P, D).transpose(1, 0, 2)
    blk = lambda w: w[0].reshape(CMP_L // 2, P, P).transpose(1, 0, 2).reshape(P, TW)
    pos = lambda p: p[0].reshape(CMP_L // 2, P).T
    tbl = np.full((BUCKETS + 1, NSA_H), NEG, np.float32)
    tbl[:BUCKETS] = a["rel_bias_2"]
    arrays = {
        "stream": stream, "x": tok(a["x"]), "mem": tok(a["mem"]), "vec": vec, "row": row, "con": con,
        "level": level, "hot": hot,
        "spatial": a["spatial_w"][0].transpose(1, 0, 2), "bucket_bias": tbl,
        "post": np.broadcast_to(a["norm_post"][0], (P, D)),
        "final": np.broadcast_to(a["final_norm_2"], (P, D)),
        "w1": np.stack([blk(a["nsa_cmp_w1_k_2"]), blk(a["nsa_cmp_w1_v_2"])], axis=1),
        "w2": np.stack([a["nsa_cmp_w2_k_2"][0], a["nsa_cmp_w2_v_2"][0]], axis=1),
        "pos": np.stack([pos(a["nsa_cmp_pos_k_2"]), pos(a["nsa_cmp_pos_v_2"])], axis=1),
    }
    return {k: np.ascontiguousarray(v, dtype=np.float32) for k, v in arrays.items()}


def build(nc, A, out):
    ctx = ExitStack()
    with ctx:
        def sb(name, shape, dt=F32):
            return ctx.enter_context(nc.sbuf_tensor(name, shape, dt))

        def sem(name):
            return ctx.enter_context(nc.semaphore(name))

        raw = [sb(f"raw{i}", [P, TW]) for i in range(SLOTS)]
        high = [sb(f"high{i}", [P, TW], F32R) for i in range(SLOTS)]
        low = [sb(f"low{i}", [P, TW], F32R) for i in range(SLOTS)]
        x = sb("x", [P, TT, D])
        xs = sb("xs", [P, TT, D])
        nth = sb("nth", [P, KC, S], F32R)
        ntl = sb("ntl", [P, KC, S], F32R)
        vec = sb("vec", [P, NVEC])
        row = sb("row", [P, NROW])
        con = sb("con", [P, NCON])
        small = sb("small", [P, 1000])
        SCR = 14336
        scr = sb("scr", [P, SCR])
        with nc.sbuf_tensor("yth", [P, NBR, 4, S], F32R) as yth, \
                nc.sbuf_tensor("ytl", [P, NBR, 4, S], F32R) as ytl:
            pass
        hth = sb("hth", [P, 2, S], F32R)
        htl = sb("htl", [P, 2, S], F32R)
        late = sb("late", [P, 7168])
        ps = [ctx.enter_context(nc.psum_tensor(f"ps{i}", [P, 512], F32)) for i in range(8)]
        line = nc.dram_tensor("bias_by_distance", (NSA_H, 2 * S), F32).ap()

        def carve(memory, sizes, base=0):
            got, at = {}, base
            for name, size in sizes:
                got[name] = memory[:, at:at + size]
                at += size
            assert at <= memory.shape[1], (at, sizes)
            return got

        def c_(name, w):
            return con[:, CON[name]:CON[name] + w]

        ident, upto, before, ones = (c_(n, P) for n in ("ident", "upto", "before", "ones"))
        causal, window = c_("causal", 256), c_("window", 256)
        used_small = [0]

        def tiny(w):
            used_small[0] += w
            assert used_small[0] <= 1000
            return small[:, used_small[0] - w:used_small[0]]

        def r3(ap, a):
            return ap.rearrange("p (a b) -> p a b", a=a)

        def vcol(name, c):
            return vec[:, VEC[name] + c:VEC[name] + c + 1]

        def rowof(name, w):
            return row[:, ROW[name]:ROW[name] + w]

        at_buf = carve(scr, [("s", 1024), ("p", 1024)])
        at_s = [at_buf["s"][:, 512 * i:512 * i + 512] for i in range(2)]
        at_p = [at_buf["p"][:, 512 * i:512 * i + 512] for i in range(2)]
        xm = carve(scr, [("k", 1024), ("v", 1024), ("q", 1024), ("z", 1024), ("y", 1024)], 2048)
        sw = carve(scr, [("q", 1024), ("k", 512), ("v", 256), ("z", 1024), ("y", 1024)], 7168)
        gm = carve(scr, [("u", 1024), ("z", 1024), ("v", 1024), ("w", 512), ("wt", 512), ("sq", 1024)], 2048)
        dn = carve(scr, [("cin", 3108), ("cact", 3072), ("tok", 3072), ("kb", 1024), ("rw", 512),
                         ("kt", 1024), ("qt", 1024), ("qgt", 512), ("kd", 512)])
        mg = carve(scr, [("sg", 2048), ("prod", 2048), ("m", 2048), ("o", 2048), ("post", 1024)])
        ff = carve(scr, [("sg", 512), ("h", 512)])
        ml = carve(scr, [("buf", 2048), ("q", 4096), ("k", 4096), ("v", 2048), ("y", 2048)])
        mlc = carve(late, [("c", 1280), ("rot", 1024), ("kr", 512)])
        ns = carve(scr, [("buf", 2048), ("q", 2048), ("ks", 1024), ("kw", 1024), ("vs", 512), ("vw", 512),
                         ("xk", 1024), ("xv", 1024), ("bias", 4096), ("cbias", 512)])
        nl = carve(late, [("w1", 4096), ("y", 2048), ("vc", 1024)])
        nt_ = carve(late, [("hot", 512), ("tbl", 16), ("line", 512)], 4096)

        sems = {}

        def s_(name):
            if name not in sems:
                sems[name] = ctx.enter_context(nc.semaphore(name))
            return sems[name]

        raw_here = [s_(f"raw_here{i}") for i in range(SLOTS)]
        w_high, w_low, w_used = s_("w_high"), s_("w_low"), s_("w_used")
        bank_done = [s_("bank_done0"), s_("bank_done1")]

        def val(base, i):
            return base if i is None else i[0] * i[1] + base

        def by(i, step):
            return None if i is None else (i, step)

        def split_high(act, t, i=None):
            act.wait_ge(raw_here[t % SLOTS], val(16 * (t // SLOTS + 1), by(i, 16)))
            if t >= SLOTS:
                act.wait_ge(w_used, val(t - SLOTS + 1, by(i, SLOTS)))
            nc.scalar.activation(high[t % SLOTS][:], raw[t % SLOTS][:], ACT.Copy).then_inc(w_high, 1)

        def split_low(dve, t, i=None):
            dve.wait_ge(w_high, val(t + 1, by(i, SLOTS)))
            nc.vector.tensor_tensor(low[t % SLOTS][:], raw[t % SLOTS][:], high[t % SLOTS][:].bitcast(F32),
                                    ALU.subtract).then_inc(w_low, 1)

        def plain_free(name):
            return UNIT[name] // 2

        def bank_of(name):
            return 4 + UNIT[name] % 2

        class Chain:

            def __init__(self, eng, name):
                self.eng, self.sem, self.n = eng, s_(name), 0

            def mark(self, ins):
                ins.then_inc(self.sem, 1)
                self.n += 1

            def link(self, ins):
                self.mark(ins)
                self.eng.wait_ge(self.sem, self.n)

            def join(self):
                self.eng.wait_ge(self.sem, self.n)

        as3 = lambda ap, n: ap.rearrange("p (t c) -> p t c", t=n)
        TURNS = {
            "mem": (xs, 8, "mem", nth, ntl), "pre": (xs, 8, "pre", nth, ntl),
            "ym": (as3(xm["y"], TT), 4, None, yth[:, 3], ytl[:, 3]),
            "yc": (as3(sw["y"], TT), 4, None, yth[:, 2], ytl[:, 2]),
            "ya": (as3(dn["kt"], TT), 4, None, yth[:, 0], ytl[:, 0]),
            "f0": (xs, 8, "fa0", nth, ntl), "mx0": (xs, 8, "mx0", nth, ntl),
            "mlc": (as3(mlc["c"], TT), 5, "qn", nth, ntl),
            "mly": (as3(ml["y"], TT), 8, None, nth, ntl),
            "f1": (xs, 8, "fb0", nth, ntl), "f2": (xs, 8, "fa1", nth, ntl),
            "mx1": (xs, 8, "mx1", nth, ntl), "nsy": (as3(nl["y"], TT), 8, None, nth, ntl),
            "f3": (xs, 8, "fb1", nth, ntl),
        }
        turn_at, n_ = {}, 0
        for name, spec in TURNS.items():
            turn_at[name] = n_
            n_ += (spec[1] + 1) // 2
        turned, turn_high, turn_low = s_("turned"), s_("turn_high"), s_("turn_low")

        def turn_banks(name):
            n = TURNS[name][1]
            return [(b, turn_at[name] + b + 1, range(2 * b, min(2 * b + 2, n))) for b in range((n + 1) // 2)]

        def pe_turn(pe, name):
            src = TURNS[name][0]
            for b, count, chunks in turn_banks(name):
                for c in chunks:
                    for t in range(TT):
                        at = 256 * (c - 2 * b) + P * t
                        last = nc.tensor.transpose(ps[b][:, at:at + P], src[:, t, P * c:P * c + P], ident)
                last.then_inc(turned, 1)

        def act_turn(act, name):
            _, _, gain, high_, _ = TURNS[name]
            for b, count, chunks in turn_banks(name):
                act.wait_ge(turned, count)
                if gain is None:
                    n = len(chunks)
                    last = nc.scalar.activation(high_[:, 2 * b:2 * b + n, :], r3(ps[b][:, 0:256 * n], n), ACT.Copy)
                else:
                    for c in chunks:
                        at = 256 * (c - 2 * b)
                        last = nc.scalar.activation(high_[:, c, :], ps[b][:, at:at + 256], ACT.Copy,
                                                    scale=vcol(gain, c))
                last.then_inc(turn_high, 1)

        def dve_turn(dve, name):
            _, _, gain, high_, low_ = TURNS[name]
            for b, count, chunks in turn_banks(name):
                dve.wait_ge(turn_high, count)
                if gain is None:
                    n = len(chunks)
                    last = nc.vector.tensor_tensor(low_[:, 2 * b:2 * b + n, :], r3(ps[b][:, 0:256 * n], n),
                                                   high_[:, 2 * b:2 * b + n, :].bitcast(F32), ALU.subtract)
                else:
                    for c in chunks:
                        at = 256 * (c - 2 * b)
                        last = nc.vector.scalar_tensor_tensor(
                            out=low_[:, c, :], in0=ps[b][:, at:at + 256], scalar=vcol(gain, c),
                            in1=high_[:, c, :].bitcast(F32), op0=ALU.mult, op1=ALU.subtract)
                last.then_inc(turn_low, 1)

        def turn_done(name):
            return turn_at[name] + len(turn_banks(name))

        NORMS = ["mem", "pre", "post", "f0", "mx0", "f1", "f2", "mx1", "f3", "final"]
        norm_src = {"mem": scr[:, 0:TT * D].rearrange("p (t c) -> p t c", t=TT), "post": as3(mg["o"], TT)}
        norm_ss = {n: tiny(TT) for n in NORMS}
        norm_ms = {n: tiny(TT) for n in NORMS}
        norm_rs = {n: tiny(TT) for n in NORMS}
        power = tiny(16)
        one_col = tiny(1)
        mark_col = tiny(1)
        norm_sum, norm_mean, norm_root, norm_scaled = (s_(n) for n in ("norm_sum", "norm_mean", "norm_root",
                                                                      "norm_scaled"))

        def act_norm(act, name):
            src = norm_src.get(name, x)
            for t in range(TT):
                nc.scalar.activation(xs[:, t, :], src[:, t, :], ACT.Square,
                                     accum_out=norm_ss[name][:, t:t + 1]).then_inc(norm_sum, 1)

        def pool_norm(pool, name):
            n = NORMS.index(name)
            pool.wait_ge(norm_sum, TT * (n + 1))
            nc.gpsimd.tensor_scalar(norm_ms[name], norm_ss[name], 1.0 / D, EPS, ALU.mult, ALU.add)\
                .then_inc(norm_mean, 1)
            pool.wait_ge(norm_mean, n + 1)
            nc.gpsimd.tensor_tensor(norm_rs[name], norm_ms[name], power[:, 0:TT], ALU.pow).then_inc(norm_root, 1)

        def dve_norm(dve, name):
            n = NORMS.index(name)
            src = norm_src.get(name, x)
            dve.wait_ge(norm_root, n + 1)
            for t in range(TT):
                nc.vector.tensor_scalar(xs[:, t, :], src[:, t, :], norm_rs[name][:, t:t + 1], None, ALU.mult)\
                    .then_inc(norm_scaled, 1)

        def pe_norm(pe, name):
            pe.wait_ge(norm_scaled, TT * (NORMS.index(name) + 1))
            pe_turn(pe, name)

        def split_product(out_, stat, mov, first, last):
            nc.tensor.matmul(out_, stat[0], mov[0], start=first, stop=False, skip_group_check=True)
            nc.tensor.matmul(out_, stat[0], mov[1], start=False, stop=False, skip_group_check=True)
            return nc.tensor.matmul(out_, stat[1], mov[0], start=False, stop=last, skip_group_check=True)

        def slot(t, k, w):
            return [h[t % SLOTS][:, 0:k * w].rearrange("p (k w) -> p k w", k=k) for h in (high, low)]

        def weights_here(pe, t, i=None):
            pe.wait_ge(w_low, val(t + 1, by(i, SLOTS)))

        def by_feature(out_, wt, col, act_, ks, k0=0):
            for k in range(ks):
                last = split_product(out_, [w[:, k, col:col + P] for w in wt],
                                     [a[:, k0 + k, :] for a in act_], k == 0, k == ks - 1)
            return last

        def by_token(out_, wt, col, n, act_, ks, t, k0=0):
            for k in range(ks):
                last = split_product(out_, [a[:, k0 + k, P * t:P * t + P] for a in act_],
                                     [w[:, k, col:col + n] for w in wt], k == 0, k == ks - 1)
            return last

        NT_ = (nth, ntl)

        def pe_plain(pe, name, kind):
            t, out_ = TILE[name], ps[bank_of(name)]
            weights_here(pe, t)
            if UNIT[name] >= 2:
                pe.wait_ge(bank_done[UNIT[name] % 2], plain_free(name))
            if kind == "F":
                for j in range(2):
                    last = by_feature(out_[:, S * j:S * j + S], slot(t, KC, CW), P * j, NT_, KC)
            elif kind == "T":
                for j in range(TT):
                    last = by_token(out_[:, CW * j:CW * j + CW], slot(t, KC, CW), 0, CW, NT_, KC, j)
            elif kind == "FT":
                by_feature(out_[:, 0:S], slot(t, KC, CW), 0, NT_, KC)
                for j in range(TT):
                    last = by_token(out_[:, S + P * j:S + P * j + P], slot(t, KC, CW), P, P, NT_, KC, j)
            elif kind == "TF":
                for j in range(TT):
                    by_token(out_[:, P * j:P * j + P], slot(t, KC, CW), 0, P, NT_, KC, j)
                last = by_feature(out_[:, S:2 * S], slot(t, KC, CW), P, NT_, KC)
            else:
                n = kind
                for j in range(TT):
                    last = by_token(out_[:, n * j:n * j + n], slot(t, KC, n), 0, n, NT_, KC, j)
            last.then_inc(w_used, 1)

        def read_bank(eng, name):
            eng.wait_ge(w_used, TILE[name] + 1)
            return ps[bank_of(name)]

        def bank_read(name, ins):
            ins.then_inc(bank_done[UNIT[name] % 2], 1)

        def wait_bank(eng, name):
            eng.wait_ge(bank_done[UNIT[name] % 2], UNIT[name] // 2 + 1)

        UNITS = []
        for h in range(XM_H):
            UNITS.append(dict(q=xm["q"][:, S * h:S * h + S], k=xm["k"][:, S * h:S * h + S],
                              v=[r3(xm["v"], TT)[:, t, P * h:P * h + P] for t in range(TT)],
                              d=P, causal=False, mask=None, scale=P ** -0.5))
        for h in range(SW_H):
            p0, kv = 64 * (h % 2), h // (SW_H // SW_KV)
            UNITS.append(dict(q=sw["q"][p0:p0 + 64, S * (h // 2):S * (h // 2) + S],
                              k=sw["k"][p0:p0 + 64, S * kv:S * kv + S],
                              v=[r3(sw["v"], TT)[:, t, 64 * kv:64 * kv + 64] for t in range(TT)],
                              d=64, causal=True, mask=window, scale=SW_D ** -0.5))
        for h in range(MLA_H):
            UNITS.append(dict(q=r3(ml["q"], MLA_H)[0:96, h, :], k=r3(ml["k"], MLA_H)[0:96, h, :],
                              v=[r3(ml["v"], TT)[:, t, 64 * h:64 * h + 64] for t in range(TT)],
                              d=64, causal=True, mask=causal, scale=(MLA_N + MLA_R) ** -0.5))
        for kk, vv in (("ks", "vs"), ("kw", "vw")):
            for h in range(NSA_H):
                p0, g = 64 * (h % 2), h // NSA_R
                UNITS.append(dict(q=ns["q"][p0:p0 + 64, S * (h // 2):S * (h // 2) + S],
                                  k=ns[kk][p0:p0 + 64, S * g:S * g + S],
                                  v=[r3(ns[vv], TT)[:, t, 64 * g:64 * g + 64] for t in range(TT)],
                                  d=64, causal=True, mask=r3(ns["bias"], NSA_H)[:, h, ::-1], scale=NSA_D ** -0.5))
        XM0, SW0 = 0, XM_H
        MLA0 = SW0 + SW_H
        NSA0 = MLA0 + MLA_H
        at_scored, at_max, at_exp, at_turned, at_out, at_read = (
            s_(n) for n in ("at_scored", "at_max", "at_exp", "at_turned", "at_out", "at_read"))
        at_copied = [s_("at_copied0"), s_("at_copied1")]
        at_mx, at_nm, at_sum, at_inv, at_sinkexp = ([tiny(TT) for _ in range(4)] for _ in range(5))
        neg_sink = tiny(SW_H)
        def cols_of(u, t):
            return slice(0, 256) if t == 1 else slice(256, 384 if u["causal"] else 512)

        def pe_units(pe, first, n):
            def scores(a):
                u = UNITS[a]
                if a >= 2:
                    pe.wait_ge(at_max if u["causal"] and UNITS[a - 2]["causal"] else at_exp, a - 1)
                for t in (1, 0):
                    c = cols_of(u, t)
                    last = nc.tensor.matmul(ps[a % 2][:, c], u["q"][:, P * t:P * t + P],
                                            u["k"][:, 0:c.stop - c.start], start=True, stop=True)
                last.then_inc(at_scored, 1)

            def turn_probs(a):
                u = UNITS[a]
                pe.wait_ge(at_exp, a + 1)
                if a >= 2:
                    pe.wait_ge(at_copied[a % 2], a // 2)
                for c in range(0, cols_of(u, 0).stop, P):
                    last = nc.tensor.transpose(ps[2 + a % 2][:, c:c + P], at_s[a % 2][:, c:c + P], ident)
                last.then_inc(at_turned, 1)

            def values(a):
                u = UNITS[a]
                pe.wait_ge(at_copied[a % 2], a // 2 + 1)
                if a >= 2:
                    pe.wait_ge(at_read, a - 1)
                d = u["d"]
                for t in (0, 1):
                    c = cols_of(u, t)
                    n_k = (c.stop - c.start) // P
                    for kt in range(n_k):
                        last = nc.tensor.matmul(ps[6 + a % 2][:, d * t:d * t + d],
                                                at_p[a % 2][:, c.start + P * kt:c.start + P * kt + P],
                                                u["v"][kt], start=kt == 0, stop=kt == n_k - 1)
                last.then_inc(at_out, 1)

            for a in range(first, first + n + 2):
                if a < first + n:
                    scores(a)
                if first <= a - 1 < first + n:
                    turn_probs(a - 1)
                if first <= a - 2:
                    values(a - 2)

        def copy_probs(eng, a):
            w = cols_of(UNITS[a], 0).stop
            eng.wait_ge(at_turned, a + 1)
            if a >= 2:
                eng.wait_ge(at_out, a - 1)
            if a % 2 == 0:
                ins = nc.scalar.activation(at_p[0][:, 0:w], ps[2][:, 0:w], ACT.Copy)
            else:
                ins = nc.vector.tensor_copy(at_p[1][:, 0:w], ps[3][:, 0:w])
            ins.then_inc(at_copied[a % 2], 1)

        def act_units(act, first, n, sinks=False):
            for a in range(first, first + n + 1):
                if a < first + n:
                    u, b, b4 = UNITS[a], a % 2, a % 4
                    act.wait_ge(at_max, a + 1)
                    if a >= 2:
                        act.wait_ge(at_turned, a - 1)
                    if a >= 4:
                        act.wait_ge(at_read, a - 3)
                    src = at_s[b] if u["causal"] else ps[b]
                    if sinks:
                        nc.scalar.activation(at_sinkexp[b4], at_nm[b4], ACT.Exp,
                                             bias=row[:, ROW["sink"] + a - first:ROW["sink"] + a - first + 1])
                    for t in (1, 0):
                        c = cols_of(u, t)
                        last = nc.scalar.activation(at_s[b][:, c], src[:, c], ACT.Exp, scale=u["scale"],
                                                    bias=at_nm[b4][:, t:t + 1], accum_out=at_sum[b4][:, t:t + 1])
                    last.then_inc(at_exp, 1)
                if a - 1 >= first and (a - 1) % 2 == 0:
                    copy_probs(act, a - 1)

        def dve_units(dve, ch, first, n, evac, sinks=False):
            for a in range(first, first + n + 2):
                if a < first + n:
                    u, b, b4 = UNITS[a], a % 2, a % 4
                    dve.wait_ge(at_scored, a + 1)
                    if a >= 2:
                        dve.wait_ge(at_turned, a - 1)
                        dve.wait_ge(at_exp, a - 1)
                    if u["causal"]:
                        for t in (1, 0):
                            c = cols_of(u, t)
                            m = u["mask"] if t == 1 else u["mask"][:, P:2 * P]
                            ch.mark(nc.vector.tensor_tensor_reduce(at_s[b][:, c], ps[b][:, c], m, 1.0, -3e38,
                                                                   ALU.add, ALU.max, at_mx[b4][:, t:t + 1]))
                    else:
                        for t in (1, 0):
                            ch.mark(nc.vector.tensor_reduce(at_mx[b4][:, t:t + 1], ps[b][:, cols_of(u, t)],
                                                            AX.X, ALU.max))
                    ch.join()
                    if sinks:
                        ins = nc.vector.tensor_scalar(at_nm[b4], at_mx[b4], -u["scale"],
                                                      neg_sink[:, a - first:a - first + 1], ALU.mult, ALU.min)
                    else:
                        ins = nc.vector.tensor_scalar(at_nm[b4], at_mx[b4], -u["scale"], None, ALU.mult)
                    ins.then_inc(at_max, 1)
                if first <= a - 1 < first + n and (a - 1) % 2 == 1:
                    copy_probs(dve, a - 1)
                if first <= a - 2:
                    b, b4 = a % 2, (a - 2) % 4
                    dve.wait_ge(at_exp, a - 1)
                    if sinks:
                        ch.link(nc.vector.tensor_tensor(at_sum[b4], at_sum[b4], at_sinkexp[b4], ALU.add))
                    ch.link(nc.vector.reciprocal(at_inv[b4], at_sum[b4]))
                    dve.wait_ge(at_out, a - 1)
                    evac(a - 2, ps[6 + b], at_inv[b4]).then_inc(at_read, 1)


        def bc(ap, n):
            return ap.unsqueeze(2).broadcast_to([ap.shape[0], ap.shape[1], n])

        def rep(ap, n):
            return ap.unsqueeze(1).broadcast_to([ap.shape[0], n, ap.shape[1]])

        inputs_here, x_ready = s_("inputs_here"), s_("x_ready")
        UPDATES = ["post", "ffn0", "mla", "ffn1", "ffn2", "nsa", "ffn3"]
        xup = lambda name: UPDATES.index(name) + 1
        setup_done = s_("setup_done")

        def act_step(act, name):
            if TILE[name] + 2 < NT:
                split_high(act, TILE[name] + 2)

        def dve_step(dve, name):
            if TILE[name] + 2 < NT:
                split_low(dve, TILE[name] + 2)

        gm_loaded, gm_sum, gm_mean, gm_root, gm_vn, gm_wturned, gm_wmask, gm_mixed, gm_y, gm_high, gm_low = (
            s_("gm_" + n) for n in ("loaded", "sum", "mean", "root", "vn", "wturned", "wmask", "mixed", "y",
                                    "high", "low"))
        gm_ss, gm_ms, gm_rs = tiny(TT), tiny(TT), tiny(TT)

        d_ba = tiny(16)
        d_beta, d_z, d_az, d_l, d_sp, d_ea, d_g, d_egc, d_dm, d_ekd = (tiny(PAIRS) for _ in range(10))
        d_gc = tiny(16)
        d_ss, d_ms, d_rs = tiny(16), tiny(16), tiny(16)
        d_os, d_om, d_or = tiny(PAIRS), tiny(PAIRS), tiny(PAIRS)
        cin = dn["cin"].rearrange("p (c t) -> p c t", c=12)
        cact = dn["cact"].rearrange("p (c t) -> p c t", c=12)
        tok = dn["tok"].rearrange("p (t c d) -> p t c d", t=TT, c=12)
        d_T, d_TT, d_P = (dn["cin"][:, 1024 * n:1024 * n + 1024] for n in range(3))
        d_E, d_Es, d_Lm = (dn["cact"][:, 1024 * n:1024 * n + 1024] for n in range(3))
        d_L, d_A = dn["kb"], dn["qt"]
        d_u, d_wt, d_S, d_vn = (dn["cact"][:, a:b] for a, b in ((0, 1024), (1024, 1536), (1536, 2048),
                                                              (2048, 2560)))
        d_qg = dn["cin"][:, 2048:2560]
        d_kbt = xs[:, 0, :]
        d_level = xs[:, 1, 0:LEVELS * P].rearrange("p (l i) -> p l i", l=LEVELS)
        d_sz = late[:, 3072:4096]
        heads = lambda ap: ap.rearrange("p (t h d) -> p t h d", t=TT, h=DN_H)
        pair = lambda ap, n: ap[:, P * n:P * n + P]
        (dn_conv, dn_act, dn_turn, dn_tok, dn_sum, dn_mean, dn_root, dn_ready, dn_fm, dn_fa, dn_fd, dn_absz,
         dn_exps, dn_g, dn_gcs, dn_gcd, dn_egs, dn_diff, dn_ed, dn_mask, dn_kk, dn_la, dn_lm, dn_p, dn_pc, dn_y,
         dn_t, dn_u, dn_uc, dn_wc, dn_o0, dn_sc, dn_ws, dn_vnd, dn_o1, dn_osum, dn_omean, dn_oroot, dn_out,
         dn_level, dn_zeroed, dn_setup) = (
            s_("dn_" + n) for n in ("conv", "act", "turn", "tok", "sum", "mean", "root", "ready", "fm", "fa", "fd",
                                    "absz", "exps", "g", "gcs", "gcd", "egs", "diff", "ed", "mask", "kk", "la",
                                    "lm", "p", "pc", "y", "t", "u", "uc", "wc", "o0", "sc", "ws", "vnd", "o1",
                                    "osum", "omean", "oroot", "out", "level", "zeroed", "setup"))
        kn_ = lambda t: [tok[:, t, 4 + h, :] for h in range(DN_H)]
        qn_ = lambda t: [tok[:, t, h, :] for h in range(DN_H)]
        DN_TURNS = [
            (kn_(0), dn["kt"][:, 0:512], 0), (kn_(1), dn["kt"][:, 512:1024], 1),
            (qn_(0), dn["qt"][:, 0:512], 2), (qn_(1), dn["qt"][:, 512:1024], 3),
            ([pair(dn["kb"], h) for h in range(4)], d_kbt[:, 0:512], 6),
            ([pair(dn["kb"], 4 + h) for h in range(4)], d_kbt[:, 512:1024], 7),
            ([pair(d_qg, h) for h in range(4)], dn["qgt"], 0),
        ]

        def attention_evac(y, first, d, z=None):
            def evac(a, o, inv):
                h = a - first
                for t in range(TT):
                    c = slice(d * h, d * h + d)
                    if z is None:
                        last = nc.vector.tensor_scalar(y[:, t, c], o[:, d * t:d * t + d], inv[:, t:t + 1], None,
                                                       ALU.mult)
                    else:
                        last = nc.vector.scalar_tensor_tensor(out=y[:, t, c], in0=o[:, d * t:d * t + d],
                                                              scalar=inv[:, t:t + 1], in1=z[:, t, c],
                                                              op0=ALU.mult, op1=ALU.mult)
                return last
            return evac

        ff_gate, ff_h, ff_hhigh, ff_hlow = (s_("ff_" + n) for n in ("gate", "h", "hhigh", "hlow"))
        NS_ = ff["sg"], ff["h"]

        def pe_ffn(pe, f):
            tb = TILE[f"f{f}g0"]
            n0 = FT * f

            def gate(t, c, i=None):
                weights_here(pe, t, i)
                if c > 0:
                    pe.wait_ge(ff_gate, val(c, by(i, 1)))
                for j in range(2):
                    last = by_feature(ps[4][:, S * j:S * j + S], slot(t, KC, CW), P * j, NT_, KC)
                last.then_inc(w_used, 1)

            def up(t, c, i=None):
                weights_here(pe, t, i)
                if c > 0:
                    pe.wait_ge(ff_h, val(c, by(i, 1)))
                for j in range(2):
                    last = by_feature(ps[5][:, S * j:S * j + S], slot(t, KC, CW), P * j, NT_, KC)
                last.then_inc(w_used, 1)

            def down(t, c, i=None, first=False, last_=False):
                weights_here(pe, t, i)
                pe.wait_ge(ff_hlow, val(c + 1, by(i, 1)))
                w = slot(t, 2, D)
                for tt in range(TT):
                    for half in range(2):
                        for j in range(2):
                            last = split_product(ps[2 * tt + half][:, :],
                                                 [h[:, j, P * tt:P * tt + P] for h in (hth, htl)],
                                                 [a[:, j, 512 * half:512 * half + 512] for a in w],
                                                 first and j == 0, last_ and j == 1)
                last.then_inc(w_used, 1)

            gate(tb, n0)
            up(tb + 1, n0)
            gate(tb + 2, n0 + 1)
            up(tb + 3, n0 + 1)
            down(tb + 4, n0, first=True)
            with pe.Fori(0, FT - 2) as i:
                gate(tb + 5, n0 + 2, i)
                up(tb + 6, n0 + 2, i)
                down(tb + 7, n0 + 1, i)
            down(tb + 3 * FT - 1, n0 + FT - 1, last_=True)

        def act_ffn(act, f):
            tb = TILE[f"f{f}g0"]
            n0 = FT * f

            def gated(t, c, i=None):
                act.wait_ge(w_used, val(t + 1, by(i, SLOTS)))
                if c > 0:
                    act.wait_ge(ff_h, val(c, by(i, 1)))
                nc.scalar.activation(ff["sg"], ps[4][:, :], ACT.Silu).then_inc(ff_gate, 1)

            def rounded(t_down_before, c, i=None):
                act.wait_ge(ff_h, val(c + 1, by(i, 1)))
                if t_down_before is not None:
                    act.wait_ge(w_used, val(t_down_before + 1, by(i, SLOTS)))
                nc.scalar.activation(hth[:, :, :], r3(ff["h"], 2), ACT.Copy).then_inc(ff_hhigh, 1)

            split_high(act, tb + 2)
            gated(tb, n0)
            split_high(act, tb + 3)
            split_high(act, tb + 4)
            rounded(None, n0)
            gated(tb + 2, n0 + 1)
            split_high(act, tb + 5)
            split_high(act, tb + 6)
            rounded(tb + 4, n0 + 1)
            with act.Fori(0, FT - 2) as i:
                split_high(act, tb + 7, i)
                gated(tb + 5, n0 + 2, i)
                split_high(act, tb + 8, i)
                split_high(act, tb + 9, i)
                rounded(tb + 7, n0 + 2, i)
            if tb + 3 * FT + 1 < NT:
                split_high(act, tb + 3 * FT + 1)

        def dve_ffn(dve, f):
            tb = TILE[f"f{f}g0"]
            n0 = FT * f

            def hidden(t, c, i=None):
                dve.wait_ge(w_used, val(t + 1, by(i, SLOTS)))
                dve.wait_ge(ff_gate, val(c + 1, by(i, 1)))
                if c > 0:
                    dve.wait_ge(ff_hlow, val(c, by(i, 1)))
                nc.vector.tensor_tensor(ff["h"], ff["sg"], ps[5][:, :], ALU.mult).then_inc(ff_h, 1)

            def rest(c, i=None):
                dve.wait_ge(ff_hhigh, val(c + 1, by(i, 1)))
                nc.vector.tensor_tensor(htl[:, :, :], r3(ff["h"], 2), hth[:, :, :].bitcast(F32), ALU.subtract)\
                    .then_inc(ff_hlow, 1)

            split_low(dve, tb + 2)
            split_low(dve, tb + 3)
            hidden(tb + 1, n0)
            split_low(dve, tb + 4)
            rest(n0)
            split_low(dve, tb + 5)
            hidden(tb + 3, n0 + 1)
            split_low(dve, tb + 6)
            rest(n0 + 1)
            with dve.Fori(0, FT - 2) as i:
                split_low(dve, tb + 7, i)
                split_low(dve, tb + 8, i)
                hidden(tb + 6, n0 + 2, i)
                split_low(dve, tb + 9, i)
                rest(n0 + 2, i)
            if tb + 3 * FT + 1 < NT:
                split_low(dve, tb + 3 * FT + 1)
            dve.wait_ge(w_used, tb + 3 * FT)
            for tt in range(TT):
                for half in range(2):
                    xo = x[:, tt, 512 * half:512 * half + 512]
                    last = nc.vector.scalar_tensor_tensor(out=xo, in0=ps[2 * tt + half][:, :], scalar=0.5,
                                                          in1=xo, op0=ALU.mult, op1=ALU.add)
            last.then_inc(x_ready, 1)


        mg_sig, mg_mul, mg_add, mg_high, mg_low, mg_post, mg_posted, mg_zero = (
            s_("mg_" + n) for n in ("sig", "mul", "add", "high", "low", "post", "posted", "zero"))
        MB = TILE["gate000"]

        def pe_merge_branch(pe, n, i=None):
            def at(t):
                return t, (i, 2 * SLOTS) if i is not None else None
            for half in range(2):
                for g in range(2):
                    t = MB + 6 * n + 3 * half + g
                    pe.wait_ge(w_low, val(t + 1, by(i, 6)))
                    q = 4 * n + 2 * half + g
                    if q >= 2:
                        pe.wait_ge(mg_sig, val(q - 1, by(i, 4)))
                    for j in range(2):
                        last = by_feature(ps[4 + g][:, S * j:S * j + S], slot(t, KC, CW), P * j, NT_, KC)
                    last.then_inc(w_used, 1)
                t = MB + 6 * n + 3 * half + 2
                pe.wait_ge(w_low, val(t + 1, by(i, 6)))
                u = 2 * (2 * n + half)
                if u >= 2:
                    pe.wait_ge(mg_mul, val(u, by(i, 4)))
                ys = (yth[:, n, :, :], ytl[:, n, :, :]) if i is None else \
                    tuple(y[:, bass.ds(i + n, 1), :, :].rearrange("p o k s -> p (o k) s") for y in (yth, ytl))
                for c in range(4):
                    last = by_feature(ps[c // 2][:, S * (c % 2):S * (c % 2) + S], slot(t, 4, 512), P * c,
                                      ys, 4)
                last.then_inc(w_used, 1)

        def act_merge_branch(act, n, i=None):
            for half in range(2):
                for g in range(2):
                    t = MB + 6 * n + 3 * half + g
                    merge_split_high(act, t + 2, i)
                    act.wait_ge(w_used, val(t + 1, by(i, 6)))
                    if n > 0:
                        act.wait_ge(mg_mul, val(4 * (n - 1) + 2 * half + g + 1, by(i, 4)))
                    nc.scalar.activation(mg["sg"][:, 1024 * half + 512 * g:1024 * half + 512 * g + 512],
                                         ps[4 + g][:, :], ACT.Sigmoid).then_inc(mg_sig, 1)
                merge_split_high(act, MB + 6 * n + 3 * half + 4, i)

        def merge_split_high(act, t, i):
            act.wait_ge(raw_here[t % SLOTS], val(16 * (t // SLOTS + 1), by(i, 32)))
            act.wait_ge(w_used, val(t - SLOTS + 1, by(i, 6)))
            nc.scalar.activation(high[t % SLOTS][:], raw[t % SLOTS][:], ACT.Copy).then_inc(w_high, 1)

        def merge_split_low(dve, t, i):
            dve.wait_ge(w_high, val(t + 1, by(i, 6)))
            nc.vector.tensor_tensor(low[t % SLOTS][:], raw[t % SLOTS][:], high[t % SLOTS][:].bitcast(F32),
                                    ALU.subtract).then_inc(w_low, 1)

        def dve_merge_branch(dve, n, i=None):
            for half in range(2):
                t = MB + 6 * n + 3 * half
                merge_split_low(dve, t + 2, i)
                merge_split_low(dve, t + 3, i)
                merge_split_low(dve, t + 4, i)
                dve.wait_ge(w_used, val(t + 3, by(i, 6)))
                for b in range(2):
                    q = 4 * n + 2 * half + b
                    c = slice(1024 * half + 512 * b, 1024 * half + 512 * b + 512)
                    dve.wait_ge(mg_sig, val(q + 1, by(i, 4)))
                    if n > 0:
                        dve.wait_ge(mg_add, val(4 * (n - 1) + 2 * half + b + 1, by(i, 4)))
                    nc.vector.tensor_tensor(mg["prod"][:, c], ps[b][:, :], mg["sg"][:, c], ALU.mult)\
                        .then_inc(mg_mul, 1)
                for b in range(2):
                    q = 4 * n + 2 * half + b
                    c = slice(1024 * half + 512 * b, 1024 * half + 512 * b + 512)
                    dve.wait_ge(mg_mul, val(q + 1, by(i, 4)))
                    if n == 0 and i is None:
                        ins = nc.vector.tensor_copy(mg["m"][:, c], mg["prod"][:, c])
                    else:
                        ins = nc.vector.tensor_tensor(mg["m"][:, c], mg["m"][:, c], mg["prod"][:, c], ALU.add)
                    ins.then_inc(mg_add, 1)

        (ml_c, ml_kr, ml_ss, ml_ms, ml_rs, ml_cs, ml_q, ml_qa, ml_qd, ml_k, ml_ka, ml_kd, ml_v, ml_va, ml_krd) = (
            s_("ml_" + n) for n in ("c", "kr", "ss", "ms", "rs", "cs", "q", "qa", "qd", "k", "ka", "kd", "v",
                                    "va", "krd"))
        m_ss, m_ms, m_rs = tiny(4), tiny(4), tiny(4)
        mc = as3(mlc["c"], TT)
        MLC = [(t, c) for c in (slice(0, MLA_QL), slice(MLA_QL, MLA_QL + MLA_KVL)) for t in range(TT)]
        mq, mk_ = r3(ml["q"], MLA_H), r3(ml["k"], MLA_H)
        mrot = mlc["rot"].rearrange("p (r h s) -> p r h s", r=2, h=2)
        cos_, sin_ = c_("cos", S), c_("sin", S)

        (ns_w1, ns_tbl, ns_line, ns_linec, ns_lined, ns_bias, ns_cb, ns_cbc, ns_hid, ns_hc, ns_kc, ns_kcd, ns_vc,
         ns_vcd, ns_cs, ns_cm, ns_ce, ns_cg, ns_ct, ns_ctc, ns_co, ns_cy, ns_zero, ns_pos) = (
            s_("ns_" + n) for n in ("w1", "tbl", "line", "linec", "lined", "bias", "cb", "cbc", "hid", "hc", "kc",
                                    "kcd", "vc", "vcd", "cs", "cm", "ce", "cg", "ct", "ctc", "co", "cy", "zero",
                                    "pos"))
        n_gate = tiny(TT * 48)
        n_hid = [tiny(64), tiny(64)]
        n_pos, n_kc = tiny(2), tiny(NSA_G * NCMP)
        n_mx, n_sum, n_inv, n_cg = (tiny(TT * NSA_H) for _ in range(4))
        n_ag = [tiny(TT) for _ in range(2)]
        w2s = sb("w2s", [P, 2, 64])
        poss = sb("poss", [P, 2, CMP_L // 2])
        sc = xs[:, 0, :].rearrange("p (t h n) -> p t h n", t=TT, h=NSA_H)
        sct = xs[:, 1, :]
        gate3 = n_gate.rearrange("p (t h b) -> p t h b", t=TT, h=NSA_H)
        xx = [r3(ns["xk"], NSA_G), r3(ns["xv"], NSA_G)]
        w1s = nl["w1"].rearrange("p (m j f) -> p m j f", m=2, j=CMP_L // 2)
        vcd = r3(nl["vc"], NSA_G)
        nbias = r3(ns["bias"], NSA_H)
        ny = as3(nl["y"], TT)
        BIAS_ROWS = BUCKETS + 1

        def doubled(dst, bank, c_dst):
            src = r3(bank, 2)
            d = r3(dst, c_dst).rearrange("p (c two) s -> p two c s", two=2)
            for g in range(2):
                for half in range(2):
                    yield d[64 * half:64 * half + 64, g], src[64 * g:64 * g + 64]


        block = ctx.enter_context(nc.Block())

        @block.sync
        def _(sp):
            for t in range(SLOTS):
                sp.dma_start(raw[t][:], A["stream"][t]).then_inc(raw_here[t], 16)
            with sp.Fori(1, (NT - 1) // SLOTS) as i:
                for c in range(SLOTS):
                    tile = sp.snap(i * SLOTS + c)
                    sp.wait_ge(w_low, i * SLOTS + (c - SLOTS + 1))
                    sp.dma_start(raw[c][:], A["stream"][bass.ds(tile, 1)].rearrange("o p w -> (o p) w"))\
                        .then_inc(raw_here[c], 16)
            t = NT - 1
            sp.wait_ge(w_low, t - SLOTS + 1)
            sp.dma_start(raw[t % SLOTS][:], A["stream"][t]).then_inc(raw_here[t % SLOTS], 16)

        @block.gpsimd
        def _(pool):
            nc.gpsimd.memset(power, -0.5).then_inc(setup_done, 1)
            nc.gpsimd.memset(one_col, 1.0).then_inc(setup_done, 1)
            pool.wait_ge(setup_done, 2)
            pool_norm(pool, "mem")
            pool_norm(pool, "pre")
            pool.wait_ge(turn_low, turn_done("ym"))
            pool.dma_start(gm["w"], A["spatial"].rearrange("p g q -> p (g q)")).then_inc(gm_loaded, 16)
            pool.dma_start(xs[:, 1, 0:LEVELS * P], A["level"]).then_inc(dn_level, 16)
            pool.wait_ge(gm_sum, TT)
            nc.gpsimd.tensor_scalar(gm_ms, gm_ss, 1.0 / BW, EPS, ALU.mult, ALU.add).then_inc(gm_mean, 1)
            pool.wait_ge(gm_mean, 1)
            nc.gpsimd.tensor_tensor(gm_rs, gm_ms, power[:, 0:TT], ALU.pow).then_inc(gm_root, 1)
            pool.wait_ge(gm_low, 1)
            nc.gpsimd.memset(cin[:, :, 0:3], 0.0).then_inc(dn_zeroed, 1)
            pool.wait_ge(dn_sum, 1)
            nc.gpsimd.tensor_scalar(d_ms, d_ss, 1.0, EPS, ALU.mult, ALU.add).then_inc(dn_mean, 1)
            pool.wait_ge(dn_mean, 1)
            nc.gpsimd.tensor_tensor(d_rs, d_ms, power, ALU.pow).then_inc(dn_root, 1)
            pool.wait_ge(dn_osum, 1)
            nc.gpsimd.tensor_scalar(d_om, d_os, 1.0 / P, EPS, ALU.mult, ALU.add).then_inc(dn_omean, 1)
            pool.wait_ge(dn_omean, 1)
            nc.gpsimd.tensor_tensor(d_or, d_om, power[:, 0:PAIRS], ALU.pow).then_inc(dn_oroot, 1)
            pool.wait_ge(turn_low, turn_done("ya"))
            pool.dma_start(mg["post"], A["post"]).then_inc(mg_post, 16)
            pool_norm(pool, "post")
            pool_norm(pool, "f0")
            pool_norm(pool, "mx0")
            pool.wait_ge(ml_ss, 4)
            nc.gpsimd.tensor_scalar(m_ms[:, 0:2], m_ss[:, 0:2], 1.0 / MLA_QL, EPS, ALU.mult, ALU.add)\
                .then_inc(ml_ms, 1)
            nc.gpsimd.tensor_scalar(m_ms[:, 2:4], m_ss[:, 2:4], 1.0 / MLA_KVL, EPS, ALU.mult, ALU.add)\
                .then_inc(ml_ms, 1)
            pool.wait_ge(ml_ms, 2)
            nc.gpsimd.tensor_tensor(m_rs, m_ms, power[:, 0:4], ALU.pow).then_inc(ml_rs, 1)
            pool.wait_ge(x_ready, xup("mla"))
            pool.dma_start(nl["w1"], A["w1"].rearrange("p m w -> p (m w)")).then_inc(ns_w1, 16)
            pool.dma_start(w2s[:, :, :], A["w2"]).then_inc(ns_w1, 16)
            pool.dma_start(poss[:, :, :], A["pos"]).then_inc(ns_w1, 16)
            pool.dma_start(nt_["hot"][0:BIAS_ROWS, :], A["hot"]).then_inc(ns_tbl, 16)
            pool.dma_start(nt_["tbl"][0:BIAS_ROWS, :], A["bucket_bias"]).then_inc(ns_tbl, 16)
            nc.gpsimd.memset(nl["vc"], 0.0).then_inc(ns_zero, 1)
            pool_norm(pool, "f1")
            pool_norm(pool, "f2")
            pool_norm(pool, "mx1")
            pool.wait_ge(ns_linec, 1)
            pool.dma_start(line, nt_["line"][0:NSA_H, :]).then_inc(ns_lined, 16)
            pool.wait_ge(ns_lined, 16)
            pool.dma_start(nbias, bass.AP(line.tensor, S - P + 1, [[1, P], [2 * S, NSA_H], [1, S]]))\
                .then_inc(ns_bias, 16)
            pool.wait_ge(turn_low, turn_done("mx1"))
            nc.gpsimd.memset(xs[:, 0, :], 0.0).then_inc(ns_zero, 1)
            pool_norm(pool, "f3")
            pool.dma_start(scr[:, 4096:4096 + D], A["final"]).then_inc(mg_post, 16)
            pool_norm(pool, "final")

        @block.scalar
        def _(act):
            act.dma_start(norm_src["mem"], A["mem"]).then_inc(inputs_here, 16)
            act.dma_start(con[:], A["con"]).then_inc(inputs_here, 16)
            act.dma_start(vec[:], A["vec"]).then_inc(inputs_here, 16)
            act.dma_start(x[:, :, :], A["x"]).then_inc(inputs_here, 16)
            act.dma_start(row[:], A["row"]).then_inc(inputs_here, 16)
            act.wait_ge(inputs_here, 80)
            act_norm(act, "mem")
            split_high(act, 0)
            split_high(act, 1)
            act_turn(act, "mem")
            for name, dst in (("mk0", xm["k"][:, 0:512]), ("mk1", xm["k"][:, 512:1024])):
                act_step(act, name)
                bank_read(name, nc.scalar.activation(dst, read_bank(act, name)[:, :], ACT.Copy))
            act_step(act, "mv0")
            act_step(act, "mv1")
            act.wait_ge(turn_low, turn_done("mem"))
            act_norm(act, "pre")
            act.wait_ge(w_used, TILE["mv1"] + 1)
            act_turn(act, "pre")
            for j in range(2):
                name = f"xmq{j}"
                act_step(act, name)
                bank_read(name, nc.scalar.activation(xm["q"][:, 512 * j:512 * j + 512], read_bank(act, name)[:, :],
                                                     ACT.Copy))
            for j in range(2):
                name = f"xmz{j}"
                act_step(act, name)
                bank_read(name, nc.scalar.activation(as3(xm["z"], TT)[:, :, CW * j:CW * j + CW],
                                                     r3(read_bank(act, name), TT), ACT.Silu))
            act_units(act, XM0, XM_H)
            act_turn(act, "ym")
            for j in range(2):
                name = f"swq{j}"
                act_step(act, name)
                bank_read(name, nc.scalar.activation(sw["q"][:, 512 * j:512 * j + 512], read_bank(act, name)[:, :],
                                                     ACT.Copy))
            act_step(act, "swkv")
            for j in range(2):
                name = f"swz{j}"
                act_step(act, name)
                bank_read(name, nc.scalar.activation(as3(sw["z"], TT)[:, :, CW * j:CW * j + CW],
                                                     r3(read_bank(act, name), TT), ACT.Silu))
            act_units(act, SW0, SW_H, sinks=True)
            act_turn(act, "yc")
            for name, dst, func in (("gmu0", gm["u"][:, 0:512], ACT.Gelu_apprx_tanh),
                                    ("gmu1", gm["u"][:, 512:1024], ACT.Gelu_apprx_tanh),
                                    ("gmz0", gm["z"][:, 0:512], ACT.Silu), ("gmz1", gm["z"][:, 512:1024], ACT.Silu)):
                act_step(act, name)
                bank_read(name, nc.scalar.activation(dst, read_bank(act, name)[:, :], func))
            for j in range(2):
                name = f"gmv{j}"
                act_step(act, name)
                bank_read(name, nc.scalar.activation(as3(gm["v"], TT)[:, :, CW * j:CW * j + CW],
                                                     r3(read_bank(act, name), TT), ACT.Gelu_apprx_tanh))
            wait_bank(act, "gmv0")
            wait_bank(act, "gmv1")
            for t in range(TT):
                nc.scalar.activation(gm["sq"][:, 512 * t:512 * t + 512], gm["v"][:, 512 * t:512 * t + 512],
                                     ACT.Square, accum_out=gm_ss[:, t:t + 1]).then_inc(gm_sum, 1)
            act.wait_ge(gm_y, 1)
            nc.scalar.activation(yth[:, 1], r3(gm["sq"], 4), ACT.Copy).then_inc(gm_high, 1)
            ch = Chain(act, "act_chain")
            act_step(act, "ba")
            act.wait_ge(dn_zeroed, 1)
            act.wait_ge(gm_low, 1)
            for j in range(6):
                name = f"dn{j}"
                act_step(act, name)
                bank_read(name, nc.scalar.activation(cin[:, 2 * j:2 * j + 2, 3:3 + S], r3(read_bank(act, name), 2),
                                                     ACT.Copy))
                if j:
                    act.wait_ge(dn_conv, j)
                    nc.scalar.activation(cact[:, 2 * j - 2:2 * j, :], cact[:, 2 * j - 2:2 * j, :], ACT.Silu)\
                        .then_inc(dn_act, 1)
            for j in range(2):
                name = f"dnz{j}"
                act_step(act, name)
                bank_read(name, nc.scalar.activation(as3(d_sz, TT)[:, :, CW * j:CW * j + CW],
                                                     r3(read_bank(act, name), TT), ACT.Silu))
            act.wait_ge(dn_conv, 6)
            nc.scalar.activation(cact[:, 10:12, :], cact[:, 10:12, :], ACT.Silu).then_inc(dn_act, 1)
            wait_bank(act, "ba")
            nc.scalar.activation(r3(d_beta, TT), r3(d_ba, TT)[:, :, 0:DN_H], ACT.Sigmoid).then_inc(dn_exps, 1)
            act.wait_ge(dn_absz, 1)
            nc.scalar.activation(d_ea, rowof("alog", PAIRS), ACT.Exp).then_inc(dn_exps, 1)
            ch.link(nc.scalar.activation(d_l, d_az, ACT.Exp, scale=-1.0))
            nc.scalar.activation(d_l, d_l, ACT.Ln, bias=one_col).then_inc(dn_exps, 1)
            act.wait_ge(dn_gcd, 1)
            nc.scalar.activation(d_egc, d_gc[:, 0:PAIRS], ACT.Exp).then_inc(dn_egs, 1)
            nc.scalar.activation(d_ekd, d_dm, ACT.Exp).then_inc(dn_egs, 1)
            act.wait_ge(dn_diff, PAIRS)
            nc.scalar.activation(d_E, d_E, ACT.Exp).then_inc(dn_ed, 1)
            for n, (_, dst, b) in enumerate(DN_TURNS):
                if n % 2 == 0:
                    act.wait_ge(dn_fm, n + 1)
                    nc.scalar.activation(dst, ps[b][:, :], ACT.Copy).then_inc(dn_fa, 1)
            for l in range(LEVELS):
                act.wait_ge(dn_p, l + 1)
                for b in range(2):
                    ins = nc.scalar.activation(d_P[:, 512 * b:512 * b + 512], ps[b][:, :], ACT.Copy)
                ins.then_inc(dn_pc, 1)
            act.wait_ge(dn_u, 2)
            nc.scalar.activation(d_wt, ps[2][:, :], ACT.Copy).then_inc(dn_wc, 1)
            act.wait_ge(dn_o0, 2)
            nc.scalar.activation(d_S, ps[6][:, :], ACT.Copy).then_inc(dn_sc, 1)
            act_turn(act, "ya")
            act_merge_branch(act, 0)
            with act.Fori(0, NBR - 1) as i:
                act_merge_branch(act, 1, i)
            act.wait_ge(mg_add, 4 * NBR)
            act.wait_ge(w_used, TILE["up31"] + 1)
            for b in range(2):
                nc.scalar.activation(nth[:, 4 * b:4 * b + 4, :], r3(mg["m"][:, 1024 * b:1024 * b + 1024], 4),
                                     ACT.Copy).then_inc(mg_high, 1)
            for j in range(4):
                name = f"out{j}"
                act_step(act, name)
                bank_read(name, nc.scalar.activation(as3(mg["o"], TT)[:, :, CW * j:CW * j + CW],
                                                     r3(read_bank(act, name), TT), ACT.Copy))
            wait_bank(act, "out2")
            wait_bank(act, "out3")
            act_norm(act, "post")
            act.wait_ge(x_ready, xup("post"))
            act_norm(act, "f0")
            act_turn(act, "f0")
            act_ffn(act, 0)
            act.wait_ge(x_ready, xup("ffn0"))
            act_norm(act, "mx0")
            act_turn(act, "mx0")
            for j in range(2):
                name = f"mlain{j}"
                act_step(act, name)
                bank_read(name, nc.scalar.activation(mc[:, :, CW * j:CW * j + CW], r3(read_bank(act, name), TT),
                                                     ACT.Copy))
            act_step(act, "mlain2")
            wait_bank(act, "mlain0")
            wait_bank(act, "mlain1")
            wait_bank(act, "mlain2")
            for n, (t, c) in enumerate(MLC):
                w = c.stop - c.start
                nc.scalar.activation(xs[:, 0, 0:w] if n % 2 else xs[:, 1, 0:w], mc[:, t, c], ACT.Square,
                                     accum_out=m_ss[:, n:n + 1]).then_inc(ml_ss, 1)
                if n == 1:
                    act.wait_ge(ml_ss, 2)
            act_turn(act, "mlc")
            for j in range(4):
                act_step(act, f"uq{j}")
                for b in range(2):
                    act.wait_ge(ml_q, 2 * j + b + 1)
                    h = 4 * j + 2 * b
                    nc.scalar.activation(mq[0:64, h:h + 2, :], r3(ps[2 * (j % 2) + b][0:64, :], 2), ACT.Copy)\
                        .then_inc(ml_qa, 1)
            act_step(act, "uk")
            act.wait_ge(ml_k, 1)
            for b in range(4):
                nc.scalar.activation(mk_[0:64, 4 * b:4 * b + 4:2, :], r3(ps[b][0:64, :], 2), ACT.Copy)\
                    .then_inc(ml_ka, 1)
            act_step(act, "uv")
            act.wait_ge(ml_v, 1)
            for n in range(4):
                t, half = n // 2, n % 2
                nc.scalar.activation(as3(ml["v"], TT)[:, t, 512 * half:512 * half + 512], ps[4 + n][:, :], ACT.Copy)\
                    .then_inc(ml_va, 1)
            act_units(act, MLA0, MLA_H)
            act_turn(act, "mly")
            for j in range(4):
                act_step(act, f"mlao{j}")
            act.wait_ge(x_ready, xup("mla"))
            act_norm(act, "f1")
            act_turn(act, "f1")
            act_ffn(act, 1)
            act.wait_ge(x_ready, xup("ffn1"))
            act_norm(act, "f2")
            act_turn(act, "f2")
            act_ffn(act, 2)
            act.wait_ge(x_ready, xup("ffn2"))
            act_norm(act, "mx1")
            act_turn(act, "mx1")
            act.wait_ge(ns_line, 1)
            nc.scalar.activation(nt_["line"][0:NSA_H, :], ps[6][0:NSA_H, :], ACT.Copy, scale=NSA_D ** 0.5)\
                .then_inc(ns_linec, 1)
            for j in range(4):
                name = f"nq{j}"
                act_step(act, name)
                bank_read(name, nc.scalar.activation(ns["q"][:, 512 * j:512 * j + 512], read_bank(act, name)[:, :],
                                                     ACT.Copy))
            for name in ("nkc", "nvc", "nks"):
                act_step(act, name)
            act_step(act, "nvs")
            bank_read("nvs", nc.scalar.activation(ns["vs"], read_bank(act, "nvs")[:, :], ACT.Copy))
            act_step(act, "nkw")
            act_step(act, "nvw")
            bank_read("nvw", nc.scalar.activation(ns["vw"], read_bank(act, "nvw")[:, :], ACT.Copy))
            act_step(act, "ng")
            bank_read("ng", nc.scalar.activation(n_gate, read_bank(act, "ng")[:, 0:TT * 48], ACT.Sigmoid))
            act.wait_ge(ns_pos, 1)
            for m in range(2):
                nc.scalar.activation(n_hid[m][:, 0:NSA_G * NCMP], ps[1][:, 64 * m:64 * m + NSA_G * NCMP],
                                     ACT.Gelu_apprx_tanh, bias=n_pos[:, m:m + 1]).then_inc(ns_hc, 1)
            for t in range(TT):
                act.wait_ge(ns_cm, t + 1)
                nc.scalar.activation(sc[:, t, :, 0:NCMP], sc[:, t, :, 0:NCMP], ACT.Exp).then_inc(ns_ce, 1)
            act_units(act, NSA0, 2 * NSA_H)
            act_turn(act, "nsy")
            for j in range(4):
                act_step(act, f"nsao{j}")
            act.wait_ge(x_ready, xup("nsa"))
            act_norm(act, "f3")
            act_turn(act, "f3")
            act_ffn(act, 3)
            act.wait_ge(x_ready, xup("ffn3"))
            act_norm(act, "final")
            act.wait_ge(mg_posted, 2)
            act.dma_start(out, x[:, :, :]).then_inc(inputs_here, 16)
            act.wait_ge(inputs_here, 96)

        @block.vector
        def _(dve):
            ch = Chain(dve, "dve_chain")
            dve.wait_ge(inputs_here, 80)
            nc.vector.tensor_scalar(neg_sink, rowof("sink", SW_H), -1.0, None, ALU.mult).then_inc(dn_setup, 1)
            dve_norm(dve, "mem")
            split_low(dve, 0)
            split_low(dve, 1)
            dve_turn(dve, "mem")
            dve_step(dve, "mk0")
            dve_step(dve, "mk1")
            for j in range(2):
                name = f"mv{j}"
                dve_step(dve, name)
                bank_read(name, nc.vector.tensor_copy(as3(xm["v"], TT)[:, :, CW * j:CW * j + CW],
                                                      r3(read_bank(dve, name), TT)))
            dve_norm(dve, "pre")
            dve_turn(dve, "pre")
            for name in ("xmq0", "xmq1", "xmz0", "xmz1"):
                dve_step(dve, name)
            wait_bank(dve, "xmz0")
            wait_bank(dve, "xmz1")
            dve_units(dve, ch, XM0, XM_H, attention_evac(as3(xm["y"], TT), XM0, P, as3(xm["z"], TT)))
            dve_turn(dve, "ym")
            dve_step(dve, "swq0")
            dve_step(dve, "swq1")
            dve_step(dve, "swkv")
            b = read_bank(dve, "swkv")
            for kv in range(SW_KV):
                for half in range(2):
                    nc.vector.tensor_copy(sw["k"][64 * half:64 * half + 64, S * kv:S * kv + S],
                                          b[64 * kv:64 * kv + 64, 0:S])
            bank_read("swkv", nc.vector.tensor_copy(sw["v"], b[:, S:2 * S]))
            dve_step(dve, "swz0")
            dve_step(dve, "swz1")
            wait_bank(dve, "swz0")
            wait_bank(dve, "swz1")
            dve.wait_ge(dn_setup, 1)
            dve_units(dve, ch, SW0, SW_H, attention_evac(as3(sw["y"], TT), SW0, SW_D, as3(sw["z"], TT)), sinks=True)
            dve_turn(dve, "yc")
            for name in ("gmu0", "gmu1", "gmz0", "gmz1", "gmv0", "gmv1"):
                dve_step(dve, name)
            for name in ("gmu0", "gmu1", "gmz0", "gmz1"):
                wait_bank(dve, name)
            dve.wait_ge(gm_wturned, 1)
            for g in range(4):
                last = nc.vector.tensor_tensor(pair(gm["wt"], g), pair(ps[0], g), upto, ALU.mult)
            last.then_inc(gm_wmask, 1)
            ch.link(nc.vector.tensor_tensor(gm["u"], gm["u"], gm["z"], ALU.mult))
            dve.wait_ge(gm_root, 1)
            for t in range(TT):
                c = slice(512 * t, 512 * t + 512)
                nc.vector.scalar_tensor_tensor(out=gm["v"][:, c], in0=gm["v"][:, c], scalar=gm_rs[:, t:t + 1],
                                               in1=rowof("gmn", 512), op0=ALU.mult, op1=ALU.mult)\
                    .then_inc(gm_vn, 1)
            dve.wait_ge(gm_mixed, 1)
            bs = r3(rowof("bs", 512), 4)
            for b in range(2):
                for t in range(TT):
                    src = ps[1 + b].rearrange("p (g t c) -> p g t c", g=2, t=TT)[:, :, t, :]
                    dst = gm["sq"].rearrange("p (g t c) -> p g t c", g=4, t=TT)[:, 2 * b:2 * b + 2, t, :]
                    ch.mark(nc.vector.tensor_tensor(dst, src, bs[:, 2 * b:2 * b + 2, :], ALU.add))
            ch.join()
            nc.vector.tensor_tensor(gm["sq"], gm["sq"], gm["u"], ALU.mult).then_inc(gm_y, 1)
            dve.wait_ge(gm_high, 1)
            nc.vector.tensor_tensor(ytl[:, 1], r3(gm["sq"], 4), yth[:, 1].bitcast(F32), ALU.subtract)\
                .then_inc(gm_low, 1)
            dve_step(dve, "ba")
            bank_read("ba", nc.vector.tensor_copy(d_ba, read_bank(dve, "ba")[:, 0:16]))
            wait_bank(dve, "ba")
            ch.link(nc.vector.tensor_tensor(r3(d_z, TT), r3(d_ba, TT)[:, :, DN_H:2 * DN_H],
                                            r3(rowof("dtb", PAIRS), TT), ALU.add))
            nc.vector.scalar_tensor_tensor(out=d_az, in0=d_z, scalar=-1.0, in1=d_z, op0=ALU.mult, op1=ALU.max)\
                .then_inc(dn_absz, 1)
            for j in range(6):
                name = f"dn{j}"
                dve_step(dve, name)
                wait_bank(dve, name)
                for tap in range(4):
                    for c in (2 * j, 2 * j + 1):
                        w = vcol("conv", 12 * tap + c)
                        if tap == 0:
                            ins = nc.vector.tensor_scalar(cact[:, c, :], cin[:, c, 0:S], w, None, ALU.mult)
                        else:
                            ins = nc.vector.scalar_tensor_tensor(out=cact[:, c, :], in0=cin[:, c, tap:tap + S],
                                                                 scalar=w, in1=cact[:, c, :], op0=ALU.mult,
                                                                 op1=ALU.add)
                        if tap == 3 and c % 2:
                            ins.then_inc(dn_conv, 1)
                        else:
                            ch.mark(ins)
                    if tap < 3:
                        ch.join()
            dve_step(dve, "dnz0")
            dve_step(dve, "dnz1")
            for j in range(6):
                dve.wait_ge(dn_turn, j + 1)
                nc.vector.tensor_copy(tok[:, :, 2 * j:2 * j + 2, :],
                                      ps[j % 4].rearrange("p (t c d) -> p t c d", t=TT, c=2)).then_inc(dn_tok, 1)
            dve.wait_ge(dn_exps, 3)
            ch.link(nc.vector.scalar_tensor_tensor(out=d_sp, in0=d_z, scalar=0.0, in1=d_l, op0=ALU.max,
                                                   op1=ALU.add))
            ch.link(nc.vector.scalar_tensor_tensor(out=d_g, in0=d_sp, scalar=-1.0, in1=d_ea, op0=ALU.mult,
                                                   op1=ALU.mult))
            nc.vector.tensor_copy(r3(d_Lm, PAIRS), bc(d_g, P)).then_inc(dn_g, 1)
            dve.wait_ge(dn_tok, 6)
            sqb = dn["cin"][:, 0:2048].rearrange("p (t c d) -> p t c d", t=TT, c=2 * DN_H)
            for t in range(TT):
                ch.mark(nc.vector.tensor_tensor(sqb[:, t], tok[:, t, 0:8, :], tok[:, t, 0:8, :], ALU.mult))
            ch.join()
            nc.vector.tensor_reduce(d_ss, dn["cin"][:, 0:2048].rearrange("p (c d) -> p c d", d=P), AX.X, ALU.add)\
                .then_inc(dn_sum, 1)
            dve.wait_ge(dn_gcs, 1)
            ch.link(nc.vector.tensor_copy(d_gc, ps[4][:, 0:16]))
            nc.vector.tensor_tensor(d_dm, d_gc[:, 8:16], d_gc[:, 0:8], ALU.subtract).then_inc(dn_gcd, 1)
            for n in range(PAIRS):
                nc.vector.scalar_tensor_tensor(out=pair(d_E, n), in0=pair(ps[1 + n // 4], n % 4),
                                               scalar=d_gc[:, n:n + 1], in1=upto, op0=ALU.subtract, op1=ALU.mult)\
                    .then_inc(dn_diff, 1)
            dve.wait_ge(dn_root, 1)
            rs = r3(d_rs, TT)
            ch.link(nc.vector.tensor_scalar(rs[:, :, 0:DN_H], rs[:, :, 0:DN_H], float(P) ** -0.5, None, ALU.mult))
            for t in range(TT):
                ch.mark(nc.vector.tensor_tensor(tok[:, t, 0:8, :], tok[:, t, 0:8, :], bc(d_rs[:, 8 * t:8 * t + 8], P),
                                                ALU.mult))
            for t in range(TT):
                ch.mark(nc.vector.tensor_tensor(tok[:, t, 8:12, :], tok[:, t, 8:12, :],
                                                bc(d_beta[:, 4 * t:4 * t + 4], P), ALU.mult))
            ch.join()
            kb = heads(dn["kb"])
            for t in range(TT):
                ch.mark(nc.vector.tensor_tensor(kb[:, t], tok[:, t, 4:8, :], bc(d_beta[:, 4 * t:4 * t + 4], P),
                                                ALU.mult))
            ch.join()
            dve.wait_ge(dn_egs, 2)
            nc.vector.tensor_tensor(r3(dn["rw"], 4), kb[:, 1], bc(d_egc[:, 4:8], P), ALU.mult)
            nc.vector.tensor_tensor(r3(dn["kd"], 4), tok[:, 0, 4:8, :], bc(d_ekd[:, 0:4], P), ALU.mult)
            nc.vector.tensor_tensor(r3(d_qg, 4), tok[:, 1, 0:4, :], bc(d_egc[:, 4:8], P), ALU.mult)\
                .then_inc(dn_ready, 1)
            dve.wait_ge(dn_ed, 1)
            ch.link(nc.vector.tensor_tensor(r3(d_E, PAIRS), r3(d_E, PAIRS), rep(upto, PAIRS), ALU.mult))
            ch.mark(nc.vector.tensor_tensor(r3(d_Es, PAIRS), r3(d_E, PAIRS), rep(before, PAIRS), ALU.mult))
            for n, (_, dst, b) in enumerate(DN_TURNS):
                if n % 2:
                    dve.wait_ge(dn_fm, n + 1)
                    nc.vector.tensor_copy(dst, ps[b][:, :]).then_inc(dn_fd, 1)
            dve.wait_ge(dn_kk, 2)
            ch.join()
            for b in range(2):
                c = slice(512 * b, 512 * b + 512)
                ch.mark(nc.vector.tensor_tensor(d_L[:, c], ps[1 + b][:, :], d_Es[:, c], ALU.mult))
            for b in range(2):
                c = slice(512 * b, 512 * b + 512)
                nc.vector.tensor_tensor(d_A[:, c], ps[(3, 6)[b]][:, :], d_E[:, c], ALU.mult).then_inc(dn_la, 1)
            ch.mark(nc.vector.tensor_copy(r3(d_T, PAIRS), rep(ident, PAIRS)))
            ch.mark(nc.vector.tensor_copy(r3(d_TT, PAIRS), rep(ident, PAIRS)))
            ch.join()
            dve.wait_ge(dn_level, 16)
            for l in range(LEVELS):
                nc.vector.tensor_tensor(r3(d_Lm, PAIRS), r3(d_L, PAIRS), rep(d_level[:, l, :], PAIRS), ALU.mult)\
                    .then_inc(dn_lm, 1)
                dve.wait_ge(dn_y, l + 1)
                for n in range(4):
                    m = (d_T, d_TT)[n // 2][:, 512 * (n % 2):512 * (n % 2) + 512]
                    ins = nc.vector.tensor_tensor(m, m, ps[(2, 3, 6, 7)[n]][:, :], ALU.subtract)
                ins.then_inc(dn_t, 1)
                dve.wait_ge(dn_t, l + 1)
            dve.wait_ge(dn_u, 1)
            for b in range(2):
                nc.vector.tensor_copy(d_u[:, 512 * b:512 * b + 512], ps[b][:, :]).then_inc(dn_uc, 1)
            dve.wait_ge(dn_ws, 1)
            dve.wait_ge(dn_uc, 2)
            nc.vector.tensor_tensor(d_vn, d_u[:, 512:1024], ps[7][:, :], ALU.subtract).then_inc(dn_vnd, 1)
            o = dn["kt"]
            ch.mark(nc.vector.tensor_copy(o[:, 0:512], ps[3][:, :]))
            dve.wait_ge(dn_o1, 1)
            ch.mark(nc.vector.tensor_copy(o[:, 512:1024], ps[0][:, :]))
            ch.join()
            ch.link(nc.vector.tensor_tensor(d_P, o, o, ALU.mult))
            nc.vector.tensor_reduce(d_os, r3(d_P, PAIRS), AX.X, ALU.add).then_inc(dn_osum, 1)
            dve.wait_ge(dn_oroot, 1)
            ch.link(nc.vector.tensor_tensor(r3(o, PAIRS), r3(o, PAIRS), bc(d_or, P), ALU.mult))
            ch.link(nc.vector.tensor_tensor(r3(o, PAIRS), r3(o, PAIRS), rep(rowof("onorm", P), PAIRS), ALU.mult))
            wait_bank(dve, "dnz0")
            wait_bank(dve, "dnz1")
            nc.vector.tensor_tensor(o, o, d_sz, ALU.mult).then_inc(dn_out, 1)
            dve_turn(dve, "ya")
            dve_merge_branch(dve, 0)
            with dve.Fori(0, NBR - 1) as i:
                dve_merge_branch(dve, 1, i)
            for b in range(2):
                dve.wait_ge(mg_high, b + 1)
                nc.vector.tensor_tensor(ntl[:, 4 * b:4 * b + 4, :], r3(mg["m"][:, 1024 * b:1024 * b + 1024], 4),
                                        nth[:, 4 * b:4 * b + 4, :].bitcast(F32), ALU.subtract).then_inc(mg_low, 1)
            for j in range(4):
                dve_step(dve, f"out{j}")
            dve_norm(dve, "post")
            dve.wait_ge(mg_post, 16)
            dve.wait_ge(norm_scaled, TT * (NORMS.index("post") + 1))
            for t in range(TT):
                ch.mark(nc.vector.tensor_tensor(xs[:, t, :], xs[:, t, :], mg["post"], ALU.mult))
            ch.join()
            nc.vector.tensor_tensor(x[:, :, :], x[:, :, :], xs[:, :, :], ALU.add).then_inc(x_ready, 1)
            dve_norm(dve, "f0")
            dve_turn(dve, "f0")
            dve_ffn(dve, 0)
            dve_norm(dve, "mx0")
            dve_turn(dve, "mx0")
            def rotate(bank, n, dst):
                cs = rep(cos_[64:96], n) if n > 1 else cos_[64:96]
                sn = rep(sin_[64:96], n) if n > 1 else sin_[64:96]
                a, b = (mrot[64:96, r, 0:n, :] if n > 1 else mrot[64:96, r, 0, :] for r in range(2))
                up, dn_ = bank[64:96, :], bank[96:128, :]
                if n > 1:
                    up, dn_ = r3(up, n), r3(dn_, n)
                ch.mark(nc.vector.tensor_tensor(a, up, cs, ALU.mult))
                ch.link(nc.vector.tensor_tensor(b, dn_, sn, ALU.mult))
                return nc.vector.tensor_tensor(dst, a, b, ALU.add)

            dve_step(dve, "mlain0")
            dve_step(dve, "mlain1")
            dve_step(dve, "mlain2")
            bank = read_bank(dve, "mlain2")
            ch.link(rotate(bank[:, S:2 * S], 1, mlc["kr"][64:96, 0:S]))
            bank_read("mlain2", nc.vector.tensor_copy(mc[:, :, 2 * CW:2 * CW + P], r3(bank[:, 0:S], TT)))
            nc.vector.tensor_copy(mk_[64:96, :, :], rep(mlc["kr"][64:96, 0:S], MLA_H)).then_inc(ml_krd, 1)
            dve.wait_ge(ml_rs, 1)
            for n, (t, c) in enumerate(MLC):
                nc.vector.tensor_scalar(mc[:, t, c], mc[:, t, c], m_rs[:, n:n + 1], None, ALU.mult).then_inc(ml_cs, 1)
            dve_turn(dve, "mlc")
            for j in range(4):
                dve_step(dve, f"uq{j}")
                for b in range(2):
                    dve.wait_ge(ml_q, 2 * j + b + 1)
                    if j + b:
                        dve.wait_ge(ml_qd, 2 * j + b)
                    h = 4 * j + 2 * b
                    rotate(ps[2 * (j % 2) + b], 2, mq[64:96, h:h + 2, :]).then_inc(ml_qd, 1)
            dve_step(dve, "uk")
            dve.wait_ge(ml_k, 1)
            for b in range(4):
                nc.vector.tensor_copy(mk_[0:64, 4 * b + 1:4 * b + 4:2, :], r3(ps[b][64:128, :], 2)).then_inc(ml_kd, 1)
            dve_step(dve, "uv")
            dve_units(dve, ch, MLA0, MLA_H, attention_evac(as3(ml["y"], TT), MLA0, MLA_V))
            dve_turn(dve, "mly")

            def add_to_x(names, stage):
                for j, name in enumerate(names):
                    dve_step(dve, name)
                    xo = x[:, :, CW * j:CW * j + CW]
                    bank_read(name, nc.vector.tensor_tensor(xo, xo, r3(read_bank(dve, name), TT), ALU.add))
                wait_bank(dve, names[-2])
                wait_bank(dve, names[-1])
                nc.vector.tensor_copy(mark_col, one_col).then_inc(x_ready, 1)

            add_to_x([f"mlao{j}" for j in range(4)], "mla")
            dve_norm(dve, "f1")
            dve_turn(dve, "f1")
            dve_ffn(dve, 1)
            dve_norm(dve, "f2")
            dve_turn(dve, "f2")
            dve_ffn(dve, 2)
            dve_norm(dve, "mx1")
            dve_turn(dve, "mx1")
            dve.wait_ge(ns_cb, 1)
            nc.vector.tensor_copy(ns["cbias"], ps[7][:, :]).then_inc(ns_cbc, 1)
            for j in range(4):
                dve_step(dve, f"nq{j}")
            for m, name in enumerate(("nkc", "nvc")):
                dve_step(dve, name)
                src = r3(read_bank(dve, name), 2)
                dst = xx[m].rearrange("p (c two) s -> p two c s", two=2)
                for g in range(2):
                    nc.vector.tensor_copy(dst[0:64, g], src[64 * g:64 * g + 64])
                    ins = nc.vector.tensor_copy(dst[64:128, g, :, 0:S - 1], src[64 * g:64 * g + 64, :, 1:S])
                bank_read(name, ins)
            for name, dst in (("nks", ns["ks"]), ("nvs", None), ("nkw", ns["kw"]), ("nvw", None), ("ng", None)):
                dve_step(dve, name)
                if dst is not None:
                    for o_, i_ in doubled(dst, read_bank(dve, name), NSA_G):
                        ins = nc.vector.tensor_copy(o_, i_)
                    bank_read(name, ins)
            dve.wait_ge(ns_hid, 1)
            nc.vector.tensor_copy(n_pos, ps[0][:, 0:2]).then_inc(ns_pos, 1)
            dve.wait_ge(ns_kc, 1)
            nc.vector.tensor_copy(n_kc[0:64], ps[2][0:64, 0:NSA_G * NCMP])
            nc.vector.tensor_copy(n_kc[64:128], ps[2][0:64, 0:NSA_G * NCMP]).then_inc(ns_kcd, 1)
            dve.wait_ge(ns_vc, 1)
            dve.wait_ge(ns_zero, 1)
            for r in range(NSA_R):
                ins = nc.vector.tensor_copy(vcd[32 * r:32 * r + NCMP, :, 64 * r:64 * r + 64],
                                            r3(ps[3][32 * r:32 * r + NCMP, 0:NSA_G * 64], NSA_G))
            ins.then_inc(ns_vcd, 1)
            dve.wait_ge(ns_cs, 1)
            dve.wait_ge(ns_cbc, 1)
            dve.wait_ge(ns_zero, 2)
            cb = ns["cbias"][:, 0:TT * 256].rearrange("p (t n h) -> p t h n", t=TT, n=16)
            for t in range(TT):
                c = slice(NSA_H * t, NSA_H * t + NSA_H)
                st = sc[:, t, :, 0:NCMP]
                for odd in range(2):
                    got = ps[7 - odd][:, 0:256].rearrange("p (t h n) -> p t h n", t=TT, h=NSA_H // 2)
                    ch.mark(nc.vector.scalar_tensor_tensor(
                        out=sc[:, t, odd::2, 0:NCMP], in0=got[:, t, :, 0:NCMP], scalar=NSA_D ** -0.5,
                        in1=cb[:, t, odd::2, 0:NCMP], op0=ALU.mult, op1=ALU.add))
                ch.join()
                ch.link(nc.vector.tensor_reduce(n_mx[:, c], st, AX.X, ALU.max))
                nc.vector.tensor_tensor(st, st, bc(n_mx[:, c], NCMP), ALU.subtract).then_inc(ns_cm, 1)
            wait_bank(dve, "ng")
            for t in range(TT):
                c = slice(NSA_H * t, NSA_H * t + NSA_H)
                dve.wait_ge(ns_ce, t + 1)
                ch.link(nc.vector.tensor_reduce(n_sum[:, c], sc[:, t, :, 0:NCMP], AX.X, ALU.add))
                ch.link(nc.vector.reciprocal(n_inv[:, c], n_sum[:, c]))
                ok = con[:, CON["rowok"] + t:CON["rowok"] + t + 1]
                ch.link(nc.vector.scalar_tensor_tensor(out=n_cg[:, c], in0=n_inv[:, c], scalar=ok,
                                                       in1=gate3[:, t, :, 0], op0=ALU.mult, op1=ALU.mult))
            for b in range(2):
                dve.wait_ge(ns_ct, b + 1)
                nc.vector.tensor_copy(sct[:, 512 * b:512 * b + 512], ps[b][:, :]).then_inc(ns_ctc, 1)
            for t in range(TT):
                for half in range(2):
                    n = 2 * t + half
                    dve.wait_ge(ns_co, n + 1)
                    h0 = 8 * half
                    nc.vector.tensor_tensor(
                        ny[:, t, 512 * half:512 * half + 512].rearrange("p (h d) -> p h d", h=8),
                        r3(ps[(2, 3, 6, 7)[n]], 8), bc(n_cg[:, NSA_H * t + h0:NSA_H * t + h0 + 8], 64), ALU.mult)\
                        .then_inc(ns_cy, 1)
            dve.wait_ge(ns_cy, 4)
            dve.wait_ge(ns_bias, 16)

            def nsa_evac(a, o, inv):
                h, branch = (a - NSA0) % NSA_H, 1 + (a - NSA0) // NSA_H
                ch.link(nc.vector.tensor_tensor(n_ag[a % 2], inv, gate3[:, :, h, branch], ALU.mult))
                if a - NSA0 >= NSA_H:
                    dve.wait_ge(at_read, a - NSA_H + 1)
                for t in range(TT):
                    yo = ny[:, t, 64 * h:64 * h + 64]
                    last = nc.vector.scalar_tensor_tensor(out=yo, in0=o[:, 64 * t:64 * t + 64],
                                                          scalar=n_ag[a % 2][:, t:t + 1], in1=yo, op0=ALU.mult,
                                                          op1=ALU.add)
                return last

            dve_units(dve, ch, NSA0, 2 * NSA_H, nsa_evac)
            dve_turn(dve, "nsy")
            add_to_x([f"nsao{j}" for j in range(4)], "nsa")
            dve_norm(dve, "f3")
            dve_turn(dve, "f3")
            dve_ffn(dve, 3)
            dve_norm(dve, "final")
            dve.wait_ge(mg_post, 32)
            dve.wait_ge(norm_scaled, TT * (NORMS.index("final") + 1))
            for t in range(TT):
                nc.vector.tensor_tensor(x[:, t, :], xs[:, t, :], scr[:, 4096:4096 + D], ALU.mult)\
                    .then_inc(mg_posted, 1)

        @block.tensor
        def _(pe):
            pe.wait_ge(inputs_here, 80)
            pe_norm(pe, "mem")
            pe.wait_ge(turn_low, turn_done("mem"))
            pe_plain(pe, "mk0", "F")
            pe_plain(pe, "mk1", "F")
            pe_plain(pe, "mv0", "T")
            pe_plain(pe, "mv1", "T")
            pe_norm(pe, "pre")
            pe.wait_ge(turn_low, turn_done("pre"))
            for name, kind in (("xmq0", "F"), ("xmq1", "F"), ("xmz0", "T"), ("xmz1", "T")):
                pe_plain(pe, name, kind)
            for name in ("mk0", "mk1", "mv0", "mv1", "xmq0", "xmq1"):
                wait_bank(pe, name)
            pe_units(pe, XM0, XM_H)
            pe.wait_ge(at_read, XM0 + XM_H)
            pe_turn(pe, "ym")
            for name, kind in (("swq0", "F"), ("swq1", "F"), ("swkv", "FT"), ("swz0", "T"), ("swz1", "T")):
                pe_plain(pe, name, kind)
            for name in ("swq0", "swq1", "swkv"):
                wait_bank(pe, name)
            pe.wait_ge(turn_low, turn_done("ym"))
            pe_units(pe, SW0, SW_H)
            pe.wait_ge(at_read, SW0 + SW_H)
            pe_turn(pe, "yc")
            for name, kind in (("gmu0", "F"), ("gmu1", "F"), ("gmz0", "F"), ("gmz1", "F"), ("gmv0", "T"),
                               ("gmv1", "T")):
                pe_plain(pe, name, kind)
            pe.wait_ge(gm_loaded, 16)
            pe.wait_ge(turn_low, turn_done("yc"))
            for g in range(4):
                last = nc.tensor.transpose(pair(ps[0], g), pair(gm["w"], g), ident)
            last.then_inc(gm_wturned, 1)
            pe.wait_ge(gm_wmask, 1)
            pe.wait_ge(gm_vn, TT)
            for g in range(4):
                for t in range(TT):
                    at = 256 * (g % 2) + P * t
                    last = nc.tensor.matmul(ps[1 + g // 2][:, at:at + P], gm["v"][:, 512 * t + P * g:512 * t + P * g + P],
                                            pair(gm["wt"], g), start=True, stop=True)
            last.then_inc(gm_mixed, 1)
            pe_plain(pe, "ba", 8)
            for j in range(6):
                pe_plain(pe, f"dn{j}", "F")
            pe_plain(pe, "dnz0", "T")
            pe_plain(pe, "dnz1", "T")
            pe.wait_ge(gm_low, 1)
            for j in range(6):
                pe.wait_ge(dn_act, j + 1)
                if j >= 4:
                    pe.wait_ge(dn_tok, j - 3)
                for t in range(TT):
                    for c in range(2):
                        at = 256 * t + P * c
                        last = nc.tensor.transpose(ps[j % 4][:, at:at + P], cact[:, 2 * j + c, P * t:P * t + P], ident)
                last.then_inc(dn_turn, 1)
            pe.wait_ge(dn_g, 1)
            wait_bank(pe, "dnz0")
            wait_bank(pe, "dnz1")
            pe.wait_ge(dn_tok, 6)
            nc.tensor.matmul(ps[4][:, 0:8], upto, d_g, start=True, stop=True)
            nc.tensor.matmul(ps[4][:, 8:16], ones, d_g, start=True, stop=True)
            for n in range(PAIRS):
                last = nc.tensor.matmul(pair(ps[1 + n // 4], n % 4), pair(d_Lm, n), upto, start=True, stop=True)
            last.then_inc(dn_gcs, 1)
            pe.wait_ge(dn_ready, 1)
            for n, (src, _, b) in enumerate(DN_TURNS):
                if n == 1:
                    pe.wait_ge(dn_diff, PAIRS)
                if n == 6:
                    pe.wait_ge(dn_fa, 1)
                for h in range(DN_H):
                    last = nc.tensor.transpose(pair(ps[b], h), src[h], ident)
                last.then_inc(dn_fm, 1)
            pe.wait_ge(dn_fa, 4)
            pe.wait_ge(dn_fd, 3)
            for rhs, banks in ((d_kbt, (1, 2)), (dn["qt"], (3, 6))):
                for n in range(PAIRS):
                    last = nc.tensor.matmul(pair(ps[banks[n // 4]], n % 4), pair(dn["kt"], n), pair(rhs, n),
                                            start=True, stop=True)
                last.then_inc(dn_kk, 1)
            pe.wait_ge(dn_la, 2)
            for l in range(LEVELS):
                pe.wait_ge(dn_lm, l + 1)
                if l:
                    pe.wait_ge(dn_t, l)
                for n in range(PAIRS):
                    last = nc.tensor.matmul(pair(ps[n // 4], n % 4), pair(d_Lm, n), pair(d_T, n), start=True,
                                            stop=True)
                last.then_inc(dn_p, 1)
                pe.wait_ge(dn_pc, l + 1)
                for n in range(PAIRS):
                    nc.tensor.matmul(pair(ps[2 + n // 4], n % 4), pair(d_TT, n), pair(d_P, n), start=True, stop=True)
                for n in range(PAIRS):
                    last = nc.tensor.matmul(pair(ps[6 + n // 4], n % 4), pair(d_P, n), pair(d_TT, n), start=True,
                                            stop=True)
                last.then_inc(dn_y, 1)
            pe.wait_ge(dn_t, LEVELS)
            for n in range(PAIRS):
                last = nc.tensor.matmul(pair(ps[n // 4], n % 4), pair(d_TT, n), tok[:, n // 4, 8 + n % 4, :],
                                        start=True, stop=True)
            last.then_inc(dn_u, 1)
            for h in range(DN_H):
                last = nc.tensor.matmul(pair(ps[2], h), pair(dn["rw"], h), pair(d_TT, 4 + h), start=True, stop=True)
            last.then_inc(dn_u, 1)
            pe.wait_ge(dn_uc, 1)
            for h in range(DN_H):
                last = nc.tensor.matmul(pair(ps[3], h), pair(d_A, h), pair(d_u, h), start=True, stop=True)
            last.then_inc(dn_o0, 1)
            for h in range(DN_H):
                last = nc.tensor.matmul(pair(ps[6], h), pair(dn["kd"], h), pair(d_u, h), start=True, stop=True)
            last.then_inc(dn_o0, 1)
            pe.wait_ge(dn_sc, 1)
            pe.wait_ge(dn_wc, 1)
            for h in range(DN_H):
                last = nc.tensor.matmul(pair(ps[7], h), pair(d_wt, h), pair(d_S, h), start=True, stop=True)
            last.then_inc(dn_ws, 1)
            pe.wait_ge(dn_vnd, 1)
            for h in range(DN_H):
                nc.tensor.matmul(pair(ps[0], h), pair(dn["qgt"], h), pair(d_S, h), start=True, stop=False,
                                 skip_group_check=True)
                last = nc.tensor.matmul(pair(ps[0], h), pair(d_A, 4 + h), pair(d_vn, h), start=False, stop=True,
                                        skip_group_check=True)
            last.then_inc(dn_o1, 1)
            pe.wait_ge(dn_out, 1)
            pe_turn(pe, "ya")
            pe.wait_ge(turn_low, turn_done("ya"))
            pe_merge_branch(pe, 0)
            with pe.Fori(0, NBR - 1) as i:
                pe_merge_branch(pe, 1, i)
            pe.wait_ge(mg_low, 2)
            pe.wait_ge(mg_sig, 4 * NBR)
            for j in range(4):
                pe_plain(pe, f"out{j}", "T")
            pe_norm(pe, "f0")
            pe.wait_ge(turn_low, turn_done("f0"))
            pe_ffn(pe, 0)
            pe_norm(pe, "mx0")
            pe.wait_ge(turn_low, turn_done("mx0"))
            pe_plain(pe, "mlain0", "T")
            pe_plain(pe, "mlain1", "T")
            pe_plain(pe, "mlain2", "TF")
            pe.wait_ge(ml_cs, 4)
            pe_turn(pe, "mlc")
            pe.wait_ge(turn_low, turn_done("mlc"))
            for j in range(4):
                t = TILE[f"uq{j}"]
                weights_here(pe, t)
                for b in range(2):
                    if j >= 2:
                        pe.wait_ge(ml_qa, 2 * (j - 2) + b + 1)
                        pe.wait_ge(ml_qd, 2 * (j - 2) + b + 1)
                    for c in range(2):
                        last = by_feature(ps[2 * (j % 2) + b][:, S * c:S * c + S], slot(t, 3, 512), P * (2 * b + c),
                                          NT_, 3)
                    last.then_inc(ml_q, 1)
                nc.tensor.matmul(ps[6][:, 0:2], ident, power[:, 0:2], start=True, stop=True).then_inc(w_used, 1)
            t = TILE["uk"]
            weights_here(pe, t)
            pe.wait_ge(ml_qa, 8)
            pe.wait_ge(ml_qd, 8)
            for c in range(8):
                last = by_feature(ps[c // 2][:, S * (c % 2):S * (c % 2) + S], slot(t, 2, D), P * c, NT_, 2, 3)
            last.then_inc(ml_k, 1)
            nc.tensor.matmul(ps[6][:, 0:2], ident, power[:, 0:2], start=True, stop=True).then_inc(w_used, 1)
            t = TILE["uv"]
            weights_here(pe, t)
            for n in range(4):
                last = by_token(ps[4 + n][:, :], slot(t, 2, D), 512 * (n % 2), 512, NT_, 2, n // 2, 3)
            last.then_inc(ml_v, 1)
            pe.wait_ge(ml_va, 4)
            nc.tensor.matmul(ps[6][:, 0:2], ident, power[:, 0:2], start=True, stop=True).then_inc(w_used, 1)
            pe.wait_ge(ml_ka, 4)
            pe.wait_ge(ml_kd, 4)
            pe.wait_ge(ml_krd, 1)
            pe_units(pe, MLA0, MLA_H)
            pe.wait_ge(at_read, MLA0 + MLA_H)
            pe_turn(pe, "mly")
            pe.wait_ge(turn_low, turn_done("mly"))
            for j in range(4):
                pe_plain(pe, f"mlao{j}", "T")
            pe_norm(pe, "f1")
            pe.wait_ge(turn_low, turn_done("f1"))
            pe_ffn(pe, 1)
            pe_norm(pe, "f2")
            pe.wait_ge(turn_low, turn_done("f2"))
            pe_ffn(pe, 2)
            pe_norm(pe, "mx1")
            pe.wait_ge(turn_low, turn_done("mx1"))
            pe.wait_ge(ns_tbl, 32)
            pe.wait_ge(ns_w1, 48)
            tbl = nt_["tbl"][0:BIAS_ROWS, 0:NSA_H]
            nc.tensor.matmul(ps[6][0:NSA_H, :], tbl, nt_["hot"][0:BIAS_ROWS, :], start=True, stop=True)\
                .then_inc(ns_line, 1)
            for t in range(TT):
                for n in range(16):
                    at = S + P * t - CMP_ST * min(n, NCMP - 1) - (CMP_L - 1)
                    last = nc.tensor.matmul(ps[7][:, 256 * t + 16 * n:256 * t + 16 * n + 16],
                                            nt_["hot"][0:BIAS_ROWS, at:at + P], tbl, start=True, stop=True)
            last.then_inc(ns_cb, 1)
            for name, kind in ([(f"nq{j}", "F") for j in range(4)] +
                               [("nkc", "F"), ("nvc", "F"), ("nks", "F"), ("nvs", "T"), ("nkw", "F"), ("nvw", "T"),
                                ("ng", 48)]):
                pe_plain(pe, name, kind)
            wait_bank(pe, "nkc")
            wait_bank(pe, "nvc")
            for m in range(2):
                for j in range(CMP_L // 2):
                    nc.tensor.matmul(ps[0][:, m:m + 1], w1s[:, m, j, :], poss[:, m, j:j + 1], start=j == 0,
                                     stop=j == CMP_L // 2 - 1)
            for m in range(2):
                for j in range(CMP_L // 2):
                    blocks = xx[m][:, :, 2 * j:2 * j + CMP_ST * (NCMP - 1) + 1:CMP_ST]
                    last = nc.tensor.matmul(ps[1][:, 64 * m:64 * m + NSA_G * NCMP], w1s[:, m, j, :], blocks,
                                            start=j == 0, stop=j == CMP_L // 2 - 1)
            last.then_inc(ns_hid, 1)
            pe.wait_ge(ns_hc, 2)
            nc.tensor.matmul(ps[2][0:64, 0:NSA_G * NCMP], w2s[:, 0, :], n_hid[0][:, 0:NSA_G * NCMP], start=True,
                             stop=True).then_inc(ns_kc, 1)
            for r in range(NSA_R):
                for g in range(NSA_G):
                    last = nc.tensor.matmul(ps[3][32 * r:32 * r + NCMP, 64 * g:64 * g + 64],
                                            n_hid[1][:, NCMP * g:NCMP * g + NCMP], w2s[:, 1, :], start=True, stop=True)
            last.then_inc(ns_vc, 1)
            pe.wait_ge(ns_kcd, 1)
            pe.wait_ge(ns_cbc, 1)
            pe.wait_ge(ns_linec, 1)
            for name in ("nq2", "nq3"):
                wait_bank(pe, name)
            for t in range(TT):
                for h in range(NSA_H):
                    p0, g = 64 * (h % 2), h // NSA_R
                    at = P * t + 16 * (h // 2)
                    last = nc.tensor.matmul(ps[7 - h % 2][:, at:at + NCMP],
                                            ns["q"][p0:p0 + 64, S * (h // 2) + P * t:S * (h // 2) + P * t + P],
                                            n_kc[p0:p0 + 64, NCMP * g:NCMP * g + NCMP], start=True, stop=True)
            last.then_inc(ns_cs, 1)
            for t in range(TT):
                pe.wait_ge(ns_ce, t + 1)
                if t == 0:
                    pe.wait_ge(ns_pos, 1)
                for g in range(NSA_G):
                    last = nc.tensor.transpose(pair(ps[t], g), xs[:, 0, 512 * t + P * g:512 * t + P * g + P], ident)
                last.then_inc(ns_ct, 1)
            pe.wait_ge(ns_vcd, 1)
            pe.wait_ge(ns_cm, 2)
            for t in range(TT):
                pe.wait_ge(ns_ctc, t + 1)
                for half in range(2):
                    for gg in range(2):
                        g = 2 * half + gg
                        last = nc.tensor.matmul(ps[(2, 3, 6, 7)[2 * t + half]][:, 256 * gg:256 * gg + 256],
                                                sct[:, 512 * t + P * g:512 * t + P * g + P], vcd[:, g, :], start=True,
                                                stop=True)
                    last.then_inc(ns_co, 1)
            for name in ("nks", "nvs", "nkw", "nvw"):
                wait_bank(pe, name)
            pe.wait_ge(ns_cy, 4)
            pe_units(pe, NSA0, 2 * NSA_H)
            pe.wait_ge(at_read, NSA0 + 2 * NSA_H)
            pe_turn(pe, "nsy")
            pe.wait_ge(turn_low, turn_done("nsy"))
            for j in range(4):
                pe_plain(pe, f"nsao{j}", "T")
            pe_norm(pe, "f3")
            pe.wait_ge(turn_low, turn_done("f3"))
            pe_ffn(pe, 3)


def kernel(**inputs):
    import concourse.bacc as bacc
    from concourse.bass_utils import run_bass_kernel_spmd as run

    arrays = lay_out({k: np.asarray(v) for k, v in inputs.items()})
    nc = bacc.Bacc("TRN2", target_bir_lowering=False, num_devices=1)
    A = {k: nc.dram_tensor(f"in_{k}", v.shape, F32, kind="ExternalInput").ap() for k, v in arrays.items()}
    out = nc.dram_tensor("out", (P, TT, D), F32, kind="ExternalOutput").ap()
    build(nc, A, out)
    r = run(nc, [{f"in_{k}": v for k, v in arrays.items()}], core_ids=[0])
    y = r.results[0]["out"]
    return np.ascontiguousarray(np.asarray(y).transpose(1, 0, 2)).reshape(1, S, D)
```

```python
import numpy as np
from contextlib import ExitStack

import concourse.bass as bass
from concourse import mybir

F32 = mybir.dt.float32
F32R = mybir.dt.float32r
ALU = mybir.AluOpType
ACT = mybir.ActivationFunctionType
AX = mybir.AxisListType

P = 128
S = 256
TT = S // P
D = 1024
KC = D // P
TW = 2048
CW = TW // KC
SLOTS = 3
EPS = 1e-6
NEG = -1e30
FFN = 2816
FT = FFN // CW
BW = 512
NBR = 4
DN_H = 4
SW_H, SW_KV, SW_D, SW_WIN = 8, 2, 64, 128
XM_H = 4
MLA_H, MLA_QL, MLA_KVL, MLA_N, MLA_R, MLA_V = 16, 384, 256, 64, 32, 64
NSA_H, NSA_G, NSA_D = 16, 4, 64
NSA_R = NSA_H // NSA_G
CMP_L, CMP_ST = 32, 16
NCMP = (S - CMP_L) // CMP_ST + 1
BUCKETS = 32
PAIRS = TT * DN_H


def plan():
    t = ["mk0", "mk1", "mv0", "mv1"]
    t += ["xmq0", "xmq1", "xmz0", "xmz1"]
    t += ["swq0", "swq1", "swkv", "swz0", "swz1"]
    t += ["gmu0", "gmu1", "gmz0", "gmz1", "gmv0", "gmv1"]
    t += ["ba"] + [f"dn{j}" for j in range(6)] + ["dnz0", "dnz1"]
    for n in range(NBR):
        for half in range(2):
            t += [f"gate{n}{half}0", f"gate{n}{half}1", f"up{n}{half}"]
    t += [f"out{j}" for j in range(4)]
    t += ffn_names(0)
    t += ["mlain0", "mlain1", "mlain2"] + [f"uq{j}" for j in range(4)] + ["uk", "uv"]
    t += [f"mlao{j}" for j in range(4)]
    t += ffn_names(1) + ffn_names(2)
    t += ["nkc", "nvc"] + [f"nq{j}" for j in range(4)] + ["nks", "nvs", "nkw", "nvw", "ng"]
    t += [f"nsao{j}" for j in range(4)]
    t += ffn_names(3)
    return t + ["pad"]


def ffn_names(f):
    t = [f"f{f}g0", f"f{f}u0"]
    for i in range(1, FT):
        t += [f"f{f}g{i}", f"f{f}u{i}", f"f{f}d{i - 1}"]
    return t + [f"f{f}d{FT - 1}"]


PLAN = plan()
TILE = {n: i for i, n in enumerate(PLAN)}
NT = len(PLAN)
PLAIN = [n for n in PLAN if n[0] not in "fu" and n[:4] != "gate" and n != "pad"]
UNIT = {n: i for i, n in enumerate(PLAIN)}

VEC = {}
_at = 0
for _n, _w in (("pre", 8), ("mem", 8), ("fa0", 8), ("fa1", 8), ("mx0", 8), ("mx1", 8), ("fb0", 8),
               ("fb1", 8), ("qn", 3), ("kvn", 2), ("conv", 48)):
    VEC[_n] = _at
    _at += _w
NVEC = _at
ROW = {}
_at = 0
for _n, _w in (("onorm", 128), ("gmn", 512), ("bs", 512), ("dtb", 8), ("alog", 8), ("sink", 8)):
    ROW[_n] = _at
    _at += _w
NROW = _at
LEVELS = 7
CON = {}
_at = 0
for _n, _w in (("ident", 128), ("upto", 128), ("before", 128), ("ones", 128), ("causal", 256),
               ("window", 256), ("rowok", 2), ("cos", 256), ("sin", 256)):
    CON[_n] = _at
    _at += _w
NCON = _at


def constants():
    j = np.arange(P)[:, None]
    i = np.arange(P)[None, :]
    con = np.zeros((P, NCON), np.float32)

    def put(name, a):
        con[:, CON[name]:CON[name] + a.shape[1]] = a

    put("ident", (i == j) * 1.0)
    put("upto", (j <= i) * 1.0)
    put("before", (j < i) * 1.0)
    put("ones", np.ones((P, P)))
    dist = P + j - np.arange(2 * P)[None, :]
    put("causal", np.where(dist >= 0, 0.0, NEG))
    put("window", np.where((dist >= 0) & (dist < SW_WIN), 0.0, NEG))
    put("rowok", (j + P * np.arange(TT)[None, :] >= CMP_L - 1) * 1.0)
    half = MLA_R // 2
    inv = np.float32(10000.0) ** (-np.arange(half, dtype=np.float32) * np.float32(2.0) / MLA_R)
    ang = np.arange(S, dtype=np.float32)[None, :] * inv[:, None].astype(np.float32)
    rope = np.zeros((2, P, S), np.float32)
    rope[0, 64:96] = np.tile(np.cos(ang), (2, 1))
    rope[1, 64:80], rope[1, 80:96] = -np.sin(ang), np.sin(ang)
    put("cos", rope[0])
    put("sin", rope[1])
    level = np.zeros((P, LEVELS, P), np.float32)
    for n in range(LEVELS):
        s = 1 << n
        level[:, n] = (j // (2 * s) == i // (2 * s)) & (i % (2 * s) >= s) & (j % (2 * s) < s)
    dist = np.arange(2 * S) - S
    n = np.maximum(dist, 0)
    exact = BUCKETS // 2
    large = exact + (np.log(np.maximum(n, 1).astype(np.float32) / exact) / np.float32(np.log(128 / exact))
                     * (BUCKETS - exact)).astype(np.int32)
    bucket = np.where(n < exact, n, np.minimum(large, BUCKETS - 1))
    hot = np.zeros((BUCKETS + 1, 2 * S), np.float32)
    hot[bucket, np.arange(2 * S)] = 1.0
    hot[BUCKETS] = dist < 0
    return con, level.reshape(P, LEVELS * P), hot


def lay_out(a):
    def cols(w, c0, n=CW):
        k = w.shape[0] // P
        return w[:, c0:c0 + n].reshape(k, P, n).transpose(1, 0, 2).reshape(P, k * n)

    w_in = a["w_in"][0]
    mkv = a["w_mem_kv"][0]
    win_m, wuq, wukv = a["mla_w_in_2"][0], a["mla_w_uq_2"][0], a["mla_w_ukv_2"][0]
    win_n = a["nsa_w_in_2"][0]
    o_qkv, o_z, o_b = 0, 1536, 2048
    o_uv = o_b + 2 * DN_H
    o_gz = o_uv + 1024
    o_sq = o_gz + 512
    o_sk = o_sq + 512
    o_sz = o_sk + 256
    o_xq = o_sz + 512
    o_xz = o_xq + 512
    o_g = o_xz + 512
    stream = np.zeros((NT, P, TW), np.float32)

    def put(name, t):
        stream[TILE[name], :, :t.shape[1]] = t

    for j in range(2):
        put(f"mk{j}", cols(mkv, CW * j))
        put(f"mv{j}", cols(mkv, BW + CW * j))
        for name, o in (("xmq", o_xq), ("xmz", o_xz), ("swq", o_sq), ("swz", o_sz), ("gmu", o_uv),
                        ("gmv", o_uv + BW), ("gmz", o_gz), ("dnz", o_z)):
            put(f"{name}{j}", cols(w_in, o + CW * j))
    put("swkv", cols(w_in, o_sk))
    put("ba", cols(w_in, o_b, 8))
    for j in range(6):
        put(f"dn{j}", cols(w_in, o_qkv + CW * j))
    for n in range(NBR):
        for h in range(2):
            for g in range(2):
                put(f"gate{n}{h}{g}", cols(w_in, o_g + D * n + 512 * h + CW * g))
            put(f"up{n}{h}", cols(a["w_up"][0, n], 512 * h, 512))
    for j in range(4):
        put(f"out{j}", cols(a["w_out"][0], CW * j))
        put(f"mlao{j}", cols(a["mla_w_o_2"][0], CW * j))
        put(f"nsao{j}", cols(a["nsa_w_o_2"][0], CW * j))
        put(f"nq{j}", cols(win_n, CW * j))
    for f in range(4):
        ab, l = "ab"[f % 2], f // 2
        g, u, d = (a[f"ffn_{ab}_w_{x}_2"][l] for x in ("gate", "up", "down"))
        for i in range(FT):
            put(f"f{f}g{i}", cols(g, CW * i))
            put(f"f{f}u{i}", cols(u, CW * i))
            put(f"f{f}d{i}", cols(d[CW * i:CW * (i + 1)], 0, D))
    put("mlain0", cols(win_m, 0))
    put("mlain1", cols(win_m, CW))
    rope = win_m[:, 640:672]
    last = np.concatenate([win_m[:, 512:640], np.zeros((D, 64), np.float32), rope, rope[:, 16:],
                           rope[:, :16]], axis=1)
    put("mlain2", cols(last, 0))
    q = wuq.reshape(MLA_QL, MLA_H, MLA_N + MLA_R)
    q = np.concatenate([q, q[:, :, 80:96], q[:, :, 64:80]], axis=2).reshape(MLA_QL, MLA_H * P)
    for j in range(4):
        put(f"uq{j}", cols(q, 512 * j, 512))
    kv = wukv.reshape(MLA_KVL, MLA_H, 2, 64)
    put("uk", cols(np.ascontiguousarray(kv[:, :, 0]).reshape(MLA_KVL, D), 0, D))
    put("uv", cols(np.ascontiguousarray(kv[:, :, 1]).reshape(MLA_KVL, D), 0, D))
    for n, name in enumerate(("nkc", "nvc", "nks", "nvs", "nkw", "nvw")):
        put(name, cols(win_n, D + CW * n))
    put("ng", cols(win_n, 2560, 48))

    vec = np.zeros((P, NVEC), np.float32)
    for name, v in (("pre", a["norm_pre"][0]), ("mem", a["norm_mem"][0]), ("fa0", a["ffn_norm_a_2"][0]),
                    ("fa1", a["ffn_norm_a_2"][1]), ("mx0", a["mix_norm_2"][0]), ("mx1", a["mix_norm_2"][1]),
                    ("fb0", a["ffn_norm_b_2"][0]), ("fb1", a["ffn_norm_b_2"][1]),
                    ("qn", a["mla_q_norm_2"][0]), ("kvn", a["mla_kv_norm_2"][0]),
                    ("conv", a["conv_w"][0])):
        v = v.reshape(-1, P).T
        vec[:, VEC[name]:VEC[name] + v.shape[1]] = v
    row = np.zeros((P, NROW), np.float32)
    for name, v in (("onorm", a["dn_norm"][0]), ("gmn", a["gm_norm"][0]), ("bs", a["spatial_b"][0].reshape(-1)),
                    ("dtb", np.tile(a["dt_bias"][0], TT)), ("alog", np.tile(a["a_log"][0], TT)),
                    ("sink", a["sinks"][0])):
        row[:, ROW[name]:ROW[name] + v.shape[0]] = v[None, :]
    con, level, hot = constants()
    tok = lambda v: v[0].reshape(TT, P, D).transpose(1, 0, 2)
    blk = lambda w: w[0].reshape(CMP_L // 2, P, P).transpose(1, 0, 2).reshape(P, TW)
    pos = lambda p: p[0].reshape(CMP_L // 2, P).T
    tbl = np.full((BUCKETS + 1, NSA_H), NEG, np.float32)
    tbl[:BUCKETS] = a["rel_bias_2"]
    arrays = {
        "stream": stream, "x": tok(a["x"]), "mem": tok(a["mem"]), "vec": vec, "row": row, "con": con,
        "level": level, "hot": hot,
        "spatial": a["spatial_w"][0].transpose(1, 0, 2), "bucket_bias": tbl,
        "post": np.broadcast_to(a["norm_post"][0], (P, D)),
        "final": np.broadcast_to(a["final_norm_2"], (P, D)),
        "w1": np.stack([blk(a["nsa_cmp_w1_k_2"]), blk(a["nsa_cmp_w1_v_2"])], axis=1),
        "w2": np.stack([a["nsa_cmp_w2_k_2"][0], a["nsa_cmp_w2_v_2"][0]], axis=1),
        "pos": np.stack([pos(a["nsa_cmp_pos_k_2"]), pos(a["nsa_cmp_pos_v_2"])], axis=1),
    }
    return {k: np.ascontiguousarray(v, dtype=np.float32) for k, v in arrays.items()}


def build(nc, A, out):
    ctx = ExitStack()
    with ctx:
        def sb(name, shape, dt=F32):
            return ctx.enter_context(nc.sbuf_tensor(name, shape, dt))

        def sem(name):
            return ctx.enter_context(nc.semaphore(name))

        raw = [sb(f"raw{i}", [P, TW]) for i in range(SLOTS)]
        high = [sb(f"high{i}", [P, TW], F32R) for i in range(SLOTS)]
        low = [sb(f"low{i}", [P, TW], F32R) for i in range(SLOTS)]
        x = sb("x", [P, TT, D])
        xs = sb("xs", [P, TT, D])
        nth = sb("nth", [P, KC, S], F32R)
        ntl = sb("ntl", [P, KC, S], F32R)
        vec = sb("vec", [P, NVEC])
        row = sb("row", [P, NROW])
        con = sb("con", [P, NCON])
        small = sb("small", [P, 1000])
        SCR = 14336
        scr = sb("scr", [P, SCR])
        with nc.sbuf_tensor("yth", [P, NBR, 4, S], F32R) as yth, \
                nc.sbuf_tensor("ytl", [P, NBR, 4, S], F32R) as ytl:
            pass
        hth = sb("hth", [P, 2, S], F32R)
        htl = sb("htl", [P, 2, S], F32R)
        late = sb("late", [P, 7168])
        ps = [ctx.enter_context(nc.psum_tensor(f"ps{i}", [P, 512], F32)) for i in range(8)]
        line = nc.dram_tensor("bias_by_distance", (NSA_H, 2 * S), F32).ap()

        def carve(memory, sizes, base=0):
            got, at = {}, base
            for name, size in sizes:
                got[name] = memory[:, at:at + size]
                at += size
            assert at <= memory.shape[1], (at, sizes)
            return got

        def c_(name, w):
            return con[:, CON[name]:CON[name] + w]

        ident, upto, before, ones = (c_(n, P) for n in ("ident", "upto", "before", "ones"))
        causal, window = c_("causal", 256), c_("window", 256)
        used_small = [0]

        def tiny(w):
            used_small[0] += w
            assert used_small[0] <= 1000
            return small[:, used_small[0] - w:used_small[0]]

        def r3(ap, a):
            return ap.rearrange("p (a b) -> p a b", a=a)

        def vcol(name, c):
            return vec[:, VEC[name] + c:VEC[name] + c + 1]

        def rowof(name, w):
            return row[:, ROW[name]:ROW[name] + w]

        at_buf = carve(scr, [("s", 1024), ("p", 1024)])
        at_s = [at_buf["s"][:, 0:512], at_buf["s"][:, 512:1024], xs[:, 0, 0:512]]
        at_p = [at_buf["p"][:, 512 * i:512 * i + 512] for i in range(2)]
        xm = carve(scr, [("k", 1024), ("v", 1024), ("q", 1024), ("z", 1024), ("y", 1024)], 2048)
        sw = carve(scr, [("q", 1024), ("k", 512), ("v", 256), ("z", 1024), ("y", 1024)], 7168)
        gm = carve(scr, [("u", 1024), ("z", 1024), ("v", 1024), ("w", 512), ("wt", 512), ("sq", 1024)], 2048)
        dn = carve(scr, [("cin", 3108), ("cact", 3072), ("tok", 3072), ("kb", 1024), ("rw", 512),
                         ("kt", 1024), ("qt", 1024), ("qgt", 512), ("kd", 512)])
        mg = carve(scr, [("sg", 2048), ("prod", 2048), ("m", 2048), ("o", 2048), ("post", 1024)])
        ff = carve(scr, [("sg", 512), ("h", 512)])
        ml = carve(scr, [("buf", 2048), ("q", 4096), ("k", 4096), ("v", 2048), ("y", 2048)])
        mlc = carve(late, [("c", 1280), ("rot", 1024), ("kr", 512)])
        ns = carve(scr, [("buf", 2048), ("q", 2048), ("ks", 1024), ("kw", 1024), ("vs", 512), ("vw", 512),
                         ("xk", 1024), ("xv", 1024), ("bias", 4096)])
        nl = carve(late, [("w1", 4096), ("y", 2048), ("vc", 1024)])
        nt_ = carve(late, [("hot", 512), ("tbl", 16), ("line", 512)], 4096)

        sems = {}

        def s_(name):
            if name not in sems:
                sems[name] = ctx.enter_context(nc.semaphore(name))
            return sems[name]

        raw_here = [s_(f"raw_here{i}") for i in range(SLOTS)]
        w_high, w_low, w_used = s_("w_high"), s_("w_low"), s_("w_used")
        bank_done = [s_("bank_done0"), s_("bank_done1")]

        def val(base, i):
            return base if i is None else i[0] * i[1] + base

        def by(i, step):
            return None if i is None else (i, step)

        def split_high(act, t, i=None):
            act.wait_ge(raw_here[t % SLOTS], val(16 * (t // SLOTS + 1), by(i, 16)))
            if t >= SLOTS:
                act.wait_ge(w_used, val(t - SLOTS + 1, by(i, SLOTS)))
            nc.scalar.activation(high[t % SLOTS][:], raw[t % SLOTS][:], ACT.Copy).then_inc(w_high, 1)

        def split_low(dve, t, i=None):
            dve.wait_ge(w_high, val(t + 1, by(i, SLOTS)))
            nc.vector.tensor_tensor(low[t % SLOTS][:], raw[t % SLOTS][:], high[t % SLOTS][:].bitcast(F32),
                                    ALU.subtract).then_inc(w_low, 1)

        def plain_free(name):
            return UNIT[name] // 2

        def bank_of(name):
            return 4 + UNIT[name] % 2

        class Chain:

            def __init__(self, eng, name):
                self.eng, self.sem, self.n = eng, s_(name), 0

            def mark(self, ins):
                ins.then_inc(self.sem, 1)
                self.n += 1

            def link(self, ins):
                self.mark(ins)
                self.eng.wait_ge(self.sem, self.n)

            def join(self):
                self.eng.wait_ge(self.sem, self.n)

        as3 = lambda ap, n: ap.rearrange("p (t c) -> p t c", t=n)
        TURNS = {
            "mem": (xs, 8, "mem", nth, ntl), "pre": (xs, 8, "pre", nth, ntl),
            "ym": (as3(xm["y"], TT), 4, None, yth[:, 3], ytl[:, 3]),
            "yc": (as3(sw["y"], TT), 4, None, yth[:, 2], ytl[:, 2]),
            "ya": (as3(dn["kt"], TT), 4, None, yth[:, 0], ytl[:, 0]),
            "f0": (xs, 8, "fa0", nth, ntl), "mx0": (xs, 8, "mx0", nth, ntl),
            "mlc": (as3(mlc["c"], TT), 5, "qn", nth, ntl),
            "mly": (as3(ml["y"], TT), 8, None, nth, ntl),
            "f1": (xs, 8, "fb0", nth, ntl), "f2": (xs, 8, "fa1", nth, ntl),
            "mx1": (xs, 8, "mx1", nth, ntl), "nsy": (as3(nl["y"], TT), 8, None, nth, ntl),
            "f3": (xs, 8, "fb1", nth, ntl),
        }
        turn_at, n_ = {}, 0
        for name, spec in TURNS.items():
            turn_at[name] = n_
            n_ += (spec[1] + 1) // 2
        turned, turn_high, turn_low = s_("turned"), s_("turn_high"), s_("turn_low")

        def turn_banks(name):
            n = TURNS[name][1]
            return [(b, turn_at[name] + b + 1, range(2 * b, min(2 * b + 2, n))) for b in range((n + 1) // 2)]

        def pe_turn(pe, name):
            src = TURNS[name][0]
            for b, count, chunks in turn_banks(name):
                for c in chunks:
                    for t in range(TT):
                        at = 256 * (c - 2 * b) + P * t
                        last = nc.tensor.transpose(ps[b][:, at:at + P], src[:, t, P * c:P * c + P], ident)
                last.then_inc(turned, 1)

        def act_turn(act, name):
            _, _, gain, high_, _ = TURNS[name]
            for b, count, chunks in turn_banks(name):
                act.wait_ge(turned, count)
                if gain is None:
                    n = len(chunks)
                    last = nc.scalar.activation(high_[:, 2 * b:2 * b + n, :], r3(ps[b][:, 0:256 * n], n), ACT.Copy)
                else:
                    for c in chunks:
                        at = 256 * (c - 2 * b)
                        last = nc.scalar.activation(high_[:, c, :], ps[b][:, at:at + 256], ACT.Copy,
                                                    scale=vcol(gain, c))
                last.then_inc(turn_high, 1)

        def dve_turn(dve, name):
            _, _, gain, high_, low_ = TURNS[name]
            for b, count, chunks in turn_banks(name):
                dve.wait_ge(turn_high, count)
                if gain is None:
                    n = len(chunks)
                    last = nc.vector.tensor_tensor(low_[:, 2 * b:2 * b + n, :], r3(ps[b][:, 0:256 * n], n),
                                                   high_[:, 2 * b:2 * b + n, :].bitcast(F32), ALU.subtract)
                else:
                    for c in chunks:
                        at = 256 * (c - 2 * b)
                        last = nc.vector.scalar_tensor_tensor(
                            out=low_[:, c, :], in0=ps[b][:, at:at + 256], scalar=vcol(gain, c),
                            in1=high_[:, c, :].bitcast(F32), op0=ALU.mult, op1=ALU.subtract)
                last.then_inc(turn_low, 1)

        def turn_done(name):
            return turn_at[name] + len(turn_banks(name))

        x_ready = s_("x_ready")
        UPDATES = ["post", "ffn0", "mla", "ffn1", "ffn2", "nsa", "ffn3"]
        NORM_OF = {"f0": "post", "mx0": "ffn0", "f1": "mla", "f2": "ffn1", "mx1": "ffn2", "f3": "nsa",
                   "final": "ffn3"}

        def updated(name, t=TT - 1):
            return TT * UPDATES.index(name) + t + 1

        NORMS = ["mem", "pre", "post", "f0", "mx0", "f1", "f2", "mx1", "f3", "final"]
        norm_src = {"mem": scr[:, 0:TT * D].rearrange("p (t c) -> p t c", t=TT), "post": as3(mg["o"], TT)}
        norm_ss = {n: tiny(TT) for n in NORMS}
        norm_ms = {n: tiny(TT) for n in NORMS}
        norm_rs = {n: tiny(TT) for n in NORMS}
        power = tiny(16)
        one_col = tiny(1)
        mark_col = tiny(1)
        norm_sum, norm_mean, norm_root, norm_scaled = (s_(n) for n in ("norm_sum", "norm_mean", "norm_root",
                                                                      "norm_scaled"))

        def act_norm(act, name):
            src = norm_src.get(name, x)
            for t in range(TT):
                if name == "mem":
                    act.wait_ge(mem_here[t], 16)
                if name == "pre":
                    act.wait_ge(x_here, 16)
                if name in NORM_OF:
                    act.wait_ge(x_ready, updated(NORM_OF[name], t))
                nc.scalar.activation(xs[:, t, :], src[:, t, :], ACT.Square,
                                     accum_out=norm_ss[name][:, t:t + 1]).then_inc(norm_sum, 1)

        def pool_norm(pool, name):
            n = NORMS.index(name)
            for t in range(TT):
                pool.wait_ge(norm_sum, TT * n + t + 1)
                nc.gpsimd.tensor_scalar(norm_ms[name][:, t:t + 1], norm_ss[name][:, t:t + 1], 1.0 / D, EPS, ALU.mult,
                                        ALU.add).then_inc(norm_mean, 1)
                pool.wait_ge(norm_mean, TT * n + t + 1)
                nc.gpsimd.tensor_tensor(norm_rs[name][:, t:t + 1], norm_ms[name][:, t:t + 1], power[:, 0:1],
                                        ALU.pow).then_inc(norm_root, 1)

        def dve_norm(dve, name, gain=None):
            n = NORMS.index(name)
            src = norm_src.get(name, x)
            for t in range(TT):
                dve.wait_ge(norm_root, TT * n + t + 1)
                root = norm_rs[name][:, t:t + 1]
                if gain is None:
                    ins = nc.vector.tensor_scalar(xs[:, t, :], src[:, t, :], root, None, ALU.mult)
                else:
                    ins = nc.vector.scalar_tensor_tensor(out=xs[:, t, :], in0=src[:, t, :], scalar=root, in1=gain,
                                                         op0=ALU.mult, op1=ALU.mult)
                ins.then_inc(norm_scaled, 1)

        def pe_norm(pe, name):
            n = NORMS.index(name)
            for t in range(TT):
                pe.wait_ge(norm_scaled, TT * n + t + 1)
                for b, _, chunks in turn_banks(name):
                    for c in chunks:
                        at = 256 * (c - 2 * b) + P * t
                        last = nc.tensor.transpose(ps[b][:, at:at + P], xs[:, t, P * c:P * c + P], ident)
                    if t == TT - 1:
                        last.then_inc(turned, 1)

        def split_product(out_, stat, mov, first, last):
            nc.tensor.matmul(out_, stat[0], mov[0], start=first, stop=False, skip_group_check=True)
            nc.tensor.matmul(out_, stat[0], mov[1], start=False, stop=False, skip_group_check=True)
            return nc.tensor.matmul(out_, stat[1], mov[0], start=False, stop=last, skip_group_check=True)

        def slot(t, k, w):
            return [h[t % SLOTS][:, 0:k * w].rearrange("p (k w) -> p k w", k=k) for h in (high, low)]

        def weights_here(pe, t, i=None):
            pe.wait_ge(w_low, val(t + 1, by(i, SLOTS)))

        def turned_chunk(pe, name, k):
            if name is not None and k % 2 == 0:
                pe.wait_ge(turn_low, turn_at[name] + k // 2 + 1)

        def by_feature(out_, wt, col, act_, ks, k0=0, pe=None, after=None):
            for k in range(ks):
                turned_chunk(pe, after, k)
                last = split_product(out_, [w[:, k, col:col + P] for w in wt],
                                     [a[:, k0 + k, :] for a in act_], k == 0, k == ks - 1)
            return last

        def by_token(out_, wt, col, n, act_, ks, t, k0=0, pe=None, after=None):
            for k in range(ks):
                turned_chunk(pe, after, k)
                last = split_product(out_, [a[:, k0 + k, P * t:P * t + P] for a in act_],
                                     [w[:, k, col:col + n] for w in wt], k == 0, k == ks - 1)
            return last

        NT_ = (nth, ntl)

        def pe_plain(pe, name, kind, after=None):
            t, out_ = TILE[name], ps[bank_of(name)]
            weights_here(pe, t)
            if UNIT[name] >= 2:
                pe.wait_ge(bank_done[UNIT[name] % 2], plain_free(name))
            if kind == "F":
                for j in range(2):
                    last = by_feature(out_[:, S * j:S * j + S], slot(t, KC, CW), P * j, NT_, KC, 0, pe,
                                      None if j else after)
            elif kind == "T":
                for j in range(TT):
                    last = by_token(out_[:, CW * j:CW * j + CW], slot(t, KC, CW), 0, CW, NT_, KC, j, 0, pe,
                                    None if j else after)
            elif kind == "FT":
                by_feature(out_[:, 0:S], slot(t, KC, CW), 0, NT_, KC)
                for j in range(TT):
                    last = by_token(out_[:, S + P * j:S + P * j + P], slot(t, KC, CW), P, P, NT_, KC, j)
            elif kind == "TF":
                for j in range(TT):
                    by_token(out_[:, P * j:P * j + P], slot(t, KC, CW), 0, P, NT_, KC, j)
                last = by_feature(out_[:, S:2 * S], slot(t, KC, CW), P, NT_, KC)
            else:
                n = kind
                for j in range(TT):
                    last = by_token(out_[:, n * j:n * j + n], slot(t, KC, n), 0, n, NT_, KC, j)
            last.then_inc(w_used, 1)

        def read_bank(eng, name):
            eng.wait_ge(w_used, TILE[name] + 1)
            return ps[bank_of(name)]

        def bank_read(name, ins):
            ins.then_inc(bank_done[UNIT[name] % 2], 1)

        def wait_bank(eng, name):
            eng.wait_ge(bank_done[UNIT[name] % 2], UNIT[name] // 2 + 1)

        UNITS = []
        for h in range(XM_H):
            UNITS.append(dict(q=xm["q"][:, S * h:S * h + S], k=xm["k"][:, S * h:S * h + S],
                              v=[r3(xm["v"], TT)[:, t, P * h:P * h + P] for t in range(TT)],
                              d=P, causal=False, mask=None, scale=P ** -0.5))
        for h in range(SW_H):
            p0, kv = 64 * (h % 2), h // (SW_H // SW_KV)
            UNITS.append(dict(q=sw["q"][p0:p0 + 64, S * (h // 2):S * (h // 2) + S],
                              k=sw["k"][p0:p0 + 64, S * kv:S * kv + S],
                              v=[r3(sw["v"], TT)[:, t, 64 * kv:64 * kv + 64] for t in range(TT)],
                              d=64, causal=True, mask=window, scale=SW_D ** -0.5))
        for h in range(MLA_H):
            UNITS.append(dict(q=r3(ml["q"], MLA_H)[0:96, h, :], k=r3(ml["k"], MLA_H)[0:96, h, :],
                              v=[r3(ml["v"], TT)[:, t, 64 * h:64 * h + 64] for t in range(TT)],
                              d=64, causal=True, mask=causal, scale=(MLA_N + MLA_R) ** -0.5))
        for kk, vv in (("ks", "vs"), ("kw", "vw")):
            for h in range(NSA_H):
                p0, g = 64 * (h % 2), h // NSA_R
                UNITS.append(dict(q=ns["q"][p0:p0 + 64, S * (h // 2):S * (h // 2) + S],
                                  k=ns[kk][p0:p0 + 64, S * g:S * g + S],
                                  v=[r3(ns[vv], TT)[:, t, 64 * g:64 * g + 64] for t in range(TT)],
                                  d=64, causal=True, mask=r3(ns["bias"], NSA_H)[:, h, ::-1], scale=NSA_D ** -0.5))
        XM0, SW0 = 0, XM_H
        MLA0 = SW0 + SW_H
        NSA0 = MLA0 + MLA_H
        at_scored, at_max, at_exp, at_turned, at_out, at_read = (
            s_(n) for n in ("at_scored", "at_max", "at_exp", "at_turned", "at_out", "at_read"))
        at_copied = [s_("at_copied0"), s_("at_copied1")]
        RING = 6
        at_mx, at_nm, at_sum, at_inv, at_sinkexp = ([tiny(TT) for _ in range(RING)] for _ in range(5))
        neg_sink = tiny(SW_H)
        def cols_of(u, t):
            return slice(0, 256) if t == 1 else slice(256, 384 if u["causal"] else 512)

        def pe_units(pe, first, n):
            def scores(a):
                u = UNITS[a]
                if a >= 2:
                    pe.wait_ge(at_max if u["causal"] and UNITS[a - 2]["causal"] else at_exp, a - 1)
                for t in (1, 0):
                    c = cols_of(u, t)
                    last = nc.tensor.matmul(ps[a % 2][:, c], u["q"][:, P * t:P * t + P],
                                            u["k"][:, 0:c.stop - c.start], start=True, stop=True)
                last.then_inc(at_scored, 1)

            def turn_probs(a):
                u = UNITS[a]
                pe.wait_ge(at_exp, a + 1)
                if a >= 2:
                    pe.wait_ge(at_copied[a % 2], a // 2)
                for c in range(0, cols_of(u, 0).stop, P):
                    last = nc.tensor.transpose(ps[2 + a % 2][:, c:c + P], at_s[a % 3][:, c:c + P], ident)
                last.then_inc(at_turned, 1)

            def values(a):
                u = UNITS[a]
                pe.wait_ge(at_copied[a % 2], a // 2 + 1)
                if a >= 2:
                    pe.wait_ge(at_read, a - 1)
                d = u["d"]
                for t in (0, 1):
                    c = cols_of(u, t)
                    n_k = (c.stop - c.start) // P
                    for kt in range(n_k):
                        last = nc.tensor.matmul(ps[6 + a % 2][:, d * t:d * t + d],
                                                at_p[a % 2][:, c.start + P * kt:c.start + P * kt + P],
                                                u["v"][kt], start=kt == 0, stop=kt == n_k - 1)
                last.then_inc(at_out, 1)

            for a in range(first, first + n + 3):
                if a < first + n:
                    scores(a)
                if first <= a - 2 < first + n:
                    turn_probs(a - 2)
                if first <= a - 3:
                    values(a - 3)

        def copy_probs(eng, a):
            w = cols_of(UNITS[a], 0).stop
            eng.wait_ge(at_turned, a + 1)
            if a >= 2:
                eng.wait_ge(at_out, a - 1)
            if a % 2 == 0:
                ins = nc.scalar.activation(at_p[0][:, 0:w], ps[2][:, 0:w], ACT.Copy)
            else:
                ins = nc.vector.tensor_copy(at_p[1][:, 0:w], ps[3][:, 0:w])
            ins.then_inc(at_copied[a % 2], 1)

        def act_units(act, first, n, sinks=False):
            for a in range(first, first + n + 2):
                if a < first + n:
                    u, b, b4 = UNITS[a], a % 3, a % RING
                    act.wait_ge(at_max, a + 1)
                    if a >= 3:
                        act.wait_ge(at_turned, a - 2)
                    if a >= RING:
                        act.wait_ge(at_read, a - RING + 1)
                    src = at_s[b] if u["causal"] else ps[a % 2]
                    if sinks:
                        nc.scalar.activation(at_sinkexp[b4], at_nm[b4], ACT.Exp,
                                             bias=row[:, ROW["sink"] + a - first:ROW["sink"] + a - first + 1])
                    for t in (1, 0):
                        c = cols_of(u, t)
                        last = nc.scalar.activation(at_s[b][:, c], src[:, c], ACT.Exp, scale=u["scale"],
                                                    bias=at_nm[b4][:, t:t + 1], accum_out=at_sum[b4][:, t:t + 1])
                    last.then_inc(at_exp, 1)
                if a - 2 >= first and a % 2 == 0:
                    copy_probs(act, a - 2)

        def dve_units(dve, ch, first, n, evac, sinks=False):
            for a in range(first, first + n + 4):
                if a < first + n:
                    u, b, b4 = UNITS[a], a % 3, a % RING
                    dve.wait_ge(at_scored, a + 1)
                    if a >= 3:
                        dve.wait_ge(at_turned, a - 2)
                    if u["causal"]:
                        for t in (1, 0):
                            c = cols_of(u, t)
                            m = u["mask"] if t == 1 else u["mask"][:, P:2 * P]
                            ch.mark(nc.vector.tensor_tensor_reduce(at_s[b][:, c], ps[a % 2][:, c], m, 1.0, -3e38,
                                                                   ALU.add, ALU.max, at_mx[b4][:, t:t + 1]))
                    else:
                        for t in (1, 0):
                            ch.mark(nc.vector.tensor_reduce(at_mx[b4][:, t:t + 1], ps[a % 2][:, cols_of(u, t)],
                                                            AX.X, ALU.max))
                    ch.join()
                    if sinks:
                        ins = nc.vector.tensor_scalar(at_nm[b4], at_mx[b4], -u["scale"],
                                                      neg_sink[:, a - first:a - first + 1], ALU.mult, ALU.min)
                    else:
                        ins = nc.vector.tensor_scalar(at_nm[b4], at_mx[b4], -u["scale"], None, ALU.mult)
                    ins.then_inc(at_max, 1)
                if first <= a - 2 < first + n and a % 2 == 1:
                    copy_probs(dve, a - 2)
                if first <= a - 4:
                    b, b4 = a % 2, (a - 4) % RING
                    dve.wait_ge(at_exp, a - 3)
                    if sinks:
                        ch.link(nc.vector.tensor_tensor(at_sum[b4], at_sum[b4], at_sinkexp[b4], ALU.add))
                    ch.link(nc.vector.reciprocal(at_inv[b4], at_sum[b4]))
                    dve.wait_ge(at_out, a - 3)
                    evac(a - 4, ps[6 + b], at_inv[b4]).then_inc(at_read, 1)


        def bc(ap, n):
            return ap.unsqueeze(2).broadcast_to([ap.shape[0], ap.shape[1], n])

        def rep(ap, n):
            return ap.unsqueeze(1).broadcast_to([ap.shape[0], n, ap.shape[1]])

        setup_done, out_written = s_("setup_done"), s_("out_written")
        mem_here, con_here, x_here, row_here = [s_("mem_here0"), s_("mem_here1")], s_("con_here"), s_("x_here"), \
            s_("row_here")

        def act_step(act, name):
            if TILE[name] + 2 < NT:
                split_high(act, TILE[name] + 2)

        def dve_step(dve, name):
            if TILE[name] + 2 < NT:
                split_low(dve, TILE[name] + 2)

        gm_loaded, gm_sum, gm_mean, gm_root, gm_vn, gm_wturned, gm_wmask, gm_mixed, gm_y, gm_high, gm_low = (
            s_("gm_" + n) for n in ("loaded", "sum", "mean", "root", "vn", "wturned", "wmask", "mixed", "y",
                                    "high", "low"))
        gm_ss, gm_ms, gm_rs = tiny(TT), tiny(TT), tiny(TT)

        d_ba = tiny(16)
        d_beta, d_z, d_az, d_l, d_sp, d_ea, d_g, d_egc, d_dm, d_ekd = (tiny(PAIRS) for _ in range(10))
        d_gc = tiny(16)
        d_ss, d_ms, d_rs = tiny(16), tiny(16), tiny(16)
        d_os, d_om, d_or = tiny(PAIRS), tiny(PAIRS), tiny(PAIRS)
        cin = dn["cin"].rearrange("p (c t) -> p c t", c=12)
        cact = dn["cact"].rearrange("p (c t) -> p c t", c=12)
        tok = dn["tok"].rearrange("p (t c d) -> p t c d", t=TT, c=12)
        d_T, d_TT, d_P = (dn["cin"][:, 1024 * n:1024 * n + 1024] for n in range(3))
        d_E, d_Es, d_Lm = (dn["cact"][:, 1024 * n:1024 * n + 1024] for n in range(3))
        d_L, d_A = dn["kb"], dn["qt"]
        d_Lms = [d_Lm, d_Es]
        d_u, d_wt, d_S, d_vn = (dn["cact"][:, a:b] for a, b in ((0, 1024), (1024, 1536), (1536, 2048),
                                                              (2048, 2560)))
        d_qg = dn["cin"][:, 2048:2560]
        d_kbt = xs[:, 0, :]
        d_level = xs[:, 1, 0:LEVELS * P].rearrange("p (l i) -> p l i", l=LEVELS)
        d_sz = late[:, 3072:4096]
        heads = lambda ap: ap.rearrange("p (t h d) -> p t h d", t=TT, h=DN_H)
        pair = lambda ap, n: ap[:, P * n:P * n + P]
        (dn_conv, dn_act, dn_turn, dn_tok, dn_sum, dn_mean, dn_root, dn_ready, dn_fm, dn_fa, dn_fd, dn_absz,
         dn_exps, dn_g, dn_gcs, dn_gcd, dn_egs, dn_diff, dn_ed, dn_mask, dn_kk, dn_la, dn_lm, dn_p, dn_pc, dn_y,
         dn_t, dn_u, dn_uc, dn_wc, dn_o0, dn_sc, dn_ws, dn_vnd, dn_o1, dn_osum, dn_omean, dn_oroot, dn_out,
         dn_level, dn_zeroed, dn_setup) = (
            s_("dn_" + n) for n in ("conv", "act", "turn", "tok", "sum", "mean", "root", "ready", "fm", "fa", "fd",
                                    "absz", "exps", "g", "gcs", "gcd", "egs", "diff", "ed", "mask", "kk", "la",
                                    "lm", "p", "pc", "y", "t", "u", "uc", "wc", "o0", "sc", "ws", "vnd", "o1",
                                    "osum", "omean", "oroot", "out", "level", "zeroed", "setup"))
        kn_ = lambda t: [tok[:, t, 4 + h, :] for h in range(DN_H)]
        qn_ = lambda t: [tok[:, t, h, :] for h in range(DN_H)]
        DN_TURNS = [
            (kn_(0), dn["kt"][:, 0:512], 0), (kn_(1), dn["kt"][:, 512:1024], 1),
            (qn_(0), dn["qt"][:, 0:512], 2), (qn_(1), dn["qt"][:, 512:1024], 3),
            ([pair(dn["kb"], h) for h in range(4)], d_kbt[:, 0:512], 6),
            ([pair(dn["kb"], 4 + h) for h in range(4)], d_kbt[:, 512:1024], 7),
            ([pair(d_qg, h) for h in range(4)], dn["qgt"], 0),
        ]

        def attention_evac(y, first, d, z=None):
            def evac(a, o, inv):
                h = a - first
                for t in range(TT):
                    c = slice(d * h, d * h + d)
                    if z is None:
                        last = nc.vector.tensor_scalar(y[:, t, c], o[:, d * t:d * t + d], inv[:, t:t + 1], None,
                                                       ALU.mult)
                    else:
                        last = nc.vector.scalar_tensor_tensor(out=y[:, t, c], in0=o[:, d * t:d * t + d],
                                                              scalar=inv[:, t:t + 1], in1=z[:, t, c],
                                                              op0=ALU.mult, op1=ALU.mult)
                return last
            return evac

        ff_gate, ff_h, ff_hhigh, ff_hlow, ff_tile0 = (s_("ff_" + n) for n in ("gate", "h", "hhigh", "hlow",
                                                                           "tile0"))

        def pe_ffn(pe, f):
            tb = TILE[f"f{f}g0"]
            n0 = FT * f

            def gate(t, c, i=None, after=None):
                weights_here(pe, t, i)
                if c > 0:
                    pe.wait_ge(ff_gate, val(c, by(i, 1)))
                for j in range(2):
                    last = by_feature(ps[4][:, S * j:S * j + S], slot(t, KC, CW), P * j, NT_, KC, 0, pe,
                                      None if j else after)
                last.then_inc(w_used, 1)

            def up(t, c, i=None):
                weights_here(pe, t, i)
                if c > 0:
                    pe.wait_ge(ff_h, val(c, by(i, 1)))
                for j in range(2):
                    last = by_feature(ps[5][:, S * j:S * j + S], slot(t, KC, CW), P * j, NT_, KC)
                last.then_inc(w_used, 1)

            def down(t, c, i=None, first=False, last_=False):
                weights_here(pe, t, i)
                pe.wait_ge(ff_hlow, val(c + 1, by(i, 1)))
                w = slot(t, 2, D)
                for tt in range(TT):
                    for half in range(2):
                        for j in range(2):
                            last = split_product(ps[2 * tt + half][:, :],
                                                 [h[:, j, P * tt:P * tt + P] for h in (hth, htl)],
                                                 [a[:, j, 512 * half:512 * half + 512] for a in w],
                                                 first and j == 0, last_ and j == 1)
                    if last_ and tt == 0:
                        last.then_inc(ff_tile0, 1)
                last.then_inc(w_used, 1)

            gate(tb, n0, after=f"f{f}")
            up(tb + 1, n0)
            gate(tb + 2, n0 + 1)
            up(tb + 3, n0 + 1)
            down(tb + 4, n0, first=True)
            with pe.Fori(0, FT - 2) as i:
                gate(tb + 5, n0 + 2, i)
                up(tb + 6, n0 + 2, i)
                down(tb + 7, n0 + 1, i)
            down(tb + 3 * FT - 1, n0 + FT - 1, last_=True)

        def act_ffn(act, f):
            tb = TILE[f"f{f}g0"]
            n0 = FT * f

            def gated(t, c, i=None):
                act.wait_ge(w_used, val(t + 1, by(i, SLOTS)))
                if c > 0:
                    act.wait_ge(ff_h, val(c, by(i, 1)))
                nc.scalar.activation(ff["sg"], ps[4][:, :], ACT.Silu).then_inc(ff_gate, 1)

            def rounded(t_down_before, c, i=None):
                act.wait_ge(ff_h, val(c + 1, by(i, 1)))
                if t_down_before is not None:
                    act.wait_ge(w_used, val(t_down_before + 1, by(i, SLOTS)))
                nc.scalar.activation(hth[:, :, :], r3(ff["h"], 2), ACT.Copy).then_inc(ff_hhigh, 1)

            split_high(act, tb + 2)
            gated(tb, n0)
            split_high(act, tb + 3)
            split_high(act, tb + 4)
            rounded(None, n0)
            gated(tb + 2, n0 + 1)
            split_high(act, tb + 5)
            split_high(act, tb + 6)
            rounded(tb + 4, n0 + 1)
            with act.Fori(0, FT - 2) as i:
                split_high(act, tb + 7, i)
                gated(tb + 5, n0 + 2, i)
                split_high(act, tb + 8, i)
                split_high(act, tb + 9, i)
                rounded(tb + 7, n0 + 2, i)
            if tb + 3 * FT + 1 < NT:
                split_high(act, tb + 3 * FT + 1)

        def dve_ffn(dve, f):
            tb = TILE[f"f{f}g0"]
            n0 = FT * f

            def hidden(t, c, i=None):
                dve.wait_ge(w_used, val(t + 1, by(i, SLOTS)))
                dve.wait_ge(ff_gate, val(c + 1, by(i, 1)))
                if c > 0:
                    dve.wait_ge(ff_hlow, val(c, by(i, 1)))
                nc.vector.tensor_tensor(ff["h"], ff["sg"], ps[5][:, :], ALU.mult).then_inc(ff_h, 1)

            def rest(c, i=None):
                dve.wait_ge(ff_hhigh, val(c + 1, by(i, 1)))
                nc.vector.tensor_tensor(htl[:, :, :], r3(ff["h"], 2), hth[:, :, :].bitcast(F32), ALU.subtract)\
                    .then_inc(ff_hlow, 1)

            split_low(dve, tb + 2)
            split_low(dve, tb + 3)
            hidden(tb + 1, n0)
            split_low(dve, tb + 4)
            rest(n0)
            split_low(dve, tb + 5)
            hidden(tb + 3, n0 + 1)
            split_low(dve, tb + 6)
            rest(n0 + 1)
            with dve.Fori(0, FT - 2) as i:
                split_low(dve, tb + 7, i)
                split_low(dve, tb + 8, i)
                hidden(tb + 6, n0 + 2, i)
                split_low(dve, tb + 9, i)
                rest(n0 + 2, i)
            if tb + 3 * FT + 1 < NT:
                split_low(dve, tb + 3 * FT + 1)
            for tt in range(TT):
                if tt == 0:
                    dve.wait_ge(ff_tile0, f + 1)
                else:
                    dve.wait_ge(w_used, tb + 3 * FT)
                for half in range(2):
                    xo = x[:, tt, 512 * half:512 * half + 512]
                    last = nc.vector.scalar_tensor_tensor(out=xo, in0=ps[2 * tt + half][:, :], scalar=0.5,
                                                          in1=xo, op0=ALU.mult, op1=ALU.add)
                last.then_inc(x_ready, 1)


        mg_sig, mg_mul, mg_add, mg_high, mg_low, mg_post = (
            s_("mg_" + n) for n in ("sig", "mul", "add", "high", "low", "post"))
        MB = TILE["gate000"]

        def pe_merge_branch(pe, n, i=None):
            def at(t):
                return t, (i, 2 * SLOTS) if i is not None else None
            for half in range(2):
                for g in range(2):
                    t = MB + 6 * n + 3 * half + g
                    pe.wait_ge(w_low, val(t + 1, by(i, 6)))
                    q = 4 * n + 2 * half + g
                    if q >= 2:
                        pe.wait_ge(mg_sig, val(q - 1, by(i, 4)))
                    for j in range(2):
                        last = by_feature(ps[4 + g][:, S * j:S * j + S], slot(t, KC, CW), P * j, NT_, KC)
                    last.then_inc(w_used, 1)
                t = MB + 6 * n + 3 * half + 2
                pe.wait_ge(w_low, val(t + 1, by(i, 6)))
                u = 2 * (2 * n + half)
                if u >= 2:
                    pe.wait_ge(mg_mul, val(u, by(i, 4)))
                ys = (yth[:, n, :, :], ytl[:, n, :, :]) if i is None else \
                    tuple(y[:, bass.ds(i + n, 1), :, :].rearrange("p o k s -> p (o k) s") for y in (yth, ytl))
                for c in range(4):
                    last = by_feature(ps[c // 2][:, S * (c % 2):S * (c % 2) + S], slot(t, 4, 512), P * c,
                                      ys, 4)
                last.then_inc(w_used, 1)

        def act_merge_branch(act, n, i=None):
            for half in range(2):
                for g in range(2):
                    t = MB + 6 * n + 3 * half + g
                    merge_split_high(act, t + 2, i)
                    act.wait_ge(w_used, val(t + 1, by(i, 6)))
                    if n > 0:
                        act.wait_ge(mg_mul, val(4 * (n - 1) + 2 * half + g + 1, by(i, 4)))
                    nc.scalar.activation(mg["sg"][:, 1024 * half + 512 * g:1024 * half + 512 * g + 512],
                                         ps[4 + g][:, :], ACT.Sigmoid).then_inc(mg_sig, 1)
                merge_split_high(act, MB + 6 * n + 3 * half + 4, i)

        def merge_split_high(act, t, i):
            act.wait_ge(raw_here[t % SLOTS], val(16 * (t // SLOTS + 1), by(i, 32)))
            act.wait_ge(w_used, val(t - SLOTS + 1, by(i, 6)))
            nc.scalar.activation(high[t % SLOTS][:], raw[t % SLOTS][:], ACT.Copy).then_inc(w_high, 1)

        def merge_split_low(dve, t, i):
            dve.wait_ge(w_high, val(t + 1, by(i, 6)))
            nc.vector.tensor_tensor(low[t % SLOTS][:], raw[t % SLOTS][:], high[t % SLOTS][:].bitcast(F32),
                                    ALU.subtract).then_inc(w_low, 1)

        def dve_merge_branch(dve, n, i=None):
            for half in range(2):
                t = MB + 6 * n + 3 * half
                merge_split_low(dve, t + 2, i)
                merge_split_low(dve, t + 3, i)
                merge_split_low(dve, t + 4, i)
                dve.wait_ge(w_used, val(t + 3, by(i, 6)))
                for b in range(2):
                    q = 4 * n + 2 * half + b
                    c = slice(1024 * half + 512 * b, 1024 * half + 512 * b + 512)
                    dve.wait_ge(mg_sig, val(q + 1, by(i, 4)))
                    if n > 0:
                        dve.wait_ge(mg_add, val(4 * (n - 1) + 2 * half + b + 1, by(i, 4)))
                    nc.vector.tensor_tensor(mg["prod"][:, c], ps[b][:, :], mg["sg"][:, c], ALU.mult)\
                        .then_inc(mg_mul, 1)
                for b in range(2):
                    q = 4 * n + 2 * half + b
                    c = slice(1024 * half + 512 * b, 1024 * half + 512 * b + 512)
                    dve.wait_ge(mg_mul, val(q + 1, by(i, 4)))
                    if n == 0 and i is None:
                        ins = nc.vector.tensor_copy(mg["m"][:, c], mg["prod"][:, c])
                    else:
                        ins = nc.vector.tensor_tensor(mg["m"][:, c], mg["m"][:, c], mg["prod"][:, c], ALU.add)
                    ins.then_inc(mg_add, 1)

        (ml_c, ml_kr, ml_ss, ml_ms, ml_rs, ml_cs, ml_q, ml_qa, ml_qd, ml_k, ml_ka, ml_kd, ml_v, ml_va, ml_krd) = (
            s_("ml_" + n) for n in ("c", "kr", "ss", "ms", "rs", "cs", "q", "qa", "qd", "k", "ka", "kd", "v",
                                    "va", "krd"))
        m_ss, m_ms, m_rs = tiny(4), tiny(4), tiny(4)
        mc = as3(mlc["c"], TT)
        MLC = [(t, c) for c in (slice(0, MLA_QL), slice(MLA_QL, MLA_QL + MLA_KVL)) for t in range(TT)]
        mq, mk_ = r3(ml["q"], MLA_H), r3(ml["k"], MLA_H)
        mrot = mlc["rot"].rearrange("p (r h s) -> p r h s", r=2, h=2)
        cos_, sin_ = c_("cos", S), c_("sin", S)

        (ns_w1, ns_tbl, ns_line, ns_linec, ns_lined, ns_bias, ns_hid, ns_hc, ns_kc, ns_kcd, ns_vc,
         ns_vcd, ns_cs, ns_cm, ns_ce, ns_posed, ns_ct, ns_ctc, ns_co, ns_cy, ns_zero, ns_pos) = (
            s_("ns_" + n) for n in ("w1", "tbl", "line", "linec", "lined", "bias", "hid", "hc", "kc",
                                    "kcd", "vc", "vcd", "cs", "cm", "ce", "posed", "ct", "ctc", "co", "cy", "zero",
                                    "pos"))
        n_gate = tiny(TT * 48)
        n_hid = [tiny(64), tiny(64)]
        n_pos, n_kc = tiny(2), tiny(NSA_G * 2 * NCMP)
        n_mx, n_sum, n_inv, n_cg = (tiny(TT * NSA_H) for _ in range(4))
        n_ag = [tiny(TT) for _ in range(2)]
        kc2 = n_kc.rearrange("p (g two n) -> p g two n", g=NSA_G, two=2)
        w2s = sb("w2s", [P, 2, 64])
        poss = sb("poss", [P, 2, CMP_L // 2])
        sc = xs[:, 0, :].rearrange("p (t h n) -> p t h n", t=TT, h=NSA_H)
        sct = xs[:, 1, :]
        gate3 = n_gate.rearrange("p (t h b) -> p t h b", t=TT, h=NSA_H)
        xx = [r3(ns["xk"], NSA_G), r3(ns["xv"], NSA_G)]
        w1s = nl["w1"].rearrange("p (m j f) -> p m j f", m=2, j=CMP_L // 2)
        vcd = r3(nl["vc"], NSA_G)
        nbias = r3(ns["bias"], NSA_H)
        ny = as3(nl["y"], TT)
        BIAS_ROWS = BUCKETS + 1

        def doubled(dst, bank, c_dst):
            src = r3(bank, 2)
            d = r3(dst, c_dst).rearrange("p (c two) s -> p two c s", two=2)
            for g in range(2):
                for half in range(2):
                    yield d[64 * half:64 * half + 64, g], src[64 * g:64 * g + 64]


        block = ctx.enter_context(nc.Block())

        @block.sync
        def _(sp):
            for t in range(TT):
                sp.dma_start(norm_src["mem"][:, t, :], A["mem"][:, t, :]).then_inc(mem_here[t], 16)
            sp.dma_start(con[:], A["con"]).then_inc(con_here, 16)
            sp.dma_start(vec[:], A["vec"]).then_inc(con_here, 16)
            sp.dma_start(raw[0][:], A["stream"][0]).then_inc(raw_here[0], 16)
            sp.dma_start(x[:, :, :], A["x"]).then_inc(x_here, 16)
            sp.dma_start(row[:], A["row"]).then_inc(row_here, 16)
            for t in range(1, SLOTS):
                sp.dma_start(raw[t][:], A["stream"][t]).then_inc(raw_here[t], 16)
            with sp.Fori(1, (NT - 1) // SLOTS) as i:
                for c in range(SLOTS):
                    tile = sp.snap(i * SLOTS + c)
                    sp.wait_ge(w_low, i * SLOTS + (c - SLOTS + 1))
                    sp.dma_start(raw[c][:], A["stream"][bass.ds(tile, 1)].rearrange("o p w -> (o p) w"))\
                        .then_inc(raw_here[c], 16)
            t = NT - 1
            sp.wait_ge(w_low, t - SLOTS + 1)
            sp.dma_start(raw[t % SLOTS][:], A["stream"][t]).then_inc(raw_here[t % SLOTS], 16)
            for t in range(TT):
                sp.wait_ge(norm_scaled, TT * NORMS.index("final") + t + 1)
                sp.dma_start(out[:, t, :], xs[:, t, :]).then_inc(out_written, 16)
            sp.wait_ge(out_written, 16 * TT)

        @block.gpsimd
        def _(pool):
            nc.gpsimd.memset(power, -0.5).then_inc(setup_done, 1)
            nc.gpsimd.memset(one_col, 1.0).then_inc(setup_done, 1)
            pool.wait_ge(setup_done, 2)
            pool_norm(pool, "mem")
            pool_norm(pool, "pre")
            pool.wait_ge(turn_low, turn_done("ym"))
            pool.dma_start(gm["w"], A["spatial"].rearrange("p g q -> p (g q)")).then_inc(gm_loaded, 16)
            pool.dma_start(xs[:, 1, 0:LEVELS * P], A["level"]).then_inc(dn_level, 16)
            pool.wait_ge(gm_sum, TT)
            nc.gpsimd.tensor_scalar(gm_ms, gm_ss, 1.0 / BW, EPS, ALU.mult, ALU.add).then_inc(gm_mean, 1)
            pool.wait_ge(gm_mean, 1)
            nc.gpsimd.tensor_tensor(gm_rs, gm_ms, power[:, 0:TT], ALU.pow).then_inc(gm_root, 1)
            pool.wait_ge(gm_low, 1)
            nc.gpsimd.memset(cin[:, :, 0:3], 0.0).then_inc(dn_zeroed, 1)
            pool.wait_ge(dn_sum, 1)
            nc.gpsimd.tensor_scalar(d_ms, d_ss, 1.0, EPS, ALU.mult, ALU.add).then_inc(dn_mean, 1)
            pool.wait_ge(dn_mean, 1)
            nc.gpsimd.tensor_tensor(d_rs, d_ms, power, ALU.pow).then_inc(dn_root, 1)
            pool.wait_ge(dn_osum, 1)
            nc.gpsimd.tensor_scalar(d_om, d_os, 1.0 / P, EPS, ALU.mult, ALU.add).then_inc(dn_omean, 1)
            pool.wait_ge(dn_omean, 1)
            nc.gpsimd.tensor_tensor(d_or, d_om, power[:, 0:PAIRS], ALU.pow).then_inc(dn_oroot, 1)
            pool.wait_ge(turn_low, turn_done("ya"))
            pool.dma_start(mg["post"], A["post"]).then_inc(mg_post, 16)
            pool_norm(pool, "post")
            pool_norm(pool, "f0")
            pool_norm(pool, "mx0")
            pool.wait_ge(ml_ss, 4)
            nc.gpsimd.tensor_scalar(m_ms[:, 0:2], m_ss[:, 0:2], 1.0 / MLA_QL, EPS, ALU.mult, ALU.add)\
                .then_inc(ml_ms, 1)
            nc.gpsimd.tensor_scalar(m_ms[:, 2:4], m_ss[:, 2:4], 1.0 / MLA_KVL, EPS, ALU.mult, ALU.add)\
                .then_inc(ml_ms, 1)
            pool.wait_ge(ml_ms, 2)
            nc.gpsimd.tensor_tensor(m_rs, m_ms, power[:, 0:4], ALU.pow).then_inc(ml_rs, 1)
            pool.wait_ge(x_ready, updated("mla"))
            pool.dma_start(nl["w1"], A["w1"].rearrange("p m w -> p (m w)")).then_inc(ns_w1, 16)
            pool.dma_start(w2s[:, :, :], A["w2"]).then_inc(ns_w1, 16)
            pool.dma_start(poss[:, :, :], A["pos"]).then_inc(ns_w1, 16)
            pool.dma_start(nt_["hot"][0:BIAS_ROWS, :], A["hot"]).then_inc(ns_tbl, 16)
            pool.dma_start(nt_["tbl"][0:BIAS_ROWS, :], A["bucket_bias"]).then_inc(ns_tbl, 16)
            nc.gpsimd.memset(n_kc, 0.0)
            nc.gpsimd.memset(nl["vc"], 0.0).then_inc(ns_zero, 1)
            pool_norm(pool, "f1")
            pool_norm(pool, "f2")
            pool.wait_ge(ns_linec, 1)
            pool.dma_start(line, nt_["line"][0:NSA_H, :]).then_inc(ns_lined, 16)
            pool.wait_ge(ns_lined, 16)
            pool.dma_start(nbias, bass.AP(line.tensor, S - P + 1, [[1, P], [2 * S, NSA_H], [1, S]]))\
                .then_inc(ns_bias, 16)
            pool_norm(pool, "mx1")
            pool.wait_ge(turn_low, turn_done("mx1"))
            nc.gpsimd.memset(xs[:, 0, :], 0.0).then_inc(ns_zero, 1)
            pool_norm(pool, "f3")
            pool.dma_start(scr[:, 4096:4096 + D], A["final"]).then_inc(mg_post, 16)
            pool_norm(pool, "final")

        @block.scalar
        def _(act):
            act_norm(act, "mem")
            split_high(act, 0)
            act.wait_ge(con_here, 32)
            act_turn(act, "mem")
            split_high(act, 1)
            for name, dst in (("mk0", xm["k"][:, 0:512]), ("mk1", xm["k"][:, 512:1024])):
                act_step(act, name)
                bank_read(name, nc.scalar.activation(dst, read_bank(act, name)[:, :], ACT.Copy))
            act_step(act, "mv0")
            act_step(act, "mv1")
            act.wait_ge(turn_low, turn_done("mem"))
            act_norm(act, "pre")
            act.wait_ge(w_used, TILE["mv1"] + 1)
            act_turn(act, "pre")
            for j in range(2):
                name = f"xmq{j}"
                act_step(act, name)
                bank_read(name, nc.scalar.activation(xm["q"][:, 512 * j:512 * j + 512], read_bank(act, name)[:, :],
                                                     ACT.Copy))
            for j in range(2):
                name = f"xmz{j}"
                act_step(act, name)
                bank_read(name, nc.scalar.activation(as3(xm["z"], TT)[:, :, CW * j:CW * j + CW],
                                                     r3(read_bank(act, name), TT), ACT.Silu))
            act_units(act, XM0, XM_H)
            act_turn(act, "ym")
            for j in range(2):
                name = f"swq{j}"
                act_step(act, name)
                bank_read(name, nc.scalar.activation(sw["q"][:, 512 * j:512 * j + 512], read_bank(act, name)[:, :],
                                                     ACT.Copy))
            act_step(act, "swkv")
            for j in range(2):
                name = f"swz{j}"
                act_step(act, name)
                bank_read(name, nc.scalar.activation(as3(sw["z"], TT)[:, :, CW * j:CW * j + CW],
                                                     r3(read_bank(act, name), TT), ACT.Silu))
            act_units(act, SW0, SW_H, sinks=True)
            act_turn(act, "yc")
            for name, dst, func in (("gmu0", gm["u"][:, 0:512], ACT.Gelu_apprx_tanh),
                                    ("gmu1", gm["u"][:, 512:1024], ACT.Gelu_apprx_tanh),
                                    ("gmz0", gm["z"][:, 0:512], ACT.Silu), ("gmz1", gm["z"][:, 512:1024], ACT.Silu)):
                act_step(act, name)
                bank_read(name, nc.scalar.activation(dst, read_bank(act, name)[:, :], func))
            for j in range(2):
                name = f"gmv{j}"
                act_step(act, name)
                bank_read(name, nc.scalar.activation(as3(gm["v"], TT)[:, :, CW * j:CW * j + CW],
                                                     r3(read_bank(act, name), TT), ACT.Gelu_apprx_tanh))
            wait_bank(act, "gmv0")
            wait_bank(act, "gmv1")
            for t in range(TT):
                nc.scalar.activation(gm["sq"][:, 512 * t:512 * t + 512], gm["v"][:, 512 * t:512 * t + 512],
                                     ACT.Square, accum_out=gm_ss[:, t:t + 1]).then_inc(gm_sum, 1)
            act.wait_ge(gm_y, 1)
            nc.scalar.activation(yth[:, 1], r3(gm["sq"], 4), ACT.Copy).then_inc(gm_high, 1)
            ch = Chain(act, "act_chain")
            act_step(act, "ba")
            act.wait_ge(dn_zeroed, 1)
            act.wait_ge(gm_low, 1)
            for j in range(6):
                name = f"dn{j}"
                act_step(act, name)
                bank_read(name, nc.scalar.activation(cin[:, 2 * j:2 * j + 2, 3:3 + S], r3(read_bank(act, name), 2),
                                                     ACT.Copy))
                if j:
                    act.wait_ge(dn_conv, j)
                    nc.scalar.activation(cact[:, 2 * j - 2:2 * j, :], cact[:, 2 * j - 2:2 * j, :], ACT.Silu)\
                        .then_inc(dn_act, 1)
            for j in range(2):
                name = f"dnz{j}"
                act_step(act, name)
                bank_read(name, nc.scalar.activation(as3(d_sz, TT)[:, :, CW * j:CW * j + CW],
                                                     r3(read_bank(act, name), TT), ACT.Silu))
            act.wait_ge(dn_conv, 6)
            nc.scalar.activation(cact[:, 10:12, :], cact[:, 10:12, :], ACT.Silu).then_inc(dn_act, 1)
            wait_bank(act, "ba")
            nc.scalar.activation(r3(d_beta, TT), r3(d_ba, TT)[:, :, 0:DN_H], ACT.Sigmoid).then_inc(dn_exps, 1)
            act.wait_ge(dn_absz, 1)
            nc.scalar.activation(d_ea, rowof("alog", PAIRS), ACT.Exp).then_inc(dn_exps, 1)
            ch.link(nc.scalar.activation(d_l, d_az, ACT.Exp, scale=-1.0))
            nc.scalar.activation(d_l, d_l, ACT.Ln, bias=one_col).then_inc(dn_exps, 1)
            act.wait_ge(dn_gcd, 1)
            nc.scalar.activation(d_egc, d_gc[:, 0:PAIRS], ACT.Exp).then_inc(dn_egs, 1)
            nc.scalar.activation(d_ekd, d_dm, ACT.Exp).then_inc(dn_egs, 1)
            act.wait_ge(dn_diff, PAIRS)
            nc.scalar.activation(d_E, d_E, ACT.Exp).then_inc(dn_ed, 1)
            for n, (_, dst, b) in enumerate(DN_TURNS):
                if n % 2 == 0:
                    act.wait_ge(dn_fm, n + 1)
                    nc.scalar.activation(dst, ps[b][:, :], ACT.Copy).then_inc(dn_fa, 1)
            for l in range(1, LEVELS):
                for b in range(2):
                    act.wait_ge(dn_p, 2 * l + b + 1)
                    nc.scalar.activation(d_P[:, 512 * b:512 * b + 512], ps[b][:, :], ACT.Copy).then_inc(dn_pc, 1)
            act.wait_ge(dn_u, 2)
            nc.scalar.activation(d_wt, ps[2][:, :], ACT.Copy).then_inc(dn_wc, 1)
            act.wait_ge(dn_o0, 2)
            nc.scalar.activation(d_S, ps[6][:, :], ACT.Copy).then_inc(dn_sc, 1)
            act_turn(act, "ya")
            act_merge_branch(act, 0)
            with act.Fori(0, NBR - 1) as i:
                act_merge_branch(act, 1, i)
            act.wait_ge(mg_add, 4 * NBR)
            act.wait_ge(w_used, TILE["up31"] + 1)
            for b in range(2):
                nc.scalar.activation(nth[:, 4 * b:4 * b + 4, :], r3(mg["m"][:, 1024 * b:1024 * b + 1024], 4),
                                     ACT.Copy).then_inc(mg_high, 1)
            for j in range(4):
                name = f"out{j}"
                act_step(act, name)
                bank_read(name, nc.scalar.activation(as3(mg["o"], TT)[:, :, CW * j:CW * j + CW],
                                                     r3(read_bank(act, name), TT), ACT.Copy))
            wait_bank(act, "out2")
            wait_bank(act, "out3")
            act_norm(act, "post")
            act_norm(act, "f0")
            act_turn(act, "f0")
            act_ffn(act, 0)
            act_norm(act, "mx0")
            act_turn(act, "mx0")
            for j in range(2):
                name = f"mlain{j}"
                act_step(act, name)
                bank_read(name, nc.scalar.activation(mc[:, :, CW * j:CW * j + CW], r3(read_bank(act, name), TT),
                                                     ACT.Copy))
            act_step(act, "mlain2")
            wait_bank(act, "mlain0")
            wait_bank(act, "mlain1")
            wait_bank(act, "mlain2")
            for n, (t, c) in enumerate(MLC):
                w = c.stop - c.start
                nc.scalar.activation(xs[:, 0, 0:w] if n % 2 else xs[:, 1, 0:w], mc[:, t, c], ACT.Square,
                                     accum_out=m_ss[:, n:n + 1]).then_inc(ml_ss, 1)
                if n == 1:
                    act.wait_ge(ml_ss, 2)
            act_turn(act, "mlc")
            for j in range(4):
                act_step(act, f"uq{j}")
                for b in range(2):
                    act.wait_ge(ml_q, 2 * j + b + 1)
                    h = 4 * j + 2 * b
                    nc.scalar.activation(mq[0:64, h:h + 2, :], r3(ps[2 * (j % 2) + b][0:64, :], 2), ACT.Copy)\
                        .then_inc(ml_qa, 1)
            act_step(act, "uk")
            act.wait_ge(ml_k, 1)
            for b in range(4):
                nc.scalar.activation(mk_[0:64, 4 * b:4 * b + 4:2, :], r3(ps[b][0:64, :], 2), ACT.Copy)\
                    .then_inc(ml_ka, 1)
            act_step(act, "uv")
            act.wait_ge(ml_v, 1)
            for n in range(4):
                t, half = n // 2, n % 2
                nc.scalar.activation(as3(ml["v"], TT)[:, t, 512 * half:512 * half + 512], ps[4 + n][:, :], ACT.Copy)\
                    .then_inc(ml_va, 1)
            act_units(act, MLA0, MLA_H)
            act_turn(act, "mly")
            for j in range(4):
                act_step(act, f"mlao{j}")
            act_norm(act, "f1")
            act_turn(act, "f1")
            act_ffn(act, 1)
            act_norm(act, "f2")
            act.wait_ge(ns_line, 1)
            nc.scalar.activation(nt_["line"][0:NSA_H, :], ps[6][0:NSA_H, :], ACT.Copy, scale=NSA_D ** 0.5)\
                .then_inc(ns_linec, 1)
            act_turn(act, "f2")
            act_ffn(act, 2)
            act_norm(act, "mx1")
            act_turn(act, "mx1")
            act_step(act, "nkc")
            act_step(act, "nvc")
            for j in range(4):
                name = f"nq{j}"
                act_step(act, name)
                bank_read(name, nc.scalar.activation(ns["q"][:, 512 * j:512 * j + 512], read_bank(act, name)[:, :],
                                                     ACT.Copy))
            act_step(act, "nks")
            act.wait_ge(ns_pos, 2)
            act.wait_ge(ns_hid, 1)
            for m in range(2):
                nc.scalar.activation(n_hid[m][:, 0:NSA_G * NCMP], ps[1][:, 64 * m:64 * m + NSA_G * NCMP],
                                     ACT.Gelu_apprx_tanh, bias=n_pos[:, m:m + 1]).then_inc(ns_hc, 1)
            act_step(act, "nvs")
            bank_read("nvs", nc.scalar.activation(ns["vs"], read_bank(act, "nvs")[:, :], ACT.Copy))
            act_step(act, "nkw")
            act_step(act, "nvw")
            bank_read("nvw", nc.scalar.activation(ns["vw"], read_bank(act, "nvw")[:, :], ACT.Copy))
            act_step(act, "ng")
            bank_read("ng", nc.scalar.activation(n_gate, read_bank(act, "ng")[:, 0:TT * 48], ACT.Sigmoid))
            for t in range(TT):
                act.wait_ge(ns_cm, t + 1)
                k = min(NCMP, (P * t + P - CMP_L) // CMP_ST + 1)
                nc.scalar.activation(sc[:, t, :, 0:k], sc[:, t, :, 0:k], ACT.Exp, scale=NSA_D ** -0.5)\
                    .then_inc(ns_ce, 1)
            act_units(act, NSA0, 2 * NSA_H)
            act_turn(act, "nsy")
            for j in range(4):
                act_step(act, f"nsao{j}")
            act_norm(act, "f3")
            act_turn(act, "f3")
            act_ffn(act, 3)
            act_norm(act, "final")

        @block.vector
        def _(dve):
            ch = Chain(dve, "dve_chain")
            dve_norm(dve, "mem")
            split_low(dve, 0)
            dve_turn(dve, "mem")
            split_low(dve, 1)
            dve.wait_ge(row_here, 16)
            nc.vector.tensor_scalar(neg_sink, rowof("sink", SW_H), -1.0, None, ALU.mult).then_inc(dn_setup, 1)
            dve_step(dve, "mk0")
            dve_step(dve, "mk1")
            for j in range(2):
                name = f"mv{j}"
                dve_step(dve, name)
                bank_read(name, nc.vector.tensor_copy(as3(xm["v"], TT)[:, :, CW * j:CW * j + CW],
                                                      r3(read_bank(dve, name), TT)))
            dve_norm(dve, "pre")
            dve_turn(dve, "pre")
            for name in ("xmq0", "xmq1", "xmz0", "xmz1"):
                dve_step(dve, name)
            wait_bank(dve, "xmz0")
            wait_bank(dve, "xmz1")
            dve_units(dve, ch, XM0, XM_H, attention_evac(as3(xm["y"], TT), XM0, P, as3(xm["z"], TT)))
            dve_turn(dve, "ym")
            dve_step(dve, "swq0")
            dve_step(dve, "swq1")
            dve_step(dve, "swkv")
            b = read_bank(dve, "swkv")
            for kv in range(SW_KV):
                for half in range(2):
                    nc.vector.tensor_copy(sw["k"][64 * half:64 * half + 64, S * kv:S * kv + S],
                                          b[64 * kv:64 * kv + 64, 0:S])
            bank_read("swkv", nc.vector.tensor_copy(sw["v"], b[:, S:2 * S]))
            dve_step(dve, "swz0")
            dve_step(dve, "swz1")
            wait_bank(dve, "swz0")
            wait_bank(dve, "swz1")
            dve.wait_ge(dn_setup, 1)
            dve_units(dve, ch, SW0, SW_H, attention_evac(as3(sw["y"], TT), SW0, SW_D, as3(sw["z"], TT)), sinks=True)
            dve_turn(dve, "yc")
            for name in ("gmu0", "gmu1", "gmz0", "gmz1", "gmv0", "gmv1"):
                dve_step(dve, name)
            for name in ("gmu0", "gmu1", "gmz0", "gmz1"):
                wait_bank(dve, name)
            dve.wait_ge(gm_wturned, 1)
            for g in range(4):
                last = nc.vector.tensor_tensor(pair(gm["wt"], g), pair(ps[0], g), upto, ALU.mult)
            last.then_inc(gm_wmask, 1)
            ch.link(nc.vector.tensor_tensor(gm["u"], gm["u"], gm["z"], ALU.mult))
            dve.wait_ge(gm_root, 1)
            for t in range(TT):
                c = slice(512 * t, 512 * t + 512)
                nc.vector.scalar_tensor_tensor(out=gm["v"][:, c], in0=gm["v"][:, c], scalar=gm_rs[:, t:t + 1],
                                               in1=rowof("gmn", 512), op0=ALU.mult, op1=ALU.mult)\
                    .then_inc(gm_vn, 1)
            dve.wait_ge(gm_mixed, 1)
            bs = r3(rowof("bs", 512), 4)
            for b in range(2):
                for t in range(TT):
                    src = ps[1 + b].rearrange("p (g t c) -> p g t c", g=2, t=TT)[:, :, t, :]
                    dst = gm["sq"].rearrange("p (g t c) -> p g t c", g=4, t=TT)[:, 2 * b:2 * b + 2, t, :]
                    ch.mark(nc.vector.tensor_tensor(dst, src, bs[:, 2 * b:2 * b + 2, :], ALU.add))
            ch.join()
            nc.vector.tensor_tensor(gm["sq"], gm["sq"], gm["u"], ALU.mult).then_inc(gm_y, 1)
            dve.wait_ge(gm_high, 1)
            nc.vector.tensor_tensor(ytl[:, 1], r3(gm["sq"], 4), yth[:, 1].bitcast(F32), ALU.subtract)\
                .then_inc(gm_low, 1)
            dve_step(dve, "ba")
            bank_read("ba", nc.vector.tensor_copy(d_ba, read_bank(dve, "ba")[:, 0:16]))
            wait_bank(dve, "ba")
            ch.link(nc.vector.tensor_tensor(r3(d_z, TT), r3(d_ba, TT)[:, :, DN_H:2 * DN_H],
                                            r3(rowof("dtb", PAIRS), TT), ALU.add))
            nc.vector.scalar_tensor_tensor(out=d_az, in0=d_z, scalar=-1.0, in1=d_z, op0=ALU.mult, op1=ALU.max)\
                .then_inc(dn_absz, 1)
            for j in range(6):
                name = f"dn{j}"
                dve_step(dve, name)
                wait_bank(dve, name)
                for tap in range(4):
                    for c in (2 * j, 2 * j + 1):
                        w = vcol("conv", 12 * tap + c)
                        if tap == 0:
                            ins = nc.vector.tensor_scalar(cact[:, c, :], cin[:, c, 0:S], w, None, ALU.mult)
                        else:
                            ins = nc.vector.scalar_tensor_tensor(out=cact[:, c, :], in0=cin[:, c, tap:tap + S],
                                                                 scalar=w, in1=cact[:, c, :], op0=ALU.mult,
                                                                 op1=ALU.add)
                        if tap == 3 and c % 2:
                            ins.then_inc(dn_conv, 1)
                        else:
                            ch.mark(ins)
                    if tap < 3:
                        ch.join()
            dve_step(dve, "dnz0")
            dve_step(dve, "dnz1")
            for j in range(6):
                dve.wait_ge(dn_turn, j + 1)
                nc.vector.tensor_copy(tok[:, :, 2 * j:2 * j + 2, :],
                                      ps[j % 4].rearrange("p (t c d) -> p t c d", t=TT, c=2)).then_inc(dn_tok, 1)
            dve.wait_ge(dn_exps, 3)
            ch.link(nc.vector.scalar_tensor_tensor(out=d_sp, in0=d_z, scalar=0.0, in1=d_l, op0=ALU.max,
                                                   op1=ALU.add))
            ch.link(nc.vector.scalar_tensor_tensor(out=d_g, in0=d_sp, scalar=-1.0, in1=d_ea, op0=ALU.mult,
                                                   op1=ALU.mult))
            nc.vector.tensor_copy(r3(d_Lm, PAIRS), bc(d_g, P)).then_inc(dn_g, 1)
            dve.wait_ge(dn_tok, 6)
            sqb = dn["cin"][:, 0:2048].rearrange("p (t c d) -> p t c d", t=TT, c=2 * DN_H)
            for t in range(TT):
                ch.mark(nc.vector.tensor_tensor(sqb[:, t], tok[:, t, 0:8, :], tok[:, t, 0:8, :], ALU.mult))
            ch.join()
            nc.vector.tensor_reduce(d_ss, dn["cin"][:, 0:2048].rearrange("p (c d) -> p c d", d=P), AX.X, ALU.add)\
                .then_inc(dn_sum, 1)
            dve.wait_ge(dn_gcs, 1)
            ch.link(nc.vector.tensor_copy(d_gc, ps[4][:, 0:16]))
            nc.vector.tensor_tensor(d_dm, d_gc[:, 8:16], d_gc[:, 0:8], ALU.subtract).then_inc(dn_gcd, 1)
            for n in range(PAIRS):
                nc.vector.scalar_tensor_tensor(out=pair(d_E, n), in0=pair(ps[1 + n // 4], n % 4),
                                               scalar=d_gc[:, n:n + 1], in1=upto, op0=ALU.subtract, op1=ALU.mult)\
                    .then_inc(dn_diff, 1)
            dve.wait_ge(dn_root, 1)
            rs = r3(d_rs, TT)
            ch.link(nc.vector.tensor_scalar(rs[:, :, 0:DN_H], rs[:, :, 0:DN_H], float(P) ** -0.5, None, ALU.mult))
            for t in range(TT):
                ch.mark(nc.vector.tensor_tensor(tok[:, t, 0:8, :], tok[:, t, 0:8, :], bc(d_rs[:, 8 * t:8 * t + 8], P),
                                                ALU.mult))
            for t in range(TT):
                ch.mark(nc.vector.tensor_tensor(tok[:, t, 8:12, :], tok[:, t, 8:12, :],
                                                bc(d_beta[:, 4 * t:4 * t + 4], P), ALU.mult))
            ch.join()
            kb = heads(dn["kb"])
            for t in range(TT):
                ch.mark(nc.vector.tensor_tensor(kb[:, t], tok[:, t, 4:8, :], bc(d_beta[:, 4 * t:4 * t + 4], P),
                                                ALU.mult))
            ch.join()
            dve.wait_ge(dn_egs, 2)
            nc.vector.tensor_tensor(r3(dn["rw"], 4), kb[:, 1], bc(d_egc[:, 4:8], P), ALU.mult)
            nc.vector.tensor_tensor(r3(dn["kd"], 4), tok[:, 0, 4:8, :], bc(d_ekd[:, 0:4], P), ALU.mult)
            nc.vector.tensor_tensor(r3(d_qg, 4), tok[:, 1, 0:4, :], bc(d_egc[:, 4:8], P), ALU.mult)\
                .then_inc(dn_ready, 1)
            dve.wait_ge(dn_ed, 1)
            ch.link(nc.vector.tensor_tensor(r3(d_E, PAIRS), r3(d_E, PAIRS), rep(upto, PAIRS), ALU.mult))
            ch.mark(nc.vector.tensor_tensor(r3(d_Es, PAIRS), r3(d_E, PAIRS), rep(before, PAIRS), ALU.mult))
            for n, (_, dst, b) in enumerate(DN_TURNS):
                if n % 2:
                    dve.wait_ge(dn_fm, n + 1)
                    nc.vector.tensor_copy(dst, ps[b][:, :]).then_inc(dn_fd, 1)
            dve.wait_ge(dn_kk, 2)
            ch.join()
            for b in range(2):
                c = slice(512 * b, 512 * b + 512)
                ch.mark(nc.vector.tensor_tensor(d_L[:, c], ps[1 + b][:, :], d_Es[:, c], ALU.mult))
            for b in range(2):
                c = slice(512 * b, 512 * b + 512)
                nc.vector.tensor_tensor(d_A[:, c], ps[(3, 6)[b]][:, :], d_E[:, c], ALU.mult).then_inc(dn_la, 1)
            ch.join()
            dve.wait_ge(dn_la, 2)
            dve.wait_ge(dn_level, 16)

            def mask_level(l):
                for b in range(2):
                    if l >= 2:
                        dve.wait_ge(dn_p, 2 * (l - 2) + b + 1)
                    c = slice(512 * b, 512 * b + 512)
                    nc.vector.tensor_tensor(r3(d_Lms[l % 2][:, c], 4), r3(d_L[:, c], 4),
                                            rep(d_level[:, l, :], 4), ALU.mult).then_inc(dn_lm, 1)

            mask_level(0)
            dve.wait_ge(dn_lm, 2)
            ch.mark(nc.vector.tensor_tensor(r3(d_TT, PAIRS), rep(ident, PAIRS), r3(d_Lms[0], PAIRS), ALU.subtract))
            mask_level(1)
            ch.join()
            for b in range(2):
                dve.wait_ge(dn_p, b + 1)
                nc.vector.tensor_tensor(r3(d_T[:, 512 * b:512 * b + 512], 4), rep(ident, 4), r3(ps[b][:, :], 4),
                                        ALU.subtract).then_inc(dn_t, 1)
            for l in range(1, LEVELS):
                if l + 1 < LEVELS:
                    mask_level(l + 1)
                for b in range(2):
                    c = slice(512 * b, 512 * b + 512)
                    dve.wait_ge(dn_y, 2 * (l - 1) + b + 1)
                    if l < LEVELS - 1:
                        nc.vector.tensor_tensor(d_T[:, c], d_T[:, c], ps[2 + b][:, :], ALU.subtract)
                    nc.vector.tensor_tensor(d_TT[:, c], d_TT[:, c], ps[6 + b][:, :], ALU.subtract)\
                        .then_inc(dn_t, 1)
                dve.wait_ge(dn_t, 2 * l + 2)
            dve.wait_ge(dn_u, 1)
            for b in range(2):
                nc.vector.tensor_copy(d_u[:, 512 * b:512 * b + 512], ps[b][:, :]).then_inc(dn_uc, 1)
            dve.wait_ge(dn_ws, 1)
            dve.wait_ge(dn_uc, 2)
            nc.vector.tensor_tensor(d_vn, d_u[:, 512:1024], ps[7][:, :], ALU.subtract).then_inc(dn_vnd, 1)
            o = dn["kt"]
            ch.mark(nc.vector.tensor_copy(o[:, 0:512], ps[3][:, :]))
            dve.wait_ge(dn_o1, 1)
            ch.mark(nc.vector.tensor_copy(o[:, 512:1024], ps[0][:, :]))
            ch.join()
            ch.link(nc.vector.tensor_tensor(d_P, o, o, ALU.mult))
            nc.vector.tensor_reduce(d_os, r3(d_P, PAIRS), AX.X, ALU.add).then_inc(dn_osum, 1)
            dve.wait_ge(dn_oroot, 1)
            ch.link(nc.vector.tensor_tensor(r3(o, PAIRS), r3(o, PAIRS), bc(d_or, P), ALU.mult))
            ch.link(nc.vector.tensor_tensor(r3(o, PAIRS), r3(o, PAIRS), rep(rowof("onorm", P), PAIRS), ALU.mult))
            wait_bank(dve, "dnz0")
            wait_bank(dve, "dnz1")
            nc.vector.tensor_tensor(o, o, d_sz, ALU.mult).then_inc(dn_out, 1)
            dve_turn(dve, "ya")
            dve_merge_branch(dve, 0)
            with dve.Fori(0, NBR - 1) as i:
                dve_merge_branch(dve, 1, i)
            for b in range(2):
                dve.wait_ge(mg_high, b + 1)
                nc.vector.tensor_tensor(ntl[:, 4 * b:4 * b + 4, :], r3(mg["m"][:, 1024 * b:1024 * b + 1024], 4),
                                        nth[:, 4 * b:4 * b + 4, :].bitcast(F32), ALU.subtract).then_inc(mg_low, 1)
            for j in range(4):
                dve_step(dve, f"out{j}")
            dve.wait_ge(mg_post, 16)
            dve_norm(dve, "post", mg["post"])
            for t in range(TT):
                dve.wait_ge(norm_scaled, TT * NORMS.index("post") + t + 1)
                nc.vector.tensor_tensor(x[:, t, :], x[:, t, :], xs[:, t, :], ALU.add).then_inc(x_ready, 1)
            dve_norm(dve, "f0")
            dve_turn(dve, "f0")
            dve_ffn(dve, 0)
            dve_norm(dve, "mx0")
            dve_turn(dve, "mx0")
            def rotate(bank, n, dst):
                cs = rep(cos_[64:96], n) if n > 1 else cos_[64:96]
                sn = rep(sin_[64:96], n) if n > 1 else sin_[64:96]
                a, b = (mrot[64:96, r, 0:n, :] if n > 1 else mrot[64:96, r, 0, :] for r in range(2))
                up, dn_ = bank[64:96, :], bank[96:128, :]
                if n > 1:
                    up, dn_ = r3(up, n), r3(dn_, n)
                ch.mark(nc.vector.tensor_tensor(a, up, cs, ALU.mult))
                ch.link(nc.vector.tensor_tensor(b, dn_, sn, ALU.mult))
                return nc.vector.tensor_tensor(dst, a, b, ALU.add)

            dve_step(dve, "mlain0")
            dve_step(dve, "mlain1")
            dve_step(dve, "mlain2")
            bank = read_bank(dve, "mlain2")
            ch.link(rotate(bank[:, S:2 * S], 1, mlc["kr"][64:96, 0:S]))
            bank_read("mlain2", nc.vector.tensor_copy(mc[:, :, 2 * CW:2 * CW + P], r3(bank[:, 0:S], TT)))
            nc.vector.tensor_copy(mk_[64:96, :, :], rep(mlc["kr"][64:96, 0:S], MLA_H)).then_inc(ml_krd, 1)
            dve.wait_ge(ml_rs, 1)
            for n, (t, c) in enumerate(MLC):
                nc.vector.tensor_scalar(mc[:, t, c], mc[:, t, c], m_rs[:, n:n + 1], None, ALU.mult).then_inc(ml_cs, 1)
            dve_turn(dve, "mlc")
            for j in range(4):
                dve_step(dve, f"uq{j}")
                for b in range(2):
                    dve.wait_ge(ml_q, 2 * j + b + 1)
                    if j + b:
                        dve.wait_ge(ml_qd, 2 * j + b)
                    h = 4 * j + 2 * b
                    rotate(ps[2 * (j % 2) + b], 2, mq[64:96, h:h + 2, :]).then_inc(ml_qd, 1)
            dve_step(dve, "uk")
            dve.wait_ge(ml_k, 1)
            for b in range(4):
                nc.vector.tensor_copy(mk_[0:64, 4 * b + 1:4 * b + 4:2, :], r3(ps[b][64:128, :], 2)).then_inc(ml_kd, 1)
            dve_step(dve, "uv")
            dve_units(dve, ch, MLA0, MLA_H, attention_evac(as3(ml["y"], TT), MLA0, MLA_V))
            dve_turn(dve, "mly")

            def add_to_x(names, stage):
                for j, name in enumerate(names):
                    dve_step(dve, name)
                    xo = x[:, :, CW * j:CW * j + CW]
                    bank_read(name, nc.vector.tensor_tensor(xo, xo, r3(read_bank(dve, name), TT), ALU.add))
                wait_bank(dve, names[-2])
                wait_bank(dve, names[-1])
                nc.vector.tensor_copy(mark_col, one_col).then_inc(x_ready, TT)

            add_to_x([f"mlao{j}" for j in range(4)], "mla")
            dve_norm(dve, "f1")
            dve_turn(dve, "f1")
            dve_ffn(dve, 1)
            dve_norm(dve, "f2")
            dve.wait_ge(ns_posed, 1)
            nc.vector.tensor_copy(n_pos[:, 0:1], ps[5][:, 0:1]).then_inc(ns_pos, 1)
            dve_turn(dve, "f2")
            dve_ffn(dve, 2)
            dve_norm(dve, "mx1")
            dve.wait_ge(ns_posed, 2)
            nc.vector.tensor_copy(n_pos[:, 1:2], ps[5][:, 1:2]).then_inc(ns_pos, 1)
            dve_turn(dve, "mx1")
            for m, name in enumerate(("nkc", "nvc")):
                dve_step(dve, name)
                src = r3(read_bank(dve, name), 2)
                dst = xx[m].rearrange("p (c two) s -> p two c s", two=2)
                for g in range(2):
                    nc.vector.tensor_copy(dst[0:64, g], src[64 * g:64 * g + 64])
                    ins = nc.vector.tensor_copy(dst[64:128, g, :, 0:S - 1], src[64 * g:64 * g + 64, :, 1:S])
                bank_read(name, ins)
            for j in range(4):
                dve_step(dve, f"nq{j}")

            def double_keys(name, dst):
                for o_, i_ in doubled(dst, read_bank(dve, name), NSA_G):
                    ins = nc.vector.tensor_copy(o_, i_)
                bank_read(name, ins)

            dve_step(dve, "nks")
            double_keys("nks", ns["ks"])
            dve_step(dve, "nvs")
            dve.wait_ge(ns_kc, 1)
            dve.wait_ge(ns_zero, 1)
            kc_ = r3(ps[2][0:64, 0:NSA_G * NCMP], NSA_G)
            nc.vector.tensor_copy(kc2[0:64, :, 0, :], kc_)
            nc.vector.tensor_copy(kc2[64:128, :, 1, :], kc_).then_inc(ns_kcd, 1)
            dve.wait_ge(ns_vc, 1)
            dve.wait_ge(ns_zero, 1)
            for r in range(NSA_R):
                ins = nc.vector.tensor_copy(vcd[32 * r:32 * r + NCMP, :, 64 * r:64 * r + 64],
                                            r3(ps[3][32 * r:32 * r + NCMP, 0:NSA_G * 64], NSA_G))
            ins.then_inc(ns_vcd, 1)
            dve_step(dve, "nkw")
            double_keys("nkw", ns["kw"])
            dve_step(dve, "nvw")
            dve_step(dve, "ng")
            dve.wait_ge(ns_cs, 1)
            dve.wait_ge(ns_bias, 16)
            dve.wait_ge(ns_zero, 2)
            got = ps[7].rearrange("p (t h n) -> p t h n", t=TT, h=NSA_H)
            for t in range(TT):
                c = slice(NSA_H * t, NSA_H * t + NSA_H)
                end = P * t + P - CMP_L
                k = min(NCMP, end // CMP_ST + 1)
                st = sc[:, t, :, 0:k]
                bias = nbias[:, :, end - CMP_ST * (k - 1):end + 1:CMP_ST][:, :, ::-1]
                ch.link(nc.vector.tensor_tensor(st, got[:, t, :, 0:k], bias, ALU.add))
                ch.link(nc.vector.tensor_reduce(n_mx[:, c], st, AX.X, ALU.max))
                nc.vector.tensor_tensor(st, st, bc(n_mx[:, c], k), ALU.subtract).then_inc(ns_cm, 1)
            wait_bank(dve, "ng")
            for t in range(TT):
                c = slice(NSA_H * t, NSA_H * t + NSA_H)
                dve.wait_ge(ns_ce, t + 1)
                k = min(NCMP, (P * t + P - CMP_L) // CMP_ST + 1)
                ch.link(nc.vector.tensor_reduce(n_sum[:, c], sc[:, t, :, 0:k], AX.X, ALU.add))
                ch.link(nc.vector.reciprocal(n_inv[:, c], n_sum[:, c]))
                ok = con[:, CON["rowok"] + t:CON["rowok"] + t + 1]
                ch.link(nc.vector.scalar_tensor_tensor(out=n_cg[:, c], in0=n_inv[:, c], scalar=ok,
                                                       in1=gate3[:, t, :, 0], op0=ALU.mult, op1=ALU.mult))
            for b in range(2):
                dve.wait_ge(ns_ct, b + 1)
                nc.vector.tensor_copy(sct[:, 512 * b:512 * b + 512], ps[b][:, :]).then_inc(ns_ctc, 1)
            for t in range(TT):
                for half in range(2):
                    n = 2 * t + half
                    dve.wait_ge(ns_co, n + 1)
                    h0 = 8 * half
                    nc.vector.tensor_tensor(
                        ny[:, t, 512 * half:512 * half + 512].rearrange("p (h d) -> p h d", h=8),
                        r3(ps[(2, 3, 6, 7)[n]], 8), bc(n_cg[:, NSA_H * t + h0:NSA_H * t + h0 + 8], 64), ALU.mult)\
                        .then_inc(ns_cy, 1)
            dve.wait_ge(ns_cy, 4)
            dve.wait_ge(ns_bias, 16)

            def nsa_evac(a, o, inv):
                h, branch = (a - NSA0) % NSA_H, 1 + (a - NSA0) // NSA_H
                ch.link(nc.vector.tensor_tensor(n_ag[a % 2], inv, gate3[:, :, h, branch], ALU.mult))
                if a - NSA0 >= NSA_H:
                    dve.wait_ge(at_read, a - NSA_H + 1)
                for t in range(TT):
                    yo = ny[:, t, 64 * h:64 * h + 64]
                    last = nc.vector.scalar_tensor_tensor(out=yo, in0=o[:, 64 * t:64 * t + 64],
                                                          scalar=n_ag[a % 2][:, t:t + 1], in1=yo, op0=ALU.mult,
                                                          op1=ALU.add)
                return last

            dve_units(dve, ch, NSA0, 2 * NSA_H, nsa_evac)
            dve_turn(dve, "nsy")
            add_to_x([f"nsao{j}" for j in range(4)], "nsa")
            dve_norm(dve, "f3")
            dve_turn(dve, "f3")
            dve_ffn(dve, 3)
            dve.wait_ge(mg_post, 32)
            dve_norm(dve, "final", scr[:, 4096:4096 + D])

        @block.tensor
        def _(pe):
            pe.wait_ge(con_here, 32)
            pe_norm(pe, "mem")
            pe_plain(pe, "mk0", "F", "mem")
            pe_plain(pe, "mk1", "F")
            pe_plain(pe, "mv0", "T")
            pe_plain(pe, "mv1", "T")
            pe_norm(pe, "pre")
            pe_plain(pe, "xmq0", "F", "pre")
            for name, kind in (("xmq1", "F"), ("xmz0", "T"), ("xmz1", "T")):
                pe_plain(pe, name, kind)
            for name in ("mk0", "mk1", "mv0", "mv1", "xmq0", "xmq1"):
                wait_bank(pe, name)
            pe_units(pe, XM0, XM_H)
            pe.wait_ge(at_read, XM0 + XM_H)
            pe_turn(pe, "ym")
            for name, kind in (("swq0", "F"), ("swq1", "F"), ("swkv", "FT"), ("swz0", "T"), ("swz1", "T")):
                pe_plain(pe, name, kind)
            for name in ("swq0", "swq1", "swkv"):
                wait_bank(pe, name)
            pe.wait_ge(turn_low, turn_done("ym"))
            pe_units(pe, SW0, SW_H)
            pe.wait_ge(at_read, SW0 + SW_H)
            pe_turn(pe, "yc")
            for name, kind in (("gmu0", "F"), ("gmu1", "F"), ("gmz0", "F"), ("gmz1", "F"), ("gmv0", "T"),
                               ("gmv1", "T")):
                pe_plain(pe, name, kind)
            pe.wait_ge(gm_loaded, 16)
            pe.wait_ge(turn_low, turn_done("yc"))
            for g in range(4):
                last = nc.tensor.transpose(pair(ps[0], g), pair(gm["w"], g), ident)
            last.then_inc(gm_wturned, 1)
            pe.wait_ge(gm_wmask, 1)
            pe.wait_ge(gm_vn, TT)
            for g in range(4):
                for t in range(TT):
                    at = 256 * (g % 2) + P * t
                    last = nc.tensor.matmul(ps[1 + g // 2][:, at:at + P], gm["v"][:, 512 * t + P * g:512 * t + P * g + P],
                                            pair(gm["wt"], g), start=True, stop=True)
            last.then_inc(gm_mixed, 1)
            pe_plain(pe, "ba", 8)
            for j in range(6):
                pe_plain(pe, f"dn{j}", "F")
            pe_plain(pe, "dnz0", "T")
            pe_plain(pe, "dnz1", "T")
            pe.wait_ge(gm_low, 1)
            for j in range(6):
                pe.wait_ge(dn_act, j + 1)
                if j >= 4:
                    pe.wait_ge(dn_tok, j - 3)
                for t in range(TT):
                    for c in range(2):
                        at = 256 * t + P * c
                        last = nc.tensor.transpose(ps[j % 4][:, at:at + P], cact[:, 2 * j + c, P * t:P * t + P], ident)
                last.then_inc(dn_turn, 1)
            pe.wait_ge(dn_g, 1)
            wait_bank(pe, "dnz0")
            wait_bank(pe, "dnz1")
            pe.wait_ge(dn_tok, 6)
            nc.tensor.matmul(ps[4][:, 0:8], upto, d_g, start=True, stop=True)
            nc.tensor.matmul(ps[4][:, 8:16], ones, d_g, start=True, stop=True)
            for n in range(PAIRS):
                last = nc.tensor.matmul(pair(ps[1 + n // 4], n % 4), pair(d_Lm, n), upto, start=True, stop=True)
            last.then_inc(dn_gcs, 1)
            pe.wait_ge(dn_ready, 1)
            for n, (src, _, b) in enumerate(DN_TURNS):
                if n == 1:
                    pe.wait_ge(dn_diff, PAIRS)
                if n == 6:
                    pe.wait_ge(dn_fa, 1)
                for h in range(DN_H):
                    last = nc.tensor.transpose(pair(ps[b], h), src[h], ident)
                last.then_inc(dn_fm, 1)
            pe.wait_ge(dn_fa, 4)
            pe.wait_ge(dn_fd, 3)
            for rhs, banks in ((d_kbt, (1, 2)), (dn["qt"], (3, 6))):
                for n in range(PAIRS):
                    last = nc.tensor.matmul(pair(ps[banks[n // 4]], n % 4), pair(dn["kt"], n), pair(rhs, n),
                                            start=True, stop=True)
                last.then_inc(dn_kk, 1)
            pe.wait_ge(dn_la, 2)
            for l in range(LEVELS):
                for b in range(2):
                    pe.wait_ge(dn_lm, 2 * l + b + 1)
                    if l:
                        pe.wait_ge(dn_t, 2 * l + b - 1)
                    for n in range(4 * b, 4 * b + 4):
                        last = nc.tensor.matmul(pair(ps[b], n % 4), pair(d_Lms[l % 2], n),
                                                pair(d_T, n) if l else ident, start=True, stop=True)
                    last.then_inc(dn_p, 1)
                if l == 0:
                    continue
                for b in range(2):
                    pe.wait_ge(dn_pc, 2 * l + b - 1)
                    for n in range(4 * b, 4 * b + 4):
                        last = nc.tensor.matmul(pair(ps[6 + b], n % 4), pair(d_P, n), pair(d_TT, n), start=True,
                                                stop=True)
                    if l < LEVELS - 1:
                        for n in range(4 * b, 4 * b + 4):
                            last = nc.tensor.matmul(pair(ps[2 + b], n % 4), pair(d_TT, n), pair(d_P, n),
                                                    start=True, stop=True)
                    last.then_inc(dn_y, 1)
            pe.wait_ge(dn_t, 2 * LEVELS)
            for n in range(PAIRS):
                last = nc.tensor.matmul(pair(ps[n // 4], n % 4), pair(d_TT, n), tok[:, n // 4, 8 + n % 4, :],
                                        start=True, stop=True)
            last.then_inc(dn_u, 1)
            for h in range(DN_H):
                last = nc.tensor.matmul(pair(ps[2], h), pair(dn["rw"], h), pair(d_TT, 4 + h), start=True, stop=True)
            last.then_inc(dn_u, 1)
            pe.wait_ge(dn_uc, 1)
            for h in range(DN_H):
                last = nc.tensor.matmul(pair(ps[3], h), pair(d_A, h), pair(d_u, h), start=True, stop=True)
            last.then_inc(dn_o0, 1)
            for h in range(DN_H):
                last = nc.tensor.matmul(pair(ps[6], h), pair(dn["kd"], h), pair(d_u, h), start=True, stop=True)
            last.then_inc(dn_o0, 1)
            pe.wait_ge(dn_sc, 1)
            pe.wait_ge(dn_wc, 1)
            for h in range(DN_H):
                last = nc.tensor.matmul(pair(ps[7], h), pair(d_wt, h), pair(d_S, h), start=True, stop=True)
            last.then_inc(dn_ws, 1)
            pe.wait_ge(dn_vnd, 1)
            for h in range(DN_H):
                nc.tensor.matmul(pair(ps[0], h), pair(dn["qgt"], h), pair(d_S, h), start=True, stop=False,
                                 skip_group_check=True)
                last = nc.tensor.matmul(pair(ps[0], h), pair(d_A, 4 + h), pair(d_vn, h), start=False, stop=True,
                                        skip_group_check=True)
            last.then_inc(dn_o1, 1)
            pe.wait_ge(dn_out, 1)
            pe_turn(pe, "ya")
            pe.wait_ge(turn_low, turn_done("ya"))
            pe_merge_branch(pe, 0)
            with pe.Fori(0, NBR - 1) as i:
                pe_merge_branch(pe, 1, i)
            pe.wait_ge(mg_low, 2)
            pe.wait_ge(mg_sig, 4 * NBR)
            for j in range(4):
                pe_plain(pe, f"out{j}", "T")
            pe_norm(pe, "f0")
            pe_ffn(pe, 0)
            pe_norm(pe, "mx0")
            pe_plain(pe, "mlain0", "T", "mx0")
            pe_plain(pe, "mlain1", "T")
            pe_plain(pe, "mlain2", "TF")
            pe.wait_ge(ml_cs, 4)
            pe_turn(pe, "mlc")
            pe.wait_ge(turn_low, turn_done("mlc"))
            for j in range(4):
                t = TILE[f"uq{j}"]
                weights_here(pe, t)
                for b in range(2):
                    if j >= 2:
                        pe.wait_ge(ml_qa, 2 * (j - 2) + b + 1)
                        pe.wait_ge(ml_qd, 2 * (j - 2) + b + 1)
                    for c in range(2):
                        last = by_feature(ps[2 * (j % 2) + b][:, S * c:S * c + S], slot(t, 3, 512), P * (2 * b + c),
                                          NT_, 3)
                    last.then_inc(ml_q, 1)
                nc.tensor.matmul(ps[6][:, 0:2], ident, power[:, 0:2], start=True, stop=True).then_inc(w_used, 1)
            t = TILE["uk"]
            weights_here(pe, t)
            pe.wait_ge(ml_qa, 8)
            pe.wait_ge(ml_qd, 8)
            for c in range(8):
                last = by_feature(ps[c // 2][:, S * (c % 2):S * (c % 2) + S], slot(t, 2, D), P * c, NT_, 2, 3)
            last.then_inc(ml_k, 1)
            nc.tensor.matmul(ps[6][:, 0:2], ident, power[:, 0:2], start=True, stop=True).then_inc(w_used, 1)
            t = TILE["uv"]
            weights_here(pe, t)
            for n in range(4):
                last = by_token(ps[4 + n][:, :], slot(t, 2, D), 512 * (n % 2), 512, NT_, 2, n // 2, 3)
            last.then_inc(ml_v, 1)
            pe.wait_ge(ml_va, 4)
            nc.tensor.matmul(ps[6][:, 0:2], ident, power[:, 0:2], start=True, stop=True).then_inc(w_used, 1)
            pe.wait_ge(ml_ka, 4)
            pe.wait_ge(ml_kd, 4)
            pe.wait_ge(ml_krd, 1)
            pe_units(pe, MLA0, MLA_H)
            pe.wait_ge(at_read, MLA0 + MLA_H)
            pe_turn(pe, "mly")
            for j in range(4):
                pe_plain(pe, f"mlao{j}", "T", None if j else "mly")
            pe_norm(pe, "f1")
            pe_ffn(pe, 1)
            def position_part(m):
                for j in range(CMP_L // 2):
                    last = nc.tensor.matmul(ps[5][:, m:m + 1], w1s[:, m, j, :], poss[:, m, j:j + 1], start=j == 0,
                                            stop=j == CMP_L // 2 - 1)
                last.then_inc(ns_posed, 1)

            pe.wait_ge(ns_tbl, 32)
            pe.wait_ge(ns_w1, 48)
            tbl = nt_["tbl"][0:BIAS_ROWS, 0:NSA_H]
            nc.tensor.matmul(ps[6][0:NSA_H, :], tbl, nt_["hot"][0:BIAS_ROWS, :], start=True, stop=True)\
                .then_inc(ns_line, 1)
            pe.wait_ge(ff_h, 2 * FT)
            position_part(0)
            pe_norm(pe, "f2")
            pe.wait_ge(ns_pos, 1)
            pe_ffn(pe, 2)
            pe.wait_ge(ff_h, 3 * FT)
            position_part(1)
            pe_norm(pe, "mx1")
            pe.wait_ge(ns_pos, 2)
            pe_plain(pe, "nkc", "F", "mx1")
            for name in ("nvc", "nq0", "nq1", "nq2", "nq3"):
                pe_plain(pe, name, "F")
            wait_bank(pe, "nkc")
            wait_bank(pe, "nvc")
            for m in range(2):
                for j in range(CMP_L // 2):
                    blocks = xx[m][:, :, 2 * j:2 * j + CMP_ST * (NCMP - 1) + 1:CMP_ST]
                    last = nc.tensor.matmul(ps[1][:, 64 * m:64 * m + NSA_G * NCMP], w1s[:, m, j, :], blocks,
                                            start=j == 0, stop=j == CMP_L // 2 - 1)
            last.then_inc(ns_hid, 1)
            pe_plain(pe, "nks", "F")
            pe.wait_ge(ns_hc, 2)
            nc.tensor.matmul(ps[2][0:64, 0:NSA_G * NCMP], w2s[:, 0, :], n_hid[0][:, 0:NSA_G * NCMP], start=True,
                             stop=True).then_inc(ns_kc, 1)
            for r in range(NSA_R):
                for g in range(NSA_G):
                    last = nc.tensor.matmul(ps[3][32 * r:32 * r + NCMP, 64 * g:64 * g + 64],
                                            n_hid[1][:, NCMP * g:NCMP * g + NCMP], w2s[:, 1, :], start=True, stop=True)
            last.then_inc(ns_vc, 1)
            pe_plain(pe, "nvs", "T")
            pe.wait_ge(ns_kcd, 1)
            pe.wait_ge(ns_linec, 1)
            for name in ("nq2", "nq3"):
                wait_bank(pe, name)
            for t in range(TT):
                for c in range(NSA_H // 2):
                    at = 256 * t + 32 * c
                    last = nc.tensor.matmul(r3(ps[7][:, at:at + 32], 2)[:, :, 0:NCMP],
                                            ns["q"][:, S * c + P * t:S * c + P * t + P],
                                            kc2[:, c // (NSA_R // 2)], start=True, stop=True)
            last.then_inc(ns_cs, 1)
            pe_plain(pe, "nkw", "F")
            pe_plain(pe, "nvw", "T")
            pe_plain(pe, "ng", 48)
            for t in range(TT):
                pe.wait_ge(ns_ce, t + 1)
                if t == 0:
                    pe.wait_ge(ns_pos, 1)
                for g in range(NSA_G):
                    last = nc.tensor.transpose(pair(ps[t], g), xs[:, 0, 512 * t + P * g:512 * t + P * g + P], ident)
                last.then_inc(ns_ct, 1)
            pe.wait_ge(ns_vcd, 1)
            for t in range(TT):
                pe.wait_ge(ns_ctc, t + 1)
                for half in range(2):
                    for gg in range(2):
                        g = 2 * half + gg
                        last = nc.tensor.matmul(ps[(2, 3, 6, 7)[2 * t + half]][:, 256 * gg:256 * gg + 256],
                                                sct[:, 512 * t + P * g:512 * t + P * g + P], vcd[:, g, :], start=True,
                                                stop=True)
                    last.then_inc(ns_co, 1)
            for name in ("nks", "nvs", "nkw", "nvw"):
                wait_bank(pe, name)
            pe.wait_ge(ns_cy, 4)
            pe_units(pe, NSA0, 2 * NSA_H)
            pe.wait_ge(at_read, NSA0 + 2 * NSA_H)
            pe_turn(pe, "nsy")
            for j in range(4):
                pe_plain(pe, f"nsao{j}", "T", None if j else "nsy")
            pe_norm(pe, "f3")
            pe_ffn(pe, 3)


def kernel(**inputs):
    import concourse.bacc as bacc
    from concourse.bass_utils import run_bass_kernel_spmd as run

    arrays = lay_out({k: np.asarray(v) for k, v in inputs.items()})
    nc = bacc.Bacc("TRN2", target_bir_lowering=False, num_devices=1)
    A = {k: nc.dram_tensor(f"in_{k}", v.shape, F32, kind="ExternalInput").ap() for k, v in arrays.items()}
    out = nc.dram_tensor("out", (P, TT, D), F32, kind="ExternalOutput").ap()
    build(nc, A, out)
    r = run(nc, [{f"in_{k}": v for k, v in arrays.items()}], core_ids=[0])
    y = r.results[0]["out"]
    return np.ascontiguousarray(np.asarray(y).transpose(1, 0, 2)).reshape(1, S, D)
```

```python
import numpy as np
from contextlib import ExitStack

import concourse.bass as bass
from concourse import mybir

F32 = mybir.dt.float32
F32R = mybir.dt.float32r
ALU = mybir.AluOpType
ACT = mybir.ActivationFunctionType
AX = mybir.AxisListType

P = 128
S = 256
TT = S // P
D = 1024
KC = D // P
TW = 2048
CW = TW // KC
SLOTS = 3
EPS = 1e-6
NEG = -1e30
FFN = 2816
FT = FFN // CW
BW = 512
NBR = 4
DN_H = 4
SW_H, SW_KV, SW_D, SW_WIN = 8, 2, 64, 128
XM_H = 4
MLA_H, MLA_QL, MLA_KVL, MLA_N, MLA_R, MLA_V = 16, 384, 256, 64, 32, 64
NSA_H, NSA_G, NSA_D = 16, 4, 64
NSA_R = NSA_H // NSA_G
CMP_L, CMP_ST = 32, 16
NCMP = (S - CMP_L) // CMP_ST + 1
BUCKETS = 32
PAIRS = TT * DN_H


def plan():
    t = ["mk0", "mk1", "mv0", "mv1"]
    t += ["xmq0", "xmq1", "xmz0", "xmz1"]
    t += ["swq0", "swq1", "swkv", "swz0", "swz1"]
    t += ["gmv0", "gmv1", "gmu0", "gmu1", "gmz0", "gmz1"]
    t += ["ba"] + [f"dn{j}" for j in range(6)] + ["dnz0", "dnz1"]
    for n in range(NBR):
        for half in range(2):
            t += [f"gate{n}{half}0", f"gate{n}{half}1", f"up{n}{half}"]
    t += [f"out{j}" for j in range(4)]
    t += ffn_names(0)
    t += ["mlain2", "mlain0", "mlain1"] + [f"uq{j}" for j in range(4)] + ["uk", "uv"]
    t += [f"mlao{j}" for j in range(4)]
    t += ffn_names(1) + ffn_names(2)
    t += ["nkc", "nvc", "nq0", "ng", "nq1", "nq2", "nq3", "nks", "nvs", "nkw", "nvw"]
    t += [f"nsao{j}" for j in range(4)]
    t += ffn_names(3)
    return t + ["pad"]


def ffn_names(f):
    t = [f"f{f}g0", f"f{f}u0"]
    for i in range(1, FT):
        t += [f"f{f}g{i}", f"f{f}u{i}", f"f{f}d{i - 1}"]
    return t + [f"f{f}d{FT - 1}"]


PLAN = plan()
USED = {"ba": KC * P, "ng": KC * P, "uq0": 1536, "uq1": 1536, "uq2": 1536, "uq3": 1536}
TILE = {n: i for i, n in enumerate(PLAN)}
NT = len(PLAN)
PLAIN = [n for n in PLAN if n[0] not in "fu" and n[:4] != "gate" and n != "pad"]
UNIT = {n: i for i, n in enumerate(PLAIN)}

VEC = {}
_at = 0
for _n, _w in (("pre", 8), ("mem", 8), ("fa0", 8), ("fa1", 8), ("mx0", 8), ("mx1", 8), ("fb0", 8),
               ("fb1", 8), ("qn", 3), ("kvn", 2), ("conv", 48)):
    VEC[_n] = _at
    _at += _w
NVEC = _at
ROW = {}
_at = 0
for _n, _w in (("onorm", 128), ("gmn", 512), ("bs", 512), ("dtb", 8), ("alog", 8), ("sink", 8)):
    ROW[_n] = _at
    _at += _w
NROW = _at
LEVELS = 7
CON = {}
_at = 0
for _n, _w in (("ident", 128), ("upto", 128), ("before", 128), ("ones", 128), ("causal", 256),
               ("window", 256), ("rowok", 2), ("rope", 256)):
    CON[_n] = _at
    _at += _w
NCON = _at


def constants():
    j = np.arange(P)[:, None]
    i = np.arange(P)[None, :]
    con = np.zeros((P, NCON), np.float32)

    def put(name, a):
        con[:, CON[name]:CON[name] + a.shape[1]] = a

    put("ident", (i == j) * 1.0)
    put("upto", (j <= i) * 1.0)
    put("before", (j < i) * 1.0)
    put("ones", np.ones((P, P)))
    dist = P + j - np.arange(2 * P)[None, :]
    put("causal", np.where(dist >= 0, 0.0, NEG))
    put("window", np.where((dist >= 0) & (dist < SW_WIN), 0.0, NEG))
    put("rowok", (j + P * np.arange(TT)[None, :] >= CMP_L - 1) * 1.0)
    half = MLA_R // 2
    inv = np.float32(10000.0) ** (-np.arange(half, dtype=np.float32) * np.float32(2.0) / MLA_R)
    ang = np.arange(S, dtype=np.float32)[None, :] * inv[:, None].astype(np.float32)
    rope = np.zeros((P, S), np.float32)
    rope[64:96] = np.tile(np.cos(ang), (2, 1))
    rope[96:112], rope[112:128] = -np.sin(ang), np.sin(ang)
    put("rope", rope)
    level = np.zeros((P, LEVELS, P), np.float32)
    for n in range(LEVELS):
        s = 1 << n
        level[:, n] = (j // (2 * s) == i // (2 * s)) & (i % (2 * s) >= s) & (j % (2 * s) < s)
    dist = np.arange(2 * S) - S
    n = np.maximum(dist, 0)
    exact = BUCKETS // 2
    large = exact + (np.log(np.maximum(n, 1).astype(np.float32) / exact) / np.float32(np.log(128 / exact))
                     * (BUCKETS - exact)).astype(np.int32)
    bucket = np.where(n < exact, n, np.minimum(large, BUCKETS - 1))
    hot = np.zeros((BUCKETS + 1, 2 * S), np.float32)
    hot[bucket, np.arange(2 * S)] = 1.0
    hot[BUCKETS] = dist < 0
    return con, level.reshape(P, LEVELS * P), hot


def lay_out(a):
    def cols(w, c0, n=CW):
        k = w.shape[0] // P
        return w[:, c0:c0 + n].reshape(k, P, n).transpose(1, 0, 2).reshape(P, k * n)

    def narrow(w, c0, n):
        return cols(np.concatenate([w[:, c0:c0 + n], np.zeros((D, P - n), np.float32)], axis=1), 0, P)

    w_in = a["w_in"][0]
    mkv = a["w_mem_kv"][0]
    win_m, wuq, wukv = a["mla_w_in_2"][0], a["mla_w_uq_2"][0], a["mla_w_ukv_2"][0]
    win_n = a["nsa_w_in_2"][0]
    o_qkv, o_z, o_b = 0, 1536, 2048
    o_uv = o_b + 2 * DN_H
    o_gz = o_uv + 1024
    o_sq = o_gz + 512
    o_sk = o_sq + 512
    o_sz = o_sk + 256
    o_xq = o_sz + 512
    o_xz = o_xq + 512
    o_g = o_xz + 512
    stream = np.zeros((NT, P, TW), np.float32)

    def put(name, t):
        stream[TILE[name], :, :t.shape[1]] = t

    for j in range(2):
        put(f"mk{j}", cols(mkv, CW * j))
        put(f"mv{j}", cols(mkv, BW + CW * j))
        for name, o in (("xmq", o_xq), ("xmz", o_xz), ("swq", o_sq), ("swz", o_sz), ("gmu", o_uv),
                        ("gmv", o_uv + BW), ("gmz", o_gz), ("dnz", o_z)):
            put(f"{name}{j}", cols(w_in, o + CW * j))
    put("swkv", cols(w_in, o_sk))
    put("ba", narrow(w_in, o_b, 2 * DN_H))
    for j in range(6):
        put(f"dn{j}", cols(w_in, o_qkv + CW * j))
    for n in range(NBR):
        for h in range(2):
            for g in range(2):
                put(f"gate{n}{h}{g}", cols(w_in, o_g + D * n + 512 * h + CW * g))
            put(f"up{n}{h}", cols(a["w_up"][0, n], 512 * h, 512))
    for j in range(4):
        put(f"out{j}", cols(a["w_out"][0], CW * j))
        put(f"mlao{j}", cols(a["mla_w_o_2"][0], CW * j))
        put(f"nsao{j}", cols(a["nsa_w_o_2"][0], CW * j))
        put(f"nq{j}", cols(win_n, CW * j))
    for f in range(4):
        ab, l = "ab"[f % 2], f // 2
        g, u, d = (a[f"ffn_{ab}_w_{x}_2"][l] for x in ("gate", "up", "down"))
        for i in range(FT):
            put(f"f{f}g{i}", cols(g, CW * i))
            put(f"f{f}u{i}", cols(u, CW * i))
            put(f"f{f}d{i}", cols(d[CW * i:CW * (i + 1)], 0, D))
    put("mlain0", cols(win_m, 0))
    put("mlain1", cols(win_m, CW))
    rope = win_m[:, 640:672]
    last = np.concatenate([win_m[:, 512:640], np.zeros((D, 64), np.float32), rope, rope[:, 16:],
                           rope[:, :16]], axis=1)
    put("mlain2", cols(last, 0))
    q = wuq.reshape(MLA_QL, MLA_H, MLA_N + MLA_R)
    q = np.concatenate([q, q[:, :, 80:96], q[:, :, 64:80]], axis=2).reshape(MLA_QL, MLA_H * P)
    for j in range(4):
        put(f"uq{j}", cols(q, 512 * j, 512))
    kv = wukv.reshape(MLA_KVL, MLA_H, 2, 64)
    put("uk", cols(np.ascontiguousarray(kv[:, :, 0]).reshape(MLA_KVL, D), 0, D))
    put("uv", cols(np.ascontiguousarray(kv[:, :, 1]).reshape(MLA_KVL, D), 0, D))
    for n, name in enumerate(("nkc", "nvc", "nks", "nvs", "nkw", "nvw")):
        put(name, cols(win_n, D + CW * n))
    put("ng", narrow(win_n, 2560, 3 * NSA_H))

    vec = np.zeros((P, NVEC), np.float32)
    for name, v in (("pre", a["norm_pre"][0]), ("mem", a["norm_mem"][0]), ("fa0", a["ffn_norm_a_2"][0]),
                    ("fa1", a["ffn_norm_a_2"][1]), ("mx0", a["mix_norm_2"][0]), ("mx1", a["mix_norm_2"][1]),
                    ("fb0", a["ffn_norm_b_2"][0]), ("fb1", a["ffn_norm_b_2"][1]),
                    ("qn", a["mla_q_norm_2"][0]), ("kvn", a["mla_kv_norm_2"][0]),
                    ("conv", a["conv_w"][0])):
        v = v.reshape(-1, P).T
        vec[:, VEC[name]:VEC[name] + v.shape[1]] = v
    row = np.zeros((P, NROW), np.float32)
    for name, v in (("onorm", a["dn_norm"][0]), ("gmn", a["gm_norm"][0]), ("bs", a["spatial_b"][0].reshape(-1)),
                    ("dtb", np.tile(a["dt_bias"][0], TT)), ("alog", np.tile(a["a_log"][0], TT)),
                    ("sink", a["sinks"][0])):
        row[:, ROW[name]:ROW[name] + v.shape[0]] = v[None, :]
    con, level, hot = constants()
    tok = lambda v: v[0].reshape(TT, P, D).transpose(1, 0, 2)
    blk = lambda w: w[0].reshape(CMP_L // 2, P, P).transpose(1, 0, 2).reshape(P, TW)
    pos = lambda p: p[0].reshape(CMP_L // 2, P).T
    tbl = np.full((BUCKETS + 1, NSA_H), NEG, np.float32)
    tbl[:BUCKETS] = a["rel_bias_2"]
    arrays = {
        "stream": stream, "x": tok(a["x"]), "mem": tok(a["mem"]), "vec": vec, "row": row, "con": con,
        "level": level, "hot": hot,
        "spatial": a["spatial_w"][0].transpose(1, 0, 2), "bucket_bias": tbl,
        "post": np.broadcast_to(a["norm_post"][0], (P, D)),
        "final": np.broadcast_to(a["final_norm_2"], (P, D)),
        "w1": np.stack([blk(a["nsa_cmp_w1_k_2"]), blk(a["nsa_cmp_w1_v_2"])], axis=1),
        "w2": np.stack([a["nsa_cmp_w2_k_2"][0], a["nsa_cmp_w2_v_2"][0]], axis=1),
        "pos": np.stack([pos(a["nsa_cmp_pos_k_2"]), pos(a["nsa_cmp_pos_v_2"])], axis=1),
    }
    return {k: np.ascontiguousarray(v, dtype=np.float32) for k, v in arrays.items()}


def build(nc, A, out):
    ctx = ExitStack()
    with ctx:
        def sb(name, shape, dt=F32):
            return ctx.enter_context(nc.sbuf_tensor(name, shape, dt))

        def sem(name):
            return ctx.enter_context(nc.semaphore(name))

        raw = [sb(f"raw{i}", [P, TW]) for i in range(SLOTS)]
        high = [sb(f"high{i}", [P, TW], F32R) for i in range(SLOTS)]
        low = [sb(f"low{i}", [P, TW], F32R) for i in range(SLOTS)]
        x = sb("x", [P, TT, D])
        xs = sb("xs", [P, TT, D])
        nth = sb("nth", [P, KC, S], F32R)
        ntl = sb("ntl", [P, KC, S], F32R)
        vec = sb("vec", [P, NVEC])
        row = sb("row", [P, NROW])
        con = sb("con", [P, NCON])
        small = sb("small", [P, 1000])
        SCR = 14336
        scr = sb("scr", [P, SCR])
        with nc.sbuf_tensor("yth", [P, NBR, 4, S], F32R) as yth, \
                nc.sbuf_tensor("ytl", [P, NBR, 4, S], F32R) as ytl:
            pass
        hth = sb("hth", [P, 2, S], F32R)
        htl = sb("htl", [P, 2, S], F32R)
        late = sb("late", [P, 7168])
        ps = [ctx.enter_context(nc.psum_tensor(f"ps{i}", [P, 512], F32)) for i in range(8)]
        line = nc.dram_tensor("bias_by_distance", (NSA_H, 2 * S), F32).ap()

        def carve(memory, sizes, base=0):
            got, at = {}, base
            for name, size in sizes:
                got[name] = memory[:, at:at + size]
                at += size
            assert at <= memory.shape[1], (at, sizes)
            return got

        def c_(name, w):
            return con[:, CON[name]:CON[name] + w]

        ident, upto, before, ones = (c_(n, P) for n in ("ident", "upto", "before", "ones"))
        causal, window = c_("causal", 256), c_("window", 256)
        used_small = [0]

        def tiny(w):
            used_small[0] += w
            assert used_small[0] <= 1000
            return small[:, used_small[0] - w:used_small[0]]

        def r3(ap, a):
            return ap.rearrange("p (a b) -> p a b", a=a)

        def vcol(name, c):
            return vec[:, VEC[name] + c:VEC[name] + c + 1]

        def rowof(name, w):
            return row[:, ROW[name]:ROW[name] + w]

        at_buf = carve(scr, [("s", 1024), ("p", 1024)])
        at_s = [at_buf["s"][:, 0:512], at_buf["s"][:, 512:1024], xs[:, 0, 0:512]]
        at_p = [at_buf["p"][:, 512 * i:512 * i + 512] for i in range(2)]
        xm = carve(scr, [("k", 1024), ("v", 1024), ("q", 1024), ("z", 1024), ("y", 1024)], 2048)
        sw = carve(scr, [("q", 1024), ("k", 1024), ("v", 256), ("z", 1024), ("y", 1024)], 7168)
        gm = carve(scr, [("u", 1024), ("z", 1024), ("v", 1024), ("w", 512), ("wt", 512), ("sq", 1024)], 2048)
        dn = carve(scr, [("cin", 3108), ("cact", 3072), ("tok", 3072), ("kb", 1024), ("rw", 512),
                         ("kt", 1024), ("qt", 1024), ("qgt", 512), ("kd", 512)])
        mg = carve(scr, [("sg", 2048), ("prod", 2048), ("m", 2048), ("o", 2048), ("post", 1024)])
        ff = carve(scr, [("sg", 512), ("h", 512)])
        ml = carve(scr, [("buf", 2048), ("q", 4096), ("k", 4096), ("v", 2048), ("y", 2048)])
        mlc = carve(late, [("c", 1280), ("rot", 512), ("kr", 512)])
        ns = carve(scr, [("buf", 2048), ("q", 2048), ("ks", 2048), ("vs", 512), ("vw", 512), ("xk", 1024),
                         ("xv", 1024), ("bias", 4096)])
        ns_xk_at = 2048 + 2048 + 2048 + 512 + 512
        ns["kw"] = scr[:, ns_xk_at:ns_xk_at + 2048]
        nl = carve(late, [("w1", 4096), ("y", 2048), ("vc", 1024)])
        nt_ = carve(late, [("hot", 512), ("tbl", 16), ("line", 512)], 4096)

        sems = {}

        def s_(name):
            if name not in sems:
                sems[name] = ctx.enter_context(nc.semaphore(name))
            return sems[name]

        raw_here = [s_(f"raw_here{i}") for i in range(SLOTS)]
        w_high, w_low, w_used = s_("w_high"), s_("w_low"), s_("w_used")
        bank_done = [s_("bank_done0"), s_("bank_done1")]

        def val(base, i):
            return base if i is None else i[0] * i[1] + base

        def by(i, step):
            return None if i is None else (i, step)

        def split_high(act, t, i=None):
            act.wait_ge(raw_here[t % SLOTS], val(16 * (t // SLOTS + 1), by(i, 16)))
            if t >= SLOTS:
                act.wait_ge(w_used, val(t - SLOTS + 1, by(i, SLOTS)))
            n = TW if i is not None else USED.get(PLAN[t], TW)
            nc.scalar.activation(high[t % SLOTS][:, 0:n], raw[t % SLOTS][:, 0:n], ACT.Copy).then_inc(w_high, 1)

        def split_low(dve, t, i=None):
            dve.wait_ge(w_high, val(t + 1, by(i, SLOTS)))
            n = TW if i is not None else USED.get(PLAN[t], TW)
            nc.vector.tensor_tensor(low[t % SLOTS][:, 0:n], raw[t % SLOTS][:, 0:n],
                                    high[t % SLOTS][:, 0:n].bitcast(F32), ALU.subtract).then_inc(w_low, 1)

        def plain_free(name):
            return UNIT[name] // 2

        def bank_of(name):
            return 4 + UNIT[name] % 2

        class Chain:

            def __init__(self, eng, name):
                self.eng, self.sem, self.n = eng, s_(name), 0

            def mark(self, ins):
                ins.then_inc(self.sem, 1)
                self.n += 1

            def link(self, ins):
                self.mark(ins)
                self.eng.wait_ge(self.sem, self.n)

            def join(self):
                self.eng.wait_ge(self.sem, self.n)

        as3 = lambda ap, n: ap.rearrange("p (t c) -> p t c", t=n)
        TURNS = {
            "mem": (xs, 8, "mem", nth, ntl), "pre": (xs, 8, "pre", nth, ntl),
            "ym": (as3(xm["y"], TT), 4, None, yth[:, 3], ytl[:, 3]),
            "yc": (as3(sw["y"], TT), 4, None, yth[:, 2], ytl[:, 2]),
            "ya": (as3(dn["kt"], TT), 4, None, yth[:, 0], ytl[:, 0]),
            "f0": (xs, 8, "fa0", nth, ntl), "mx0": (xs, 8, "mx0", nth, ntl),
            "mlc": (as3(mlc["c"], TT), 5, "qn", nth, ntl),
            "mly": (as3(ml["y"], TT), 8, None, nth, ntl),
            "f1": (xs, 8, "fb0", nth, ntl), "f2": (xs, 8, "fa1", nth, ntl),
            "mx1": (xs, 8, "mx1", nth, ntl), "nsy": (as3(nl["y"], TT), 8, None, nth, ntl),
            "f3": (xs, 8, "fb1", nth, ntl),
        }
        turn_at, n_ = {}, 0
        for name, spec in TURNS.items():
            turn_at[name] = n_
            n_ += (spec[1] + 1) // 2
        turned, turn_high, turn_low = s_("turned"), s_("turn_high"), s_("turn_low")

        def turn_banks(name):
            n = TURNS[name][1]
            return [(b, turn_at[name] + b + 1, range(2 * b, min(2 * b + 2, n))) for b in range((n + 1) // 2)]

        def pe_turn(pe, name, waits={}):
            src = TURNS[name][0]
            for b, count, chunks in turn_banks(name):
                if b in waits:
                    pe.wait_ge(*waits[b])
                for c in chunks:
                    for t in range(TT):
                        at = 256 * (c - 2 * b) + P * t
                        last = nc.tensor.transpose(ps[b][:, at:at + P], src[:, t, P * c:P * c + P], ident)
                last.then_inc(turned, 1)

        def act_turn(act, name):
            _, _, gain, high_, _ = TURNS[name]
            for b, count, chunks in turn_banks(name):
                act.wait_ge(turned, count)
                if gain is None:
                    n = len(chunks)
                    last = nc.scalar.activation(high_[:, 2 * b:2 * b + n, :], r3(ps[b][:, 0:256 * n], n), ACT.Copy)
                else:
                    for c in chunks:
                        at = 256 * (c - 2 * b)
                        last = nc.scalar.activation(high_[:, c, :], ps[b][:, at:at + 256], ACT.Copy,
                                                    scale=vcol(gain, c))
                last.then_inc(turn_high, 1)

        def dve_turn(dve, name):
            _, _, gain, high_, low_ = TURNS[name]
            for b, count, chunks in turn_banks(name):
                dve.wait_ge(turn_high, count)
                if gain is None:
                    n = len(chunks)
                    last = nc.vector.tensor_tensor(low_[:, 2 * b:2 * b + n, :], r3(ps[b][:, 0:256 * n], n),
                                                   high_[:, 2 * b:2 * b + n, :].bitcast(F32), ALU.subtract)
                else:
                    for c in chunks:
                        at = 256 * (c - 2 * b)
                        last = nc.vector.scalar_tensor_tensor(
                            out=low_[:, c, :], in0=ps[b][:, at:at + 256], scalar=vcol(gain, c),
                            in1=high_[:, c, :].bitcast(F32), op0=ALU.mult, op1=ALU.subtract)
                last.then_inc(turn_low, 1)

        def turn_done(name):
            return turn_at[name] + len(turn_banks(name))

        x_ready = s_("x_ready")
        UPDATES = ["post", "ffn0", "mla", "ffn1", "ffn2", "nsa", "ffn3"]
        NORM_OF = {"f0": "post", "mx0": "ffn0", "f1": "mla", "f2": "ffn1", "mx1": "ffn2", "f3": "nsa",
                   "final": "ffn3"}

        def updated(name, t=TT - 1):
            return TT * UPDATES.index(name) + t + 1

        NORMS = ["mem", "pre", "post", "f0", "mx0", "f1", "f2", "mx1", "f3", "final"]
        norm_src = {"mem": scr[:, 0:TT * D].rearrange("p (t c) -> p t c", t=TT), "post": as3(mg["o"], TT)}
        norm_ss = {n: tiny(TT) for n in NORMS}
        norm_ms = {n: tiny(TT) for n in NORMS}
        norm_rs = {n: tiny(TT) for n in NORMS}
        power = tiny(16)
        one_col = tiny(1)
        mark_col = tiny(1)
        norm_sum, norm_mean, norm_root, norm_scaled = (s_(n) for n in ("norm_sum", "norm_mean", "norm_root",
                                                                      "norm_scaled"))

        def act_norm(act, name):
            src = norm_src.get(name, x)
            for t in range(TT):
                if name == "mem":
                    act.wait_ge(mem_here[t], 16)
                if name == "pre":
                    act.wait_ge(x_here, 16)
                if name in NORM_OF:
                    act.wait_ge(x_ready, updated(NORM_OF[name], t))
                nc.scalar.activation(xs[:, t, :], src[:, t, :], ACT.Square,
                                     accum_out=norm_ss[name][:, t:t + 1]).then_inc(norm_sum, 1)

        def pool_norm(pool, name):
            n = NORMS.index(name)
            for t in range(TT):
                pool.wait_ge(norm_sum, TT * n + t + 1)
                nc.gpsimd.tensor_scalar(norm_ms[name][:, t:t + 1], norm_ss[name][:, t:t + 1], 1.0 / D, EPS, ALU.mult,
                                        ALU.add).then_inc(norm_mean, 1)
                pool.wait_ge(norm_mean, TT * n + t + 1)
                nc.gpsimd.tensor_tensor(norm_rs[name][:, t:t + 1], norm_ms[name][:, t:t + 1], power[:, 0:1],
                                        ALU.pow).then_inc(norm_root, 1)

        def dve_norm(dve, name, gain=None, tiles=range(TT)):
            n = NORMS.index(name)
            src = norm_src.get(name, x)
            for t in tiles:
                dve.wait_ge(norm_root, TT * n + t + 1)
                root = norm_rs[name][:, t:t + 1]
                if gain is None:
                    ins = nc.vector.tensor_scalar(xs[:, t, :], src[:, t, :], root, None, ALU.mult)
                else:
                    ins = nc.vector.scalar_tensor_tensor(out=xs[:, t, :], in0=src[:, t, :], scalar=root, in1=gain,
                                                         op0=ALU.mult, op1=ALU.mult)
                ins.then_inc(norm_scaled, 1)

        def pe_norm(pe, name):
            n = NORMS.index(name)
            for t in range(TT):
                pe.wait_ge(norm_scaled, TT * n + t + 1)
                for b, _, chunks in turn_banks(name):
                    for c in chunks:
                        at = 256 * (c - 2 * b) + P * t
                        last = nc.tensor.transpose(ps[b][:, at:at + P], xs[:, t, P * c:P * c + P], ident)
                    if t == TT - 1:
                        last.then_inc(turned, 1)

        def split_product(out_, stat, mov, first, last):
            nc.tensor.matmul(out_, stat[0], mov[0], start=first, stop=False, skip_group_check=True)
            nc.tensor.matmul(out_, stat[0], mov[1], start=False, stop=False, skip_group_check=True)
            return nc.tensor.matmul(out_, stat[1], mov[0], start=False, stop=last, skip_group_check=True)

        def slot(t, k, w):
            return [h[t % SLOTS][:, 0:k * w].rearrange("p (k w) -> p k w", k=k) for h in (high, low)]

        def weights_here(pe, t, i=None):
            pe.wait_ge(w_low, val(t + 1, by(i, SLOTS)))

        def turned_chunk(pe, name, k):
            if isinstance(name, dict):
                if k in name:
                    pe.wait_ge(*name[k])
            elif name is not None and k % 2 == 0:
                pe.wait_ge(turn_low, turn_at[name] + k // 2 + 1)

        def by_feature(out_, wt, col, act_, ks, k0=0, pe=None, after=None):
            for k in range(ks):
                turned_chunk(pe, after, k)
                last = split_product(out_, [w[:, k, col:col + P] for w in wt],
                                     [a[:, k0 + k, :] for a in act_], k == 0, k == ks - 1)
            return last

        def by_token(out_, wt, col, n, act_, ks, t, k0=0, pe=None, after=None):
            for k in range(ks):
                turned_chunk(pe, after, k)
                last = split_product(out_, [a[:, k0 + k, P * t:P * t + P] for a in act_],
                                     [w[:, k, col:col + n] for w in wt], k == 0, k == ks - 1)
            return last

        NT_ = (nth, ntl)

        def pe_plain(pe, name, kind, after=None):
            t, out_ = TILE[name], ps[bank_of(name)]
            weights_here(pe, t)
            if UNIT[name] >= 2:
                pe.wait_ge(bank_done[UNIT[name] % 2], plain_free(name))
            if kind == "F":
                for j in range(2):
                    last = by_feature(out_[:, S * j:S * j + S], slot(t, KC, CW), P * j, NT_, KC, 0, pe,
                                      None if j else after)
            elif kind == "T":
                for j in range(TT):
                    last = by_token(out_[:, CW * j:CW * j + CW], slot(t, KC, CW), 0, CW, NT_, KC, j, 0, pe,
                                    None if j else after)
            elif kind == "FT":
                by_feature(out_[:, 0:S], slot(t, KC, CW), 0, NT_, KC)
                for j in range(TT):
                    last = by_token(out_[:, S + P * j:S + P * j + P], slot(t, KC, CW), P, P, NT_, KC, j)
            elif kind == "TF":
                for j in range(TT):
                    by_token(out_[:, P * j:P * j + P], slot(t, KC, CW), 0, P, NT_, KC, j, 0, pe,
                             None if j else after)
                last = by_feature(out_[:, S:2 * S], slot(t, KC, CW), P, NT_, KC)
            else:
                last = by_feature(out_[:, 0:S], slot(t, KC, P), 0, NT_, KC)
            last.then_inc(w_used, 1)

        def read_bank(eng, name):
            eng.wait_ge(w_used, TILE[name] + 1)
            return ps[bank_of(name)]

        def bank_read(name, ins):
            ins.then_inc(bank_done[UNIT[name] % 2], 1)

        def wait_bank(eng, name):
            eng.wait_ge(bank_done[UNIT[name] % 2], UNIT[name] // 2 + 1)

        def padded(k, g, odd):
            return k[:, S * (2 * g + odd):S * (2 * g + odd) + S]

        UNITS = []
        for h in range(XM_H):
            UNITS.append(dict(q=xm["q"][:, S * h:S * h + S], k=xm["k"][:, S * h:S * h + S],
                              v=[r3(xm["v"], TT)[:, t, P * h:P * h + P] for t in range(TT)],
                              d=P, causal=False, mask=None, scale=P ** -0.5))
        for h in range(SW_H):
            kv = h // (SW_H // SW_KV)
            UNITS.append(dict(q=sw["q"][:, S * (h // 2):S * (h // 2) + S], k=padded(sw["k"], kv, h % 2),
                              v=[r3(sw["v"], TT)[:, t, 64 * kv:64 * kv + 64] for t in range(TT)],
                              d=64, causal=True, mask=window, scale=SW_D ** -0.5))
        for h in range(MLA_H):
            UNITS.append(dict(q=r3(ml["q"], MLA_H)[:, h, :], k=r3(ml["k"], MLA_H)[:, h, :],
                              v=[r3(ml["v"], TT)[:, t, 64 * h:64 * h + 64] for t in range(TT)],
                              d=64, causal=True, mask=causal, scale=(MLA_N + MLA_R) ** -0.5))
        for kk, vv in (("ks", "vs"), ("kw", "vw")):
            for h in range(NSA_H):
                g = h // NSA_R
                UNITS.append(dict(q=ns["q"][:, S * (h // 2):S * (h // 2) + S], k=padded(ns[kk], g, h % 2),
                                  v=[r3(ns[vv], TT)[:, t, 64 * g:64 * g + 64] for t in range(TT)],
                                  d=64, causal=True, mask=r3(ns["bias"], NSA_H)[:, h, ::-1], scale=NSA_D ** -0.5))
        XM0, SW0 = 0, XM_H
        MLA0 = SW0 + SW_H
        NSA0 = MLA0 + MLA_H
        at_scored, at_max, at_exp, at_turned, at_out, at_read = (
            s_(n) for n in ("at_scored", "at_max", "at_exp", "at_turned", "at_out", "at_read"))
        at_copied = [s_("at_copied0"), s_("at_copied1")]
        RING = 6
        at_mx, at_nm, at_sum, at_inv, at_sinkexp = ([tiny(TT) for _ in range(RING)] for _ in range(5))
        neg_sink = tiny(SW_H)
        def cols_of(u, t):
            return slice(0, 256) if t == 1 else slice(256, 384 if u["causal"] else 512)

        def pe_units(pe, first, n):
            def scores(a):
                u = UNITS[a]
                if a >= 2:
                    pe.wait_ge(at_max if u["causal"] and UNITS[a - 2]["causal"] else at_exp, a - 1)
                for t in (1, 0):
                    c = cols_of(u, t)
                    last = nc.tensor.matmul(ps[a % 2][:, c], u["q"][:, P * t:P * t + P],
                                            u["k"][:, 0:c.stop - c.start], start=True, stop=True)
                last.then_inc(at_scored, 1)

            def turn_probs(a):
                u = UNITS[a]
                pe.wait_ge(at_exp, a + 1)
                if a >= 2:
                    pe.wait_ge(at_copied[a % 2], a // 2)
                for c in range(0, cols_of(u, 0).stop, P):
                    last = nc.tensor.transpose(ps[2 + a % 2][:, c:c + P], at_s[a % 3][:, c:c + P], ident)
                last.then_inc(at_turned, 1)

            def values(a):
                u = UNITS[a]
                pe.wait_ge(at_copied[a % 2], a // 2 + 1)
                if a >= 2:
                    pe.wait_ge(at_read, a - 1)
                d = u["d"]
                for t in (0, 1):
                    c = cols_of(u, t)
                    n_k = (c.stop - c.start) // P
                    for kt in range(n_k):
                        last = nc.tensor.matmul(ps[6 + a % 2][:, d * t:d * t + d],
                                                at_p[a % 2][:, c.start + P * kt:c.start + P * kt + P],
                                                u["v"][kt], start=kt == 0, stop=kt == n_k - 1)
                last.then_inc(at_out, 1)

            for a in range(first, first + n + 3):
                if a < first + n:
                    scores(a)
                if first <= a - 2 < first + n:
                    turn_probs(a - 2)
                if first <= a - 3:
                    values(a - 3)

        def copy_probs(eng, a):
            w = cols_of(UNITS[a], 0).stop
            eng.wait_ge(at_turned, a + 1)
            if a >= 2:
                eng.wait_ge(at_out, a - 1)
            if a % 2 == 0:
                ins = nc.scalar.activation(at_p[0][:, 0:w], ps[2][:, 0:w], ACT.Copy)
            else:
                ins = nc.scalar.activation(at_p[1][:, 0:w], ps[3][:, 0:w], ACT.Copy)
            ins.then_inc(at_copied[a % 2], 1)

        def act_units(act, first, n, sinks=False):
            for a in range(first, first + n + 2):
                if a - 2 >= first:
                    copy_probs(act, a - 2)
                if a < first + n:
                    u, b, r = UNITS[a], a % 3, a % RING
                    act.wait_ge(at_max, a + 1)
                    if a >= 3:
                        act.wait_ge(at_turned, a - 2)
                    if a >= RING:
                        act.wait_ge(at_read, a - RING + 1)
                    src = at_s[b] if u["causal"] else ps[a % 2]
                    if sinks:
                        nc.scalar.activation(at_sinkexp[r], at_nm[r], ACT.Exp,
                                             bias=row[:, ROW["sink"] + a - first:ROW["sink"] + a - first + 1])
                    for t in (1, 0):
                        c = cols_of(u, t)
                        last = nc.scalar.activation(at_s[b][:, c], src[:, c], ACT.Exp, scale=u["scale"],
                                                    bias=at_nm[r][:, t:t + 1], accum_out=at_sum[r][:, t:t + 1])
                    last.then_inc(at_exp, 1)

        def dve_units(dve, ch, first, n, evac, sinks=False):
            for a in range(first, first + n + 4):
                if a < first + n:
                    u, b, r = UNITS[a], a % 3, a % RING
                    dve.wait_ge(at_scored, a + 1)
                    if a >= 3:
                        dve.wait_ge(at_turned, a - 2)
                    if u["causal"]:
                        for t in (1, 0):
                            c = cols_of(u, t)
                            m = u["mask"] if t == 1 else u["mask"][:, P:2 * P]
                            ch.mark(nc.vector.tensor_tensor_reduce(at_s[b][:, c], ps[a % 2][:, c], m, 1.0, -3e38,
                                                                   ALU.add, ALU.max, at_mx[r][:, t:t + 1]))
                    else:
                        for t in (1, 0):
                            ch.mark(nc.vector.tensor_reduce(at_mx[r][:, t:t + 1], ps[a % 2][:, cols_of(u, t)],
                                                            AX.X, ALU.max))
                    ch.join()
                    if sinks:
                        ins = nc.vector.tensor_scalar(at_nm[r], at_mx[r], -u["scale"],
                                                      neg_sink[:, a - first:a - first + 1], ALU.mult, ALU.min)
                    else:
                        ins = nc.vector.tensor_scalar(at_nm[r], at_mx[r], -u["scale"], None, ALU.mult)
                    ins.then_inc(at_max, 1)
                if first <= a - 4:
                    b, r = a % 2, (a - 4) % RING
                    dve.wait_ge(at_exp, a - 3)
                    if sinks:
                        ch.link(nc.vector.tensor_tensor(at_sum[r], at_sum[r], at_sinkexp[r], ALU.add))
                    ch.link(nc.vector.reciprocal(at_inv[r], at_sum[r]))
                    dve.wait_ge(at_out, a - 3)
                    evac(a - 4, ps[6 + b], at_inv[r]).then_inc(at_read, 1)


        def bc(ap, n):
            return ap.unsqueeze(2).broadcast_to([ap.shape[0], ap.shape[1], n])

        def rep(ap, n):
            return ap.unsqueeze(1).broadcast_to([ap.shape[0], n, ap.shape[1]])

        zeroed = s_("zeroed")
        setup_done, out_written = s_("setup_done"), s_("out_written")
        mem_here, ident_here, x_here, row_here = [s_("mem_here0"), s_("mem_here1")], s_("ident_here"), s_("x_here"), \
            s_("row_here")

        def act_step(act, name):
            if TILE[name] + 2 < NT:
                split_high(act, TILE[name] + 2)

        def dve_step(dve, name):
            if TILE[name] + 2 < NT:
                split_low(dve, TILE[name] + 2)

        gm_loaded, gm_sum, gm_mean, gm_root, gm_vn, gm_wturned, gm_wmask, gm_mixed, gm_y, gm_high, gm_low = (
            s_("gm_" + n) for n in ("loaded", "sum", "mean", "root", "vn", "wturned", "wmask", "mixed", "y",
                                    "high", "low"))
        gm_ss, gm_ms, gm_rs = tiny(TT), tiny(TT), tiny(TT)

        d_ba = tiny(16)
        d_beta, d_z, d_az, d_l, d_sp, d_ea, d_g, d_egc, d_dm, d_ekd = (tiny(PAIRS) for _ in range(10))
        d_gc = tiny(16)
        d_ss, d_ms, d_rs = tiny(16), tiny(16), tiny(16)
        d_os, d_om, d_or = tiny(PAIRS), tiny(PAIRS), tiny(PAIRS)
        d_bat = dn["kb"][0:2 * DN_H, 0:S]
        n_gt = scr[0:3 * NSA_H, 0:S]
        cin = dn["cin"].rearrange("p (c t) -> p c t", c=12)
        cact = dn["cact"].rearrange("p (c t) -> p c t", c=12)
        tok = dn["tok"].rearrange("p (t c d) -> p t c d", t=TT, c=12)
        d_T, d_TT, d_P = (dn["cin"][:, 1024 * n:1024 * n + 1024] for n in range(3))
        d_E, d_Es, d_Lm = (dn["cact"][:, 1024 * n:1024 * n + 1024] for n in range(3))
        d_L, d_A = dn["kb"], dn["qt"]
        d_Lms = [d_Lm, d_Es]
        d_u, d_wt, d_S, d_vn = (dn["cact"][:, a:b] for a, b in ((0, 1024), (1024, 1536), (1536, 2048),
                                                              (2048, 2560)))
        d_qg = dn["cin"][:, 2048:2560]
        d_kbt = xs[:, 0, :]
        d_level = xs[:, 1, 0:LEVELS * P].rearrange("p (l i) -> p l i", l=LEVELS)
        d_sz = late[:, 3072:4096]
        heads = lambda ap: ap.rearrange("p (t h d) -> p t h d", t=TT, h=DN_H)
        pair = lambda ap, n: ap[:, P * n:P * n + P]
        (dn_conv, dn_act, dn_turn, dn_tok, dn_sum, dn_mean, dn_root, dn_ready, dn_fm, dn_fa, dn_fd, dn_absz,
         dn_exps, dn_g, dn_gcs, dn_gcd, dn_egs, dn_diff, dn_ed, dn_kk, dn_la, dn_lm, dn_p, dn_pc, dn_y,
         dn_t, dn_u, dn_uc, dn_wc, dn_o0, dn_sc, dn_ws, dn_vnd, dn_o1, dn_osum, dn_omean, dn_oroot, dn_out,
         dn_level, dn_zeroed, dn_setup, dn_tap0, dn_bas) = (
            s_("dn_" + n) for n in ("conv", "act", "turn", "tok", "sum", "mean", "root", "ready", "fm", "fa", "fd",
                                    "absz", "exps", "g", "gcs", "gcd", "egs", "diff", "ed", "kk", "la",
                                    "lm", "p", "pc", "y", "t", "u", "uc", "wc", "o0", "sc", "ws", "vnd", "o1",
                                    "osum", "omean", "oroot", "out", "level", "zeroed", "setup",
                                    "tap0", "bas"))
        kn_ = lambda t: [tok[:, t, 4 + h, :] for h in range(DN_H)]
        qn_ = lambda t: [tok[:, t, h, :] for h in range(DN_H)]
        DN_TURNS = [
            (kn_(0), dn["kt"][:, 0:512], 0), (kn_(1), dn["kt"][:, 512:1024], 1),
            (qn_(0), dn["qt"][:, 0:512], 2), (qn_(1), dn["qt"][:, 512:1024], 3),
            ([pair(dn["kb"], h) for h in range(4)], d_kbt[:, 0:512], 6),
            ([pair(dn["kb"], 4 + h) for h in range(4)], d_kbt[:, 512:1024], 7),
            ([pair(d_qg, h) for h in range(4)], dn["qgt"], 0),
        ]

        def attention_evac(y, first, d, z=None):
            def evac(a, o, inv):
                h = a - first
                for t in range(TT):
                    c = slice(d * h, d * h + d)
                    if z is None:
                        last = nc.vector.tensor_scalar(y[:, t, c], o[:, d * t:d * t + d], inv[:, t:t + 1], None,
                                                       ALU.mult)
                    else:
                        last = nc.vector.scalar_tensor_tensor(out=y[:, t, c], in0=o[:, d * t:d * t + d],
                                                              scalar=inv[:, t:t + 1], in1=z[:, t, c],
                                                              op0=ALU.mult, op1=ALU.mult)
                return last
            return evac

        ff_gate, ff_h, ff_hhigh, ff_hlow, ff_tile0 = (s_("ff_" + n) for n in ("gate", "h", "hhigh", "hlow",
                                                                           "tile0"))

        def pe_ffn(pe, f):
            tb = TILE[f"f{f}g0"]
            n0 = FT * f

            def gate(t, c, i=None, after=None):
                weights_here(pe, t, i)
                if c > 0:
                    pe.wait_ge(ff_gate, val(c, by(i, 1)))
                for j in range(2):
                    last = by_feature(ps[4][:, S * j:S * j + S], slot(t, KC, CW), P * j, NT_, KC, 0, pe,
                                      None if j else after)
                last.then_inc(w_used, 1)

            def up(t, c, i=None):
                weights_here(pe, t, i)
                if c > 0:
                    pe.wait_ge(ff_h, val(c, by(i, 1)))
                for j in range(2):
                    last = by_feature(ps[5][:, S * j:S * j + S], slot(t, KC, CW), P * j, NT_, KC)
                last.then_inc(w_used, 1)

            def down(t, c, i=None, first=False, last_=False):
                weights_here(pe, t, i)
                pe.wait_ge(ff_hlow, val(c + 1, by(i, 1)))
                w = slot(t, 2, D)
                for tt in range(TT):
                    for half in range(2):
                        for j in range(2):
                            last = split_product(ps[2 * tt + half][:, :],
                                                 [h[:, j, P * tt:P * tt + P] for h in (hth, htl)],
                                                 [a[:, j, 512 * half:512 * half + 512] for a in w],
                                                 first and j == 0, last_ and j == 1)
                    if last_ and tt == 0:
                        last.then_inc(ff_tile0, 1)
                last.then_inc(w_used, 1)

            gate(tb, n0, after=f"f{f}")
            up(tb + 1, n0)
            gate(tb + 2, n0 + 1)
            up(tb + 3, n0 + 1)
            down(tb + 4, n0, first=True)
            with pe.Fori(0, FT - 2) as i:
                gate(tb + 5, n0 + 2, i)
                up(tb + 6, n0 + 2, i)
                down(tb + 7, n0 + 1, i)
            down(tb + 3 * FT - 1, n0 + FT - 1, last_=True)

        def act_ffn(act, f):
            tb = TILE[f"f{f}g0"]
            n0 = FT * f

            def gated(t, c, i=None):
                act.wait_ge(w_used, val(t + 1, by(i, SLOTS)))
                if c > 0:
                    act.wait_ge(ff_h, val(c, by(i, 1)))
                nc.scalar.activation(ff["sg"], ps[4][:, :], ACT.Silu).then_inc(ff_gate, 1)

            def rounded(t_down_before, c, i=None):
                act.wait_ge(ff_h, val(c + 1, by(i, 1)))
                if t_down_before is not None:
                    act.wait_ge(w_used, val(t_down_before + 1, by(i, SLOTS)))
                nc.scalar.activation(hth[:, :, :], r3(ff["h"], 2), ACT.Copy).then_inc(ff_hhigh, 1)

            split_high(act, tb + 2)
            gated(tb, n0)
            split_high(act, tb + 3)
            split_high(act, tb + 4)
            rounded(None, n0)
            gated(tb + 2, n0 + 1)
            split_high(act, tb + 5)
            split_high(act, tb + 6)
            rounded(tb + 4, n0 + 1)
            with act.Fori(0, FT - 2) as i:
                split_high(act, tb + 7, i)
                gated(tb + 5, n0 + 2, i)
                split_high(act, tb + 8, i)
                split_high(act, tb + 9, i)
                rounded(tb + 7, n0 + 2, i)
            if tb + 3 * FT + 1 < NT:
                split_high(act, tb + 3 * FT + 1)

        def dve_ffn(dve, f):
            tb = TILE[f"f{f}g0"]
            n0 = FT * f

            def hidden(t, c, i=None):
                dve.wait_ge(w_used, val(t + 1, by(i, SLOTS)))
                dve.wait_ge(ff_gate, val(c + 1, by(i, 1)))
                if c > 0:
                    dve.wait_ge(ff_hlow, val(c, by(i, 1)))
                nc.vector.tensor_tensor(ff["h"], ff["sg"], ps[5][:, :], ALU.mult).then_inc(ff_h, 1)

            def rest(c, i=None):
                dve.wait_ge(ff_hhigh, val(c + 1, by(i, 1)))
                nc.vector.tensor_tensor(htl[:, :, :], r3(ff["h"], 2), hth[:, :, :].bitcast(F32), ALU.subtract)\
                    .then_inc(ff_hlow, 1)

            split_low(dve, tb + 2)
            split_low(dve, tb + 3)
            hidden(tb + 1, n0)
            split_low(dve, tb + 4)
            rest(n0)
            split_low(dve, tb + 5)
            hidden(tb + 3, n0 + 1)
            split_low(dve, tb + 6)
            rest(n0 + 1)
            with dve.Fori(0, FT - 2) as i:
                split_low(dve, tb + 7, i)
                split_low(dve, tb + 8, i)
                hidden(tb + 6, n0 + 2, i)
                split_low(dve, tb + 9, i)
                rest(n0 + 2, i)
            if tb + 3 * FT + 1 < NT:
                split_low(dve, tb + 3 * FT + 1)
            for tt in range(TT):
                if tt == 0:
                    dve.wait_ge(ff_tile0, f + 1)
                else:
                    dve.wait_ge(w_used, tb + 3 * FT)
                for half in range(2):
                    xo = x[:, tt, 512 * half:512 * half + 512]
                    last = nc.vector.scalar_tensor_tensor(out=xo, in0=ps[2 * tt + half][:, :], scalar=0.5,
                                                          in1=xo, op0=ALU.mult, op1=ALU.add)
                last.then_inc(x_ready, 1)


        mg_sig, mg_mul, mg_add, mg_high, mg_low, mg_post = (
            s_("mg_" + n) for n in ("sig", "mul", "add", "high", "low", "post"))
        MB = TILE["gate000"]

        MERGED = [(0, 4, 1), (4, 6, 2), (6, 8, 3)]

        def pe_merge_gates(pe, n, half, i=None):
            for g in range(2):
                t = MB + 6 * n + 3 * half + g
                pe.wait_ge(w_low, val(t + 1, by(i, 6)))
                q = 4 * n + 2 * half + g
                if q >= 2:
                    pe.wait_ge(mg_sig, val(q - 1, by(i, 4)))
                for j in range(2):
                    last = by_feature(ps[4 + g][:, S * j:S * j + S], slot(t, KC, CW), P * j, NT_, KC)
                last.then_inc(w_used, 1)

        def pe_merge_up(pe, n, half, i=None):
            t = MB + 6 * n + 3 * half + 2
            pe.wait_ge(w_low, val(t + 1, by(i, 6)))
            u = 2 * (2 * n + half)
            if u >= 2:
                pe.wait_ge(mg_mul, val(u, by(i, 4)))
            ys = (yth[:, n, :, :], ytl[:, n, :, :]) if i is None else \
                tuple(y[:, bass.ds(i + n, 1), :, :].rearrange("p o k s -> p (o k) s") for y in (yth, ytl))
            for c in range(4):
                last = by_feature(ps[c // 2][:, S * (c % 2):S * (c % 2) + S], slot(t, 4, 512), P * c, ys, 4)
            last.then_inc(w_used, 1)

        def act_merge_branch(act, n, i=None):
            for half in range(2):
                for g in range(2):
                    t = MB + 6 * n + 3 * half + g
                    if i is not None or half + g:
                        merge_split_high(act, t + 2, i)
                    act.wait_ge(w_used, val(t + 1, by(i, 6)))
                    if n > 0:
                        act.wait_ge(mg_mul, val(4 * (n - 1) + 2 * half + g + 1, by(i, 4)))
                    nc.scalar.activation(mg["sg"][:, 1024 * half + 512 * g:1024 * half + 512 * g + 512],
                                         ps[4 + g][:, :], ACT.Sigmoid).then_inc(mg_sig, 1)
                merge_split_high(act, MB + 6 * n + 3 * half + 4, i)

        def merge_split_high(act, t, i):
            act.wait_ge(raw_here[t % SLOTS], val(16 * (t // SLOTS + 1), by(i, 32)))
            act.wait_ge(w_used, val(t - SLOTS + 1, by(i, 6)))
            nc.scalar.activation(high[t % SLOTS][:], raw[t % SLOTS][:], ACT.Copy).then_inc(w_high, 1)

        def merge_split_low(dve, t, i):
            dve.wait_ge(w_high, val(t + 1, by(i, 6)))
            nc.vector.tensor_tensor(low[t % SLOTS][:], raw[t % SLOTS][:], high[t % SLOTS][:].bitcast(F32),
                                    ALU.subtract).then_inc(w_low, 1)

        def dve_merge_branch(dve, n, i=None):
            for half in range(2):
                t = MB + 6 * n + 3 * half
                if i is not None or half:
                    merge_split_low(dve, t + 2, i)
                merge_split_low(dve, t + 3, i)
                merge_split_low(dve, t + 4, i)
                dve.wait_ge(w_used, val(t + 3, by(i, 6)))
                for b in range(2):
                    q = 4 * n + 2 * half + b
                    c = slice(1024 * half + 512 * b, 1024 * half + 512 * b + 512)
                    dve.wait_ge(mg_sig, val(q + 1, by(i, 4)))
                    if n > 0:
                        dve.wait_ge(mg_add, val(4 * (n - 1) + 2 * half + b + 1, by(i, 4)))
                    nc.vector.tensor_tensor(mg["prod"][:, c], ps[b][:, :], mg["sg"][:, c], ALU.mult)\
                        .then_inc(mg_mul, 1)
                    dve.wait_ge(mg_mul, val(q + 1, by(i, 4)))
                    if n == 0 and i is None:
                        ins = nc.vector.tensor_copy(mg["m"][:, c], mg["prod"][:, c])
                    else:
                        ins = nc.vector.tensor_tensor(mg["m"][:, c], mg["m"][:, c], mg["prod"][:, c], ALU.add)
                    ins.then_inc(mg_add, 1)

        (ml_ss, ml_ms, ml_rs, ml_cs, ml_q, ml_qa, ml_qd, ml_ka, ml_kd, ml_va, ml_vd, ml_krd, ml_zero) = (
            s_("ml_" + n) for n in ("ss", "ms", "rs", "cs", "q", "qa", "qd", "ka", "kd", "va",
                                    "vd", "krd", "zero"))

        def uq_here(eng, j, b):
            if b:
                eng.wait_ge(w_used, TILE[f"uq{j}"] + 1)
            else:
                eng.wait_ge(ml_q, j + 1)

        m_ss, m_ms, m_rs = tiny(4), tiny(4), tiny(4)
        mc = as3(mlc["c"], TT)
        MLC = [(t, c) for c in (slice(0, MLA_QL), slice(MLA_QL, MLA_QL + MLA_KVL)) for t in range(TT)]
        mq, mk_ = r3(ml["q"], MLA_H), r3(ml["k"], MLA_H)
        mrot = mlc["rot"]
        rope_ = c_("rope", S)

        (ns_w1, ns_tbl, ns_line, ns_linec, ns_lined, ns_bias, ns_hid, ns_hc, ns_kc, ns_kcd, ns_vc,
         ns_vcd, ns_cs, ns_cm, ns_ce, ns_posed, ns_ct, ns_ctc, ns_co, ns_cy, ns_zero, ns_pos, ns_gt) = (
            s_("ns_" + n) for n in ("w1", "tbl", "line", "linec", "lined", "bias", "hid", "hc", "kc",
                                    "kcd", "vc", "vcd", "cs", "cm", "ce", "posed", "ct", "ctc", "co", "cy", "zero",
                                    "pos", "gt"))
        n_gate = tiny(TT * 48)
        n_hid = [tiny(64), tiny(64)]
        n_pos, n_kc = tiny(2), tiny(NSA_G * 2 * NCMP)
        n_mx, n_sum, n_inv, n_cg = (tiny(TT * NSA_H) for _ in range(4))
        n_ag = [tiny(TT) for _ in range(2)]
        kc2 = n_kc.rearrange("p (g two n) -> p g two n", g=NSA_G, two=2)
        w2s = sb("w2s", [P, 2, 64])
        poss = sb("poss", [P, 2, CMP_L // 2])
        sc = xs[:, 0, :].rearrange("p (t h n) -> p t h n", t=TT, h=NSA_H)
        sct = xs[:, 1, :]
        gate3 = n_gate.rearrange("p (t h b) -> p t h b", t=TT, h=NSA_H)
        xx = [r3(ns["xk"], NSA_G), r3(ns["xv"], NSA_G)]
        w1s = nl["w1"].rearrange("p (m j f) -> p m j f", m=2, j=CMP_L // 2)
        vcd = r3(nl["vc"], NSA_G)
        nbias = r3(ns["bias"], NSA_H)
        ny = as3(nl["y"], TT)
        BIAS_ROWS = BUCKETS + 1

        def doubled(dst, bank, c_dst):
            src = r3(bank, 2)
            d = dst.rearrange("p (c g two s) -> p g two c s", c=c_dst // 2, g=2, two=2)
            for g in range(2):
                for half in range(2):
                    yield d[64 * half:64 * half + 64, g, half], src[64 * g:64 * g + 64]


        block = ctx.enter_context(nc.Block())

        @block.sync
        def _(sp):
            for t in range(TT):
                sp.dma_start(norm_src["mem"][:, t, :], A["mem"][:, t, :]).then_inc(mem_here[t], 16)
            sp.dma_start(ident, A["con"][:, 0:P]).then_inc(ident_here, 16)
            sp.dma_start(vec[:], A["vec"]).then_inc(ident_here, 16)
            sp.dma_start(raw[0][:], A["stream"][0]).then_inc(raw_here[0], 16)
            sp.dma_start(x[:, :, :], A["x"]).then_inc(x_here, 16)
            sp.dma_start(con[:, P:NCON], A["con"][:, P:NCON]).then_inc(row_here, 16)
            sp.dma_start(row[:], A["row"]).then_inc(row_here, 16)
            for t in range(1, SLOTS):
                sp.dma_start(raw[t][:], A["stream"][t]).then_inc(raw_here[t], 16)
            with sp.Fori(1, (NT - 1) // SLOTS) as i:
                for c in range(SLOTS):
                    tile = sp.snap(i * SLOTS + c)
                    sp.wait_ge(w_low, i * SLOTS + (c - SLOTS + 1))
                    sp.dma_start(raw[c][:], A["stream"][bass.ds(tile, 1)].rearrange("o p w -> (o p) w"))\
                        .then_inc(raw_here[c], 16)
            t = NT - 1
            sp.wait_ge(w_low, t - SLOTS + 1)
            sp.dma_start(raw[t % SLOTS][:], A["stream"][t]).then_inc(raw_here[t % SLOTS], 16)
            for t in range(TT):
                sp.wait_ge(norm_scaled, TT * NORMS.index("final") + t + 1)
                sp.dma_start(out[:, t, :], xs[:, t, :]).then_inc(out_written, 16)
            sp.wait_ge(out_written, 16 * TT)

        @block.gpsimd
        def _(pool):
            nc.gpsimd.memset(power, -0.5).then_inc(setup_done, 1)
            nc.gpsimd.memset(one_col, 1.0).then_inc(setup_done, 1)
            pool.wait_ge(setup_done, 2)
            nc.gpsimd.memset(sw["k"], 0.0).then_inc(zeroed, 1)
            pool_norm(pool, "mem")
            pool_norm(pool, "pre")
            pool.wait_ge(turn_low, turn_done("ym"))
            pool.dma_start(gm["w"], A["spatial"].rearrange("p g q -> p (g q)")).then_inc(gm_loaded, 16)
            pool.dma_start(xs[:, 1, 0:LEVELS * P], A["level"]).then_inc(dn_level, 16)
            pool.wait_ge(gm_sum, TT)
            nc.gpsimd.tensor_scalar(gm_ms, gm_ss, 1.0 / BW, EPS, ALU.mult, ALU.add).then_inc(gm_mean, 1)
            pool.wait_ge(gm_mean, 1)
            nc.gpsimd.tensor_tensor(gm_rs, gm_ms, power[:, 0:TT], ALU.pow).then_inc(gm_root, 1)
            pool.wait_ge(gm_low, 1)
            nc.gpsimd.memset(cin[:, :, 0:3], 0.0).then_inc(dn_zeroed, 1)
            pool.wait_ge(dn_sum, 2)
            nc.gpsimd.tensor_scalar(d_ms, d_ss, 1.0, EPS, ALU.mult, ALU.add).then_inc(dn_mean, 1)
            pool.wait_ge(dn_mean, 1)
            nc.gpsimd.tensor_tensor(d_rs, d_ms, power, ALU.pow).then_inc(dn_root, 1)
            pool.wait_ge(dn_osum, 1)
            nc.gpsimd.tensor_scalar(d_om, d_os, 1.0 / P, EPS, ALU.mult, ALU.add).then_inc(dn_omean, 1)
            pool.wait_ge(dn_omean, 1)
            nc.gpsimd.tensor_tensor(d_or, d_om, power[:, 0:PAIRS], ALU.pow).then_inc(dn_oroot, 1)
            pool.wait_ge(turn_low, turn_done("ya"))
            pool.dma_start(mg["post"], A["post"]).then_inc(mg_post, 16)
            pool_norm(pool, "post")
            pool_norm(pool, "f0")
            pool.wait_ge(norm_root, TT * (NORMS.index("f0") + 1))
            nc.gpsimd.memset(scr[96:128, 2048:2048 + 2 * MLA_H * S], 0.0).then_inc(ml_zero, 1)
            pool.wait_ge(ml_zero, 1)
            pool_norm(pool, "mx0")
            for n, w in enumerate((MLA_QL, MLA_KVL)):
                c = slice(TT * n, TT * n + TT)
                pool.wait_ge(ml_ss, TT * n + TT)
                nc.gpsimd.tensor_scalar(m_ms[:, c], m_ss[:, c], 1.0 / w, EPS, ALU.mult, ALU.add).then_inc(ml_ms, 1)
                pool.wait_ge(ml_ms, n + 1)
                nc.gpsimd.tensor_tensor(m_rs[:, c], m_ms[:, c], power[:, 0:TT], ALU.pow).then_inc(ml_rs, 1)
            pool_norm(pool, "f1")
            pool.wait_ge(x_ready, updated("mla"))
            pool.dma_start(nl["w1"], A["w1"].rearrange("p m w -> p (m w)")).then_inc(ns_w1, 16)
            pool.dma_start(w2s[:, :, :], A["w2"]).then_inc(ns_w1, 16)
            pool.dma_start(poss[:, :, :], A["pos"]).then_inc(ns_w1, 16)
            pool.dma_start(nt_["hot"][0:BIAS_ROWS, :], A["hot"]).then_inc(ns_tbl, 16)
            pool.dma_start(nt_["tbl"][0:BIAS_ROWS, :], A["bucket_bias"]).then_inc(ns_tbl, 16)
            nc.gpsimd.memset(ns["ks"], 0.0).then_inc(zeroed, 1)
            nc.gpsimd.memset(n_kc, 0.0)
            nc.gpsimd.memset(nl["vc"], 0.0).then_inc(ns_zero, 1)
            pool_norm(pool, "f2")
            pool.wait_ge(ns_linec, 1)
            pool.dma_start(line, nt_["line"][0:NSA_H, :]).then_inc(ns_lined, 16)
            pool.wait_ge(ns_lined, 16)
            pool.dma_start(nbias, bass.AP(line.tensor, S - P + 1, [[1, P], [2 * S, NSA_H], [1, S]]))\
                .then_inc(ns_bias, 16)
            pool_norm(pool, "mx1")
            pool.wait_ge(turn_low, turn_done("mx1"))
            nc.gpsimd.memset(xs[:, 0, :], 0.0).then_inc(ns_zero, 1)
            pool.wait_ge(ns_hid, 1)
            nc.gpsimd.memset(ns["kw"], 0.0).then_inc(zeroed, 1)
            pool_norm(pool, "f3")
            pool.dma_start(scr[:, 4096:4096 + D], A["final"]).then_inc(mg_post, 16)
            pool_norm(pool, "final")

        @block.scalar
        def _(act):
            act_norm(act, "mem")
            split_high(act, 0)
            act.wait_ge(ident_here, 32)
            act_turn(act, "mem")
            split_high(act, 1)
            for name, dst in (("mk0", xm["k"][:, 0:512]), ("mk1", xm["k"][:, 512:1024])):
                act_step(act, name)
                bank_read(name, nc.scalar.activation(dst, read_bank(act, name)[:, :], ACT.Copy))
            act_step(act, "mv0")
            act_step(act, "mv1")
            act.wait_ge(turn_low, turn_done("mem"))
            act_norm(act, "pre")
            act.wait_ge(w_used, TILE["mv1"] + 1)
            act_turn(act, "pre")
            for j in range(2):
                name = f"xmq{j}"
                act_step(act, name)
                bank_read(name, nc.scalar.activation(xm["q"][:, 512 * j:512 * j + 512], read_bank(act, name)[:, :],
                                                     ACT.Copy))
            for j in range(2):
                name = f"xmz{j}"
                act_step(act, name)
                bank_read(name, nc.scalar.activation(as3(xm["z"], TT)[:, :, CW * j:CW * j + CW],
                                                     r3(read_bank(act, name), TT), ACT.Silu))
            act_units(act, XM0, XM_H)
            act_turn(act, "ym")
            for j in range(2):
                name = f"swq{j}"
                act_step(act, name)
                bank_read(name, nc.scalar.activation(sw["q"][:, 512 * j:512 * j + 512], read_bank(act, name)[:, :],
                                                     ACT.Copy))
            act_step(act, "swkv")
            for j in range(2):
                name = f"swz{j}"
                act_step(act, name)
                bank_read(name, nc.scalar.activation(as3(sw["z"], TT)[:, :, CW * j:CW * j + CW],
                                                     r3(read_bank(act, name), TT), ACT.Silu))
            act_units(act, SW0, SW_H, sinks=True)
            act_turn(act, "yc")
            for j in range(2):
                name = f"gmv{j}"
                act_step(act, name)
                bank_read(name, nc.scalar.activation(as3(gm["v"], TT)[:, :, CW * j:CW * j + CW],
                                                     r3(read_bank(act, name), TT), ACT.Gelu_apprx_tanh))
            wait_bank(act, "gmv0")
            wait_bank(act, "gmv1")
            for t in range(TT):
                nc.scalar.activation(gm["sq"][:, 512 * t:512 * t + 512], gm["v"][:, 512 * t:512 * t + 512],
                                     ACT.Square, accum_out=gm_ss[:, t:t + 1]).then_inc(gm_sum, 1)
            for name, dst, func in (("gmu0", gm["u"][:, 0:512], ACT.Gelu_apprx_tanh),
                                    ("gmu1", gm["u"][:, 512:1024], ACT.Gelu_apprx_tanh),
                                    ("gmz0", gm["z"][:, 0:512], ACT.Silu), ("gmz1", gm["z"][:, 512:1024], ACT.Silu)):
                act_step(act, name)
                bank_read(name, nc.scalar.activation(dst, read_bank(act, name)[:, :], func))
            act.wait_ge(gm_y, 1)
            nc.scalar.activation(yth[:, 1], r3(gm["sq"], 4), ACT.Copy).then_inc(gm_high, 1)
            ch = Chain(act, "act_chain")
            act_step(act, "ba")
            act.wait_ge(dn_zeroed, 1)
            act.wait_ge(gm_low, 1)
            for j in range(6):
                name = f"dn{j}"
                act_step(act, name)
                bank_read(name, nc.scalar.activation(cin[:, 2 * j:2 * j + 2, 3:3 + S], r3(read_bank(act, name), 2),
                                                     ACT.Copy))
                wait_bank(act, name)
                for c in (2 * j, 2 * j + 1):
                    last = nc.scalar.activation(cact[:, c, :], cin[:, c, 0:S], ACT.Copy, scale=vcol("conv", c))
                last.then_inc(dn_tap0, 1)
                if j == 2:
                    act.wait_ge(dn_absz, 1)
                    nc.scalar.activation(r3(d_beta, TT), r3(d_ba, TT)[:, :, 0:DN_H], ACT.Sigmoid).then_inc(dn_exps, 1)
                    nc.scalar.activation(d_ea, rowof("alog", PAIRS), ACT.Exp).then_inc(dn_exps, 1)
                    ch.link(nc.scalar.activation(d_l, d_az, ACT.Exp, scale=-1.0))
                    nc.scalar.activation(d_l, d_l, ACT.Ln, bias=one_col).then_inc(dn_exps, 1)
                if j:
                    act.wait_ge(dn_conv, j)
                    nc.scalar.activation(cact[:, 2 * j - 2:2 * j, :], cact[:, 2 * j - 2:2 * j, :], ACT.Silu)\
                        .then_inc(dn_act, 1)
            act.wait_ge(dn_conv, 6)
            nc.scalar.activation(cact[:, 10:12, :], cact[:, 10:12, :], ACT.Silu).then_inc(dn_act, 1)
            act.wait_ge(dn_tok, 6)
            for c in range(2 * DN_H):
                last = nc.scalar.activation(dn["cin"][:, 1024 + P * c:1024 + P * c + P], tok[:, 1, c, :], ACT.Square,
                                            accum_out=d_ss[:, 8 + c:9 + c])
            last.then_inc(dn_sum, 1)
            act.wait_ge(dn_gcd, 1)
            nc.scalar.activation(d_egc, d_gc[:, 0:PAIRS], ACT.Exp).then_inc(dn_egs, 1)
            nc.scalar.activation(d_ekd, d_dm, ACT.Exp).then_inc(dn_egs, 1)
            act.wait_ge(dn_diff, PAIRS)
            nc.scalar.activation(d_E, d_E, ACT.Exp).then_inc(dn_ed, 1)
            for n, (_, dst, b) in enumerate(DN_TURNS):
                if n % 2 == 0:
                    act.wait_ge(dn_fm, n + 1)
                    nc.scalar.activation(dst, ps[b][:, :], ACT.Copy).then_inc(dn_fa, 1)
            for j in range(2):
                name = f"dnz{j}"
                act_step(act, name)
                bank_read(name, nc.scalar.activation(as3(d_sz, TT)[:, :, CW * j:CW * j + CW],
                                                     r3(read_bank(act, name), TT), ACT.Silu))
            for l in range(1, LEVELS):
                for b in range(2):
                    act.wait_ge(dn_p, 2 * l + b + 1)
                    nc.scalar.activation(d_P[:, 512 * b:512 * b + 512], ps[b][:, :], ACT.Copy).then_inc(dn_pc, 1)
            act.wait_ge(dn_u, 2)
            nc.scalar.activation(d_wt, ps[2][:, :], ACT.Copy).then_inc(dn_wc, 1)
            act.wait_ge(dn_o0, 2)
            nc.scalar.activation(d_S, ps[6][:, :], ACT.Copy).then_inc(dn_sc, 1)
            merge_split_high(act, MB + 2, None)
            act_turn(act, "ya")
            act_merge_branch(act, 0)
            with act.Fori(0, NBR - 1) as i:
                act_merge_branch(act, 1, i)
            for n, (a, b, _) in enumerate(MERGED):
                act.wait_ge(mg_add, 4 * NBR - 2 + n)
                if n == 0:
                    act.wait_ge(w_used, TILE["gate311"] + 1)
                nc.scalar.activation(nth[:, a:b, :], r3(mg["m"][:, S * a:S * b], b - a), ACT.Copy)\
                    .then_inc(mg_high, 1)
            for j in range(4):
                name = f"out{j}"
                act_step(act, name)
                bank_read(name, nc.scalar.activation(as3(mg["o"], TT)[:, :, CW * j:CW * j + CW],
                                                     r3(read_bank(act, name), TT), ACT.Copy))
            wait_bank(act, "out2")
            wait_bank(act, "out3")
            act_norm(act, "post")
            act_norm(act, "f0")
            act_turn(act, "f0")
            act_ffn(act, 0)
            act_norm(act, "mx0")
            act_turn(act, "mx0")
            act_step(act, "mlain2")
            for j in range(2):
                name = f"mlain{j}"
                act_step(act, name)
                bank_read(name, nc.scalar.activation(mc[:, :, CW * j:CW * j + CW], r3(read_bank(act, name), TT),
                                                     ACT.Copy))
            wait_bank(act, "mlain0")
            wait_bank(act, "mlain1")
            wait_bank(act, "mlain2")
            for n, (t, c) in enumerate(MLC):
                w = c.stop - c.start
                nc.scalar.activation(xs[:, 0, 0:w] if n % 2 else xs[:, 1, 0:w], mc[:, t, c], ACT.Square,
                                     accum_out=m_ss[:, n:n + 1]).then_inc(ml_ss, 1)
                if n == 1:
                    act.wait_ge(ml_ss, 2)
            act_turn(act, "mlc")
            for j in range(4):
                act_step(act, f"uq{j}")
                for b in range(2):
                    uq_here(act, j, b)
                    h = 4 * j + 2 * b
                    nc.scalar.activation(mq[0:64, h:h + 2, :], r3(ps[2 * (j % 2) + b][0:64, :], 2), ACT.Copy)\
                        .then_inc(ml_qa, 1)
            act_step(act, "uk")
            act.wait_ge(w_used, TILE["uk"] + 1)
            for b in range(4):
                nc.scalar.activation(mk_[0:64, 4 * b:4 * b + 4:2, :], r3(ps[4 + b][0:64, :], 2), ACT.Copy)\
                    .then_inc(ml_ka, 1)
            act_step(act, "uv")
            act.wait_ge(w_used, TILE["uv"] + 1)
            for t in range(TT):
                nc.scalar.activation(as3(ml["v"], TT)[:, t, 0:512], ps[2 * t][:, :], ACT.Copy).then_inc(ml_va, 1)
            act_units(act, MLA0, MLA_H)
            act_turn(act, "mly")
            for j in range(4):
                act_step(act, f"mlao{j}")
            act_norm(act, "f1")
            act_turn(act, "f1")
            act_ffn(act, 1)
            act_norm(act, "f2")
            act.wait_ge(ns_line, 1)
            nc.scalar.activation(nt_["line"][0:NSA_H, :], ps[6][0:NSA_H, :], ACT.Copy, scale=NSA_D ** 0.5)\
                .then_inc(ns_linec, 1)
            act_turn(act, "f2")
            act_ffn(act, 2)
            act_norm(act, "mx1")
            act_turn(act, "mx1")
            act_step(act, "nkc")
            act_step(act, "nvc")
            for j in range(4):
                name = f"nq{j}"
                act_step(act, name)
                bank_read(name, nc.scalar.activation(ns["q"][:, 512 * j:512 * j + 512], read_bank(act, name)[:, :],
                                                     ACT.Copy))
                if j == 0:
                    act_step(act, "ng")
                    bank_read("ng", nc.scalar.activation(n_gt, read_bank(act, "ng")[0:48, 0:S], ACT.Sigmoid))
            act_step(act, "nks")
            act.wait_ge(ns_pos, 2)
            act.wait_ge(ns_hid, 1)
            for m in range(2):
                nc.scalar.activation(n_hid[m][:, 0:NSA_G * NCMP], ps[1][:, 64 * m:64 * m + NSA_G * NCMP],
                                     ACT.Gelu_apprx_tanh, bias=n_pos[:, m:m + 1]).then_inc(ns_hc, 1)
            act_step(act, "nvs")
            bank_read("nvs", nc.scalar.activation(ns["vs"], read_bank(act, "nvs")[:, :], ACT.Copy))
            act_step(act, "nkw")
            for t in range(TT):
                act.wait_ge(ns_cm, t + 1)
                k = min(NCMP, (P * t + P - CMP_L) // CMP_ST + 1)
                nc.scalar.activation(sc[:, t, :, 0:k], sc[:, t, :, 0:k], ACT.Exp, scale=NSA_D ** -0.5)\
                    .then_inc(ns_ce, 1)
            bank_read("nvw", nc.scalar.activation(ns["vw"], read_bank(act, "nvw")[:, :], ACT.Copy))
            act_units(act, NSA0, 2 * NSA_H)
            act_step(act, "nvw")
            act_turn(act, "nsy")
            for j in range(4):
                act_step(act, f"nsao{j}")
            act_norm(act, "f3")
            act_turn(act, "f3")
            act_ffn(act, 3)
            act_norm(act, "final")

        @block.vector
        def _(dve):
            ch = Chain(dve, "dve_chain")
            dve_norm(dve, "mem")
            split_low(dve, 0)
            dve_turn(dve, "mem")
            split_low(dve, 1)
            dve.wait_ge(row_here, 32)
            nc.vector.tensor_scalar(neg_sink, rowof("sink", SW_H), -1.0, None, ALU.mult).then_inc(dn_setup, 1)
            dve_step(dve, "mk0")
            dve_step(dve, "mk1")
            for j in range(2):
                name = f"mv{j}"
                dve_step(dve, name)
                if j == 1:
                    dve_norm(dve, "pre")
                bank_read(name, nc.vector.tensor_copy(as3(xm["v"], TT)[:, :, CW * j:CW * j + CW],
                                                      r3(read_bank(dve, name), TT)))
            dve_turn(dve, "pre")
            for name in ("xmq0", "xmq1", "xmz0", "xmz1"):
                dve_step(dve, name)
            wait_bank(dve, "xmz0")
            wait_bank(dve, "xmz1")
            dve_units(dve, ch, XM0, XM_H, attention_evac(as3(xm["y"], TT), XM0, P, as3(xm["z"], TT)))
            dve_turn(dve, "ym")
            dve_step(dve, "swq0")
            dve_step(dve, "swq1")
            dve_step(dve, "swkv")
            b = read_bank(dve, "swkv")
            dve.wait_ge(zeroed, 1)
            for kv in range(SW_KV):
                for half in range(2):
                    nc.vector.tensor_copy(padded(sw["k"], kv, half)[64 * half:64 * half + 64],
                                          b[64 * kv:64 * kv + 64, 0:S])
            bank_read("swkv", nc.vector.tensor_copy(sw["v"], b[:, S:2 * S]))
            dve_step(dve, "swz0")
            dve_step(dve, "swz1")
            wait_bank(dve, "swz0")
            wait_bank(dve, "swz1")
            dve.wait_ge(dn_setup, 1)
            dve_units(dve, ch, SW0, SW_H, attention_evac(as3(sw["y"], TT), SW0, SW_D, as3(sw["z"], TT)), sinks=True)
            dve_turn(dve, "yc")
            for name in ("gmv0", "gmv1", "gmu0"):
                dve_step(dve, name)
            dve.wait_ge(gm_root, 1)
            for t in range(TT):
                c = slice(512 * t, 512 * t + 512)
                nc.vector.scalar_tensor_tensor(out=gm["v"][:, c], in0=gm["v"][:, c], scalar=gm_rs[:, t:t + 1],
                                               in1=rowof("gmn", 512), op0=ALU.mult, op1=ALU.mult)\
                    .then_inc(gm_vn, 1)
            for name in ("gmu1", "gmz0", "gmz1"):
                dve_step(dve, name)
            for name in ("gmu0", "gmu1", "gmz0", "gmz1"):
                wait_bank(dve, name)
            dve.wait_ge(gm_wturned, 1)
            for g in range(4):
                last = nc.vector.tensor_tensor(pair(gm["wt"], g), pair(ps[0], g), upto, ALU.mult)
            last.then_inc(gm_wmask, 1)
            ch.link(nc.vector.tensor_tensor(gm["u"], gm["u"], gm["z"], ALU.mult))
            dve.wait_ge(gm_mixed, 1)
            bs = r3(rowof("bs", 512), 4)
            for b in range(2):
                for t in range(TT):
                    src = ps[1 + b].rearrange("p (g t c) -> p g t c", g=2, t=TT)[:, :, t, :]
                    dst = gm["sq"].rearrange("p (g t c) -> p g t c", g=4, t=TT)[:, 2 * b:2 * b + 2, t, :]
                    ch.mark(nc.vector.tensor_tensor(dst, src, bs[:, 2 * b:2 * b + 2, :], ALU.add))
            ch.join()
            nc.vector.tensor_tensor(gm["sq"], gm["sq"], gm["u"], ALU.mult).then_inc(gm_y, 1)
            dve.wait_ge(gm_high, 1)
            nc.vector.tensor_tensor(ytl[:, 1], r3(gm["sq"], 4), yth[:, 1].bitcast(F32), ALU.subtract)\
                .then_inc(gm_low, 1)
            dve_step(dve, "ba")
            bank_read("ba", nc.vector.tensor_copy(d_bat, read_bank(dve, "ba")[0:2 * DN_H, 0:S]))
            for j in range(6):
                name = f"dn{j}"
                dve_step(dve, name)
                dve.wait_ge(dn_tap0, j + 1)
                if j == 1:
                    dve.wait_ge(dn_bas, 1)
                    ch.link(nc.vector.tensor_copy(d_ba, ps[3][:, 0:16]))
                    ch.link(nc.vector.tensor_tensor(r3(d_z, TT), r3(d_ba, TT)[:, :, DN_H:2 * DN_H],
                                                    r3(rowof("dtb", PAIRS), TT), ALU.add))
                    nc.vector.scalar_tensor_tensor(out=d_az, in0=d_z, scalar=-1.0, in1=d_z, op0=ALU.mult,
                                                   op1=ALU.max).then_inc(dn_absz, 1)
                if j == 3:
                    dve.wait_ge(dn_exps, 3)
                    ch.link(nc.vector.scalar_tensor_tensor(out=d_sp, in0=d_z, scalar=0.0, in1=d_l, op0=ALU.max,
                                                           op1=ALU.add))
                    ch.link(nc.vector.scalar_tensor_tensor(out=d_g, in0=d_sp, scalar=-1.0, in1=d_ea, op0=ALU.mult,
                                                           op1=ALU.mult))
                for tap in range(1, 4):
                    for c in (2 * j, 2 * j + 1):
                        w = vcol("conv", 12 * tap + c)
                        ins = nc.vector.scalar_tensor_tensor(out=cact[:, c, :], in0=cin[:, c, tap:tap + S],
                                                             scalar=w, in1=cact[:, c, :], op0=ALU.mult,
                                                             op1=ALU.add)
                        if tap == 3 and c % 2:
                            ins.then_inc(dn_conv, 1)
                        else:
                            ch.mark(ins)
                    if tap < 3:
                        ch.join()
            for j in range(6):
                dve.wait_ge(dn_turn, j + 1)
                nc.vector.tensor_copy(tok[:, :, 2 * j:2 * j + 2, :],
                                      ps[j % 4].rearrange("p (t c d) -> p t c d", t=TT, c=2)).then_inc(dn_tok, 1)
            nc.vector.tensor_copy(r3(d_Lm, PAIRS), bc(d_g, P)).then_inc(dn_g, 1)
            dve.wait_ge(dn_tok, 6)
            sqb = dn["cin"][:, 0:2048].rearrange("p (t c d) -> p t c d", t=TT, c=2 * DN_H)
            ch.link(nc.vector.tensor_tensor(sqb[:, 0], tok[:, 0, 0:8, :], tok[:, 0, 0:8, :], ALU.mult))
            nc.vector.tensor_reduce(d_ss[:, 0:8], sqb[:, 0], AX.X, ALU.add).then_inc(dn_sum, 1)
            dve.wait_ge(dn_gcs, 1)
            ch.link(nc.vector.tensor_copy(d_gc, ps[0][:, 0:16]))
            nc.vector.tensor_tensor(d_dm, d_gc[:, 8:16], d_gc[:, 0:8], ALU.subtract).then_inc(dn_gcd, 1)
            for n in range(PAIRS):
                nc.vector.scalar_tensor_tensor(out=pair(d_E, n), in0=pair(ps[1 + n // 4], n % 4),
                                               scalar=d_gc[:, n:n + 1], in1=upto, op0=ALU.subtract, op1=ALU.mult)\
                    .then_inc(dn_diff, 1)
            dve.wait_ge(dn_root, 1)
            rs = r3(d_rs, TT)
            ch.link(nc.vector.tensor_scalar(rs[:, :, 0:DN_H], rs[:, :, 0:DN_H], float(P) ** -0.5, None, ALU.mult))
            for t in range(TT):
                ch.mark(nc.vector.tensor_tensor(tok[:, t, 0:8, :], tok[:, t, 0:8, :], bc(d_rs[:, 8 * t:8 * t + 8], P),
                                                ALU.mult))
            for t in range(TT):
                ch.mark(nc.vector.tensor_tensor(tok[:, t, 8:12, :], tok[:, t, 8:12, :],
                                                bc(d_beta[:, 4 * t:4 * t + 4], P), ALU.mult))
            ch.join()
            kb = heads(dn["kb"])
            for t in range(TT):
                ch.mark(nc.vector.tensor_tensor(kb[:, t], tok[:, t, 4:8, :], bc(d_beta[:, 4 * t:4 * t + 4], P),
                                                ALU.mult))
            ch.join()
            dve.wait_ge(dn_egs, 2)
            nc.vector.tensor_tensor(r3(dn["rw"], 4), kb[:, 1], bc(d_egc[:, 4:8], P), ALU.mult)
            nc.vector.tensor_tensor(r3(dn["kd"], 4), tok[:, 0, 4:8, :], bc(d_ekd[:, 0:4], P), ALU.mult)
            nc.vector.tensor_tensor(r3(d_qg, 4), tok[:, 1, 0:4, :], bc(d_egc[:, 4:8], P), ALU.mult)\
                .then_inc(dn_ready, 1)
            dve.wait_ge(dn_ed, 1)
            ch.link(nc.vector.tensor_tensor(r3(d_E, PAIRS), r3(d_E, PAIRS), rep(upto, PAIRS), ALU.mult))
            ch.mark(nc.vector.tensor_tensor(r3(d_Es, PAIRS), r3(d_E, PAIRS), rep(before, PAIRS), ALU.mult))
            for n, (_, dst, b) in enumerate(DN_TURNS):
                if n % 2:
                    dve.wait_ge(dn_fm, n + 1)
                    nc.vector.tensor_copy(dst, ps[b][:, :]).then_inc(dn_fd, 1)
            dve_step(dve, "dnz0")
            dve.wait_ge(dn_kk, 2)
            ch.join()
            for b in range(2):
                c = slice(512 * b, 512 * b + 512)
                ch.mark(nc.vector.tensor_tensor(d_L[:, c], ps[1 + b][:, :], d_Es[:, c], ALU.mult))
            for b in range(2):
                c = slice(512 * b, 512 * b + 512)
                nc.vector.tensor_tensor(d_A[:, c], ps[(3, 6)[b]][:, :], d_E[:, c], ALU.mult).then_inc(dn_la, 1)
            ch.join()
            dve.wait_ge(dn_la, 2)
            dve.wait_ge(dn_level, 16)

            def mask_level(l):
                for b in range(2):
                    if l >= 2:
                        dve.wait_ge(dn_p, 2 * (l - 2) + b + 1)
                    c = slice(512 * b, 512 * b + 512)
                    nc.vector.tensor_tensor(r3(d_Lms[l % 2][:, c], 4), r3(d_L[:, c], 4),
                                            rep(d_level[:, l, :], 4), ALU.mult).then_inc(dn_lm, 1)

            mask_level(0)
            dve.wait_ge(dn_lm, 2)
            ch.mark(nc.vector.tensor_tensor(r3(d_TT, PAIRS), rep(ident, PAIRS), r3(d_Lms[0], PAIRS), ALU.subtract))
            mask_level(1)
            ch.join()
            for b in range(2):
                dve.wait_ge(dn_p, b + 1)
                nc.vector.tensor_tensor(r3(d_T[:, 512 * b:512 * b + 512], 4), rep(ident, 4), r3(ps[b][:, :], 4),
                                        ALU.subtract).then_inc(dn_t, 1)
            for l in range(1, LEVELS):
                if l + 1 < LEVELS:
                    mask_level(l + 1)
                for b in range(2):
                    c = slice(512 * b, 512 * b + 512)
                    dve.wait_ge(dn_y, 2 * (l - 1) + b + 1)
                    if l < LEVELS - 1:
                        nc.vector.tensor_tensor(d_T[:, c], d_T[:, c], ps[2 + b][:, :], ALU.subtract)
                    nc.vector.tensor_tensor(d_TT[:, c], d_TT[:, c], ps[6 + b][:, :], ALU.subtract)\
                        .then_inc(dn_t, 1)
                dve.wait_ge(dn_t, 2 * l + 2)
            dve_step(dve, "dnz1")
            dve.wait_ge(dn_u, 1)
            for b in range(2):
                nc.vector.tensor_copy(d_u[:, 512 * b:512 * b + 512], ps[b][:, :]).then_inc(dn_uc, 1)
            dve.wait_ge(dn_ws, 1)
            dve.wait_ge(dn_uc, 2)
            nc.vector.tensor_tensor(d_vn, d_u[:, 512:1024], ps[7][:, :], ALU.subtract).then_inc(dn_vnd, 1)
            o = dn["kt"]
            ch.mark(nc.vector.tensor_copy(o[:, 0:512], ps[3][:, :]))
            dve.wait_ge(dn_o1, 1)
            ch.mark(nc.vector.tensor_copy(o[:, 512:1024], ps[0][:, :]))
            ch.join()
            ch.link(nc.vector.tensor_tensor(d_P, o, o, ALU.mult))
            nc.vector.tensor_reduce(d_os, r3(d_P, PAIRS), AX.X, ALU.add).then_inc(dn_osum, 1)
            merge_split_low(dve, MB + 2, None)
            dve.wait_ge(dn_oroot, 1)
            ch.link(nc.vector.tensor_tensor(r3(o, PAIRS), r3(o, PAIRS), bc(d_or, P), ALU.mult))
            ch.link(nc.vector.tensor_tensor(r3(o, PAIRS), r3(o, PAIRS), rep(rowof("onorm", P), PAIRS), ALU.mult))
            wait_bank(dve, "dnz0")
            wait_bank(dve, "dnz1")
            nc.vector.tensor_tensor(o, o, d_sz, ALU.mult).then_inc(dn_out, 1)
            dve_turn(dve, "ya")
            dve_merge_branch(dve, 0)
            with dve.Fori(0, NBR - 1) as i:
                dve_merge_branch(dve, 1, i)
            for n, (a, b, _) in enumerate(MERGED):
                dve.wait_ge(mg_high, n + 1)
                nc.vector.tensor_tensor(ntl[:, a:b, :], r3(mg["m"][:, S * a:S * b], b - a),
                                        nth[:, a:b, :].bitcast(F32), ALU.subtract).then_inc(mg_low, 1)
            for j in range(4):
                dve_step(dve, f"out{j}")
            dve.wait_ge(mg_post, 16)
            for t in range(TT):
                dve_norm(dve, "post", mg["post"], (t,))
                dve.wait_ge(norm_scaled, TT * NORMS.index("post") + t + 1)
                nc.vector.tensor_tensor(x[:, t, :], x[:, t, :], xs[:, t, :], ALU.add).then_inc(x_ready, 1)
            dve_norm(dve, "f0")
            dve_turn(dve, "f0")
            dve_ffn(dve, 0)
            dve_norm(dve, "mx0")
            dve_turn(dve, "mx0")
            def rotate(bank, n, dst):
                a = mrot[:, 0:n * S]
                ch.link(nc.vector.tensor_tensor(r3(a, n)[64:128], r3(bank, n)[64:128], rep(rope_[64:128], n),
                                                ALU.mult))
                return nc.vector.tensor_tensor(dst, r3(a, n)[64:96], r3(a, n)[96:128], ALU.add)

            dve_step(dve, "mlain2")
            bank = read_bank(dve, "mlain2")
            ch.link(rotate(bank[:, S:2 * S], 1, r3(mlc["kr"][64:96, 0:S], 1)))
            bank_read("mlain2", nc.vector.tensor_copy(mc[:, :, 2 * CW:2 * CW + P], r3(bank[:, 0:S], TT)))
            dve_step(dve, "mlain0")
            nc.vector.tensor_copy(mk_[64:96, :, :], rep(mlc["kr"][64:96, 0:S], MLA_H)).then_inc(ml_krd, 1)
            dve_step(dve, "mlain1")
            for n, (t, c) in enumerate(MLC):
                dve.wait_ge(ml_rs, n // TT + 1)
                nc.vector.tensor_scalar(mc[:, t, c], mc[:, t, c], m_rs[:, n:n + 1], None, ALU.mult).then_inc(ml_cs, 1)
            dve_turn(dve, "mlc")
            for j in range(4):
                dve_step(dve, f"uq{j}")
                for b in range(2):
                    uq_here(dve, j, b)
                    if j + b:
                        dve.wait_ge(ml_qd, 2 * j + b)
                    h = 4 * j + 2 * b
                    rotate(ps[2 * (j % 2) + b], 2, mq[64:96, h:h + 2, :]).then_inc(ml_qd, 1)
            dve_step(dve, "uk")
            dve.wait_ge(w_used, TILE["uk"] + 1)
            for b in range(4):
                nc.vector.tensor_copy(mk_[0:64, 4 * b + 1:4 * b + 4:2, :], r3(ps[4 + b][64:128, :], 2))\
                    .then_inc(ml_kd, 1)
            dve_step(dve, "uv")
            dve.wait_ge(w_used, TILE["uv"] + 1)
            for t in range(TT):
                nc.vector.tensor_copy(as3(ml["v"], TT)[:, t, 512:1024], ps[2 * t + 1][:, :]).then_inc(ml_vd, 1)
            dve_units(dve, ch, MLA0, MLA_H, attention_evac(as3(ml["y"], TT), MLA0, MLA_V))
            dve_turn(dve, "mly")

            def add_to_x(names):
                for j, name in enumerate(names):
                    dve_step(dve, name)
                    xo = x[:, :, CW * j:CW * j + CW]
                    bank_read(name, nc.vector.tensor_tensor(xo, xo, r3(read_bank(dve, name), TT), ALU.add))
                wait_bank(dve, names[-2])
                wait_bank(dve, names[-1])
                nc.vector.tensor_copy(mark_col, one_col).then_inc(x_ready, TT)

            add_to_x([f"mlao{j}" for j in range(4)])
            dve_norm(dve, "f1")
            dve_turn(dve, "f1")
            dve_ffn(dve, 1)
            dve_norm(dve, "f2")
            dve.wait_ge(ns_posed, 1)
            nc.vector.tensor_copy(n_pos[:, 0:1], ps[5][:, 0:1]).then_inc(ns_pos, 1)
            dve_turn(dve, "f2")
            dve_ffn(dve, 2)
            dve_norm(dve, "mx1")
            dve.wait_ge(ns_posed, 2)
            nc.vector.tensor_copy(n_pos[:, 1:2], ps[5][:, 1:2]).then_inc(ns_pos, 1)
            dve_turn(dve, "mx1")
            for m, name in enumerate(("nkc", "nvc")):
                dve_step(dve, name)
                src = r3(read_bank(dve, name), 2)
                dst = xx[m].rearrange("p (c two) s -> p two c s", two=2)
                for g in range(2):
                    nc.vector.tensor_copy(dst[0:64, g], src[64 * g:64 * g + 64])
                    ins = nc.vector.tensor_copy(dst[64:128, g, :, 0:S - 1], src[64 * g:64 * g + 64, :, 1:S])
                bank_read(name, ins)
            for name in ("nq0", "ng", "nq1", "nq2", "nq3"):
                dve_step(dve, name)

            def double_keys(name, dst):
                for o_, i_ in doubled(dst, read_bank(dve, name), NSA_G):
                    ins = nc.vector.tensor_copy(o_, i_)
                bank_read(name, ins)

            dve_step(dve, "nks")
            dve.wait_ge(zeroed, 2)
            double_keys("nks", ns["ks"])
            dve_step(dve, "nvs")
            dve.wait_ge(ns_kc, 1)
            dve.wait_ge(ns_zero, 1)
            kc_ = r3(ps[2][0:64, 0:NSA_G * NCMP], NSA_G)
            nc.vector.tensor_copy(kc2[0:64, :, 0, :], kc_)
            nc.vector.tensor_copy(kc2[64:128, :, 1, :], kc_).then_inc(ns_kcd, 1)
            dve.wait_ge(ns_vc, 1)
            dve.wait_ge(ns_zero, 1)
            for r in range(NSA_R):
                ins = nc.vector.tensor_copy(vcd[32 * r:32 * r + NCMP, :, 64 * r:64 * r + 64],
                                            r3(ps[3][32 * r:32 * r + NCMP, 0:NSA_G * 64], NSA_G))
            ins.then_inc(ns_vcd, 1)
            dve.wait_ge(ns_cs, 1)
            dve.wait_ge(ns_bias, 16)
            dve.wait_ge(ns_zero, 2)
            got = ps[7].rearrange("p (t h n) -> p t h n", t=TT, h=NSA_H)
            for t in range(TT):
                c = slice(NSA_H * t, NSA_H * t + NSA_H)
                end = P * t + P - CMP_L
                k = min(NCMP, end // CMP_ST + 1)
                st = sc[:, t, :, 0:k]
                bias = nbias[:, :, end - CMP_ST * (k - 1):end + 1:CMP_ST][:, :, ::-1]
                ch.link(nc.vector.tensor_tensor(st, got[:, t, :, 0:k], bias, ALU.add))
                ch.link(nc.vector.tensor_reduce(n_mx[:, c], st, AX.X, ALU.max))
                nc.vector.tensor_tensor(st, st, bc(n_mx[:, c], k), ALU.subtract).then_inc(ns_cm, 1)
            dve_step(dve, "nkw")
            dve.wait_ge(ns_gt, 1)
            ch.link(nc.vector.tensor_copy(n_gate, ps[6][:, 0:TT * 48]))
            for t in range(TT):
                c = slice(NSA_H * t, NSA_H * t + NSA_H)
                dve.wait_ge(ns_ce, t + 1)
                k = min(NCMP, (P * t + P - CMP_L) // CMP_ST + 1)
                ch.link(nc.vector.tensor_reduce(n_sum[:, c], sc[:, t, :, 0:k], AX.X, ALU.add))
                ch.link(nc.vector.reciprocal(n_inv[:, c], n_sum[:, c]))
                ok = con[:, CON["rowok"] + t:CON["rowok"] + t + 1]
                ch.link(nc.vector.scalar_tensor_tensor(out=n_cg[:, c], in0=n_inv[:, c], scalar=ok,
                                                       in1=gate3[:, t, :, 0], op0=ALU.mult, op1=ALU.mult))
            for b in range(2):
                dve.wait_ge(ns_ct, b + 1)
                nc.vector.tensor_copy(sct[:, 512 * b:512 * b + 512], ps[b][:, :]).then_inc(ns_ctc, 1)
            dve.wait_ge(zeroed, 3)
            double_keys("nkw", ns["kw"])
            for t in range(TT):
                for half in range(2):
                    n = 2 * t + half
                    dve.wait_ge(ns_co, n + 1)
                    h0 = 8 * half
                    nc.vector.tensor_tensor(
                        ny[:, t, 512 * half:512 * half + 512].rearrange("p (h d) -> p h d", h=8),
                        r3(ps[(2, 3, 6, 7)[n]], 8), bc(n_cg[:, NSA_H * t + h0:NSA_H * t + h0 + 8], 64), ALU.mult)\
                        .then_inc(ns_cy, 1)
            dve.wait_ge(ns_cy, 4)
            dve.wait_ge(ns_bias, 16)

            def nsa_evac(a, o, inv):
                h, branch = (a - NSA0) % NSA_H, 1 + (a - NSA0) // NSA_H
                ch.link(nc.vector.tensor_tensor(n_ag[a % 2], inv, gate3[:, :, h, branch], ALU.mult))
                if a - NSA0 >= NSA_H:
                    dve.wait_ge(at_read, a - NSA_H + 1)
                for t in range(TT):
                    yo = ny[:, t, 64 * h:64 * h + 64]
                    last = nc.vector.scalar_tensor_tensor(out=yo, in0=o[:, 64 * t:64 * t + 64],
                                                          scalar=n_ag[a % 2][:, t:t + 1], in1=yo, op0=ALU.mult,
                                                          op1=ALU.add)
                return last

            dve_units(dve, ch, NSA0, 2 * NSA_H, nsa_evac)
            dve_step(dve, "nvw")
            dve_turn(dve, "nsy")
            add_to_x([f"nsao{j}" for j in range(4)])
            dve_norm(dve, "f3")
            dve_turn(dve, "f3")
            dve_ffn(dve, 3)
            dve.wait_ge(mg_post, 32)
            dve_norm(dve, "final", scr[:, 4096:4096 + D])

        @block.tensor
        def _(pe):
            pe.wait_ge(ident_here, 32)
            pe_norm(pe, "mem")
            pe_plain(pe, "mk0", "F", "mem")
            pe_plain(pe, "mk1", "F")
            pe_plain(pe, "mv0", "T")
            pe_plain(pe, "mv1", "T")
            pe_norm(pe, "pre")
            pe_plain(pe, "xmq0", "F", "pre")
            for name, kind in (("xmq1", "F"), ("xmz0", "T"), ("xmz1", "T")):
                pe_plain(pe, name, kind)
            for name in ("mk0", "mk1", "mv0", "mv1", "xmq0", "xmq1"):
                wait_bank(pe, name)
            pe_units(pe, XM0, XM_H)
            pe.wait_ge(at_read, XM0 + XM_H)
            pe_turn(pe, "ym")
            for name, kind in (("swq0", "F"), ("swq1", "F"), ("swkv", "FT"), ("swz0", "T"), ("swz1", "T")):
                pe_plain(pe, name, kind)
            for name in ("swq0", "swq1", "swkv"):
                wait_bank(pe, name)
            pe.wait_ge(turn_low, turn_done("ym"))
            pe_units(pe, SW0, SW_H)
            pe.wait_ge(at_read, SW0 + SW_H)
            pe_turn(pe, "yc")
            for name, kind in (("gmv0", "T"), ("gmv1", "T"), ("gmu0", "F"), ("gmu1", "F"), ("gmz0", "F"),
                               ("gmz1", "F")):
                pe_plain(pe, name, kind)
            pe.wait_ge(gm_loaded, 16)
            pe.wait_ge(turn_low, turn_done("yc"))
            for g in range(4):
                last = nc.tensor.transpose(pair(ps[0], g), pair(gm["w"], g), ident)
            last.then_inc(gm_wturned, 1)
            pe.wait_ge(gm_wmask, 1)
            pe.wait_ge(gm_vn, TT)
            for g in range(4):
                for t in range(TT):
                    at = 256 * (g % 2) + P * t
                    last = nc.tensor.matmul(ps[1 + g // 2][:, at:at + P], gm["v"][:, 512 * t + P * g:512 * t + P * g + P],
                                            pair(gm["wt"], g), start=True, stop=True)
            last.then_inc(gm_mixed, 1)
            pe_plain(pe, "ba", "N")
            for j in range(6):
                pe_plain(pe, f"dn{j}", "F")
                if j == 0:
                    wait_bank(pe, "ba")
                    for t in range(TT):
                        last = nc.tensor.transpose(ps[3][:, 8 * t:8 * t + 8], d_bat[:, P * t:P * t + P],
                                                   ident[0:2 * DN_H, 0:2 * DN_H])
                    last.then_inc(dn_bas, 1)
            pe.wait_ge(gm_low, 1)
            for j in range(6):
                pe.wait_ge(dn_act, j + 1)
                if j >= 4:
                    pe.wait_ge(dn_tok, j - 3)
                for t in range(TT):
                    for c in range(2):
                        at = 256 * t + P * c
                        last = nc.tensor.transpose(ps[j % 4][:, at:at + P], cact[:, 2 * j + c, P * t:P * t + P], ident)
                last.then_inc(dn_turn, 1)
            pe.wait_ge(dn_g, 1)
            pe.wait_ge(dn_tok, 6)
            nc.tensor.matmul(ps[0][:, 0:8], upto, d_g, start=True, stop=True)
            nc.tensor.matmul(ps[0][:, 8:16], ones, d_g, start=True, stop=True)
            for n in range(PAIRS):
                last = nc.tensor.matmul(pair(ps[1 + n // 4], n % 4), pair(d_Lm, n), upto, start=True, stop=True)
            last.then_inc(dn_gcs, 1)
            pe_plain(pe, "dnz0", "T")
            pe_plain(pe, "dnz1", "T")
            pe.wait_ge(dn_ready, 1)
            for n, (src, _, b) in enumerate(DN_TURNS):
                if n == 1:
                    pe.wait_ge(dn_diff, PAIRS)
                if n == 6:
                    pe.wait_ge(dn_fa, 1)
                for h in range(DN_H):
                    last = nc.tensor.transpose(pair(ps[b], h), src[h], ident)
                last.then_inc(dn_fm, 1)
            pe.wait_ge(dn_fa, 4)
            pe.wait_ge(dn_fd, 3)
            for rhs, banks in ((d_kbt, (1, 2)), (dn["qt"], (3, 6))):
                for n in range(PAIRS):
                    last = nc.tensor.matmul(pair(ps[banks[n // 4]], n % 4), pair(dn["kt"], n), pair(rhs, n),
                                            start=True, stop=True)
                last.then_inc(dn_kk, 1)
            pe.wait_ge(dn_la, 2)
            for l in range(LEVELS):
                for b in range(2):
                    pe.wait_ge(dn_lm, 2 * l + b + 1)
                    if l:
                        pe.wait_ge(dn_t, 2 * l + b - 1)
                    for n in range(4 * b, 4 * b + 4):
                        last = nc.tensor.matmul(pair(ps[b], n % 4), pair(d_Lms[l % 2], n),
                                                pair(d_T, n) if l else ident, start=True, stop=True)
                    last.then_inc(dn_p, 1)
                if l == 0:
                    continue
                for b in range(2):
                    pe.wait_ge(dn_pc, 2 * l + b - 1)
                    for n in range(4 * b, 4 * b + 4):
                        last = nc.tensor.matmul(pair(ps[6 + b], n % 4), pair(d_P, n), pair(d_TT, n), start=True,
                                                stop=True)
                    if l < LEVELS - 1:
                        for n in range(4 * b, 4 * b + 4):
                            last = nc.tensor.matmul(pair(ps[2 + b], n % 4), pair(d_TT, n), pair(d_P, n),
                                                    start=True, stop=True)
                    last.then_inc(dn_y, 1)
            pe.wait_ge(dn_t, 2 * LEVELS)
            for n in range(PAIRS):
                last = nc.tensor.matmul(pair(ps[n // 4], n % 4), pair(d_TT, n), tok[:, n // 4, 8 + n % 4, :],
                                        start=True, stop=True)
            last.then_inc(dn_u, 1)
            for h in range(DN_H):
                last = nc.tensor.matmul(pair(ps[2], h), pair(dn["rw"], h), pair(d_TT, 4 + h), start=True, stop=True)
            last.then_inc(dn_u, 1)
            pe.wait_ge(dn_uc, 1)
            for h in range(DN_H):
                last = nc.tensor.matmul(pair(ps[3], h), pair(d_A, h), pair(d_u, h), start=True, stop=True)
            last.then_inc(dn_o0, 1)
            for h in range(DN_H):
                last = nc.tensor.matmul(pair(ps[6], h), pair(dn["kd"], h), pair(d_u, h), start=True, stop=True)
            last.then_inc(dn_o0, 1)
            pe.wait_ge(dn_sc, 1)
            pe.wait_ge(dn_wc, 1)
            for h in range(DN_H):
                last = nc.tensor.matmul(pair(ps[7], h), pair(d_wt, h), pair(d_S, h), start=True, stop=True)
            last.then_inc(dn_ws, 1)
            pe.wait_ge(dn_vnd, 1)
            for h in range(DN_H):
                nc.tensor.matmul(pair(ps[0], h), pair(dn["qgt"], h), pair(d_S, h), start=True, stop=False,
                                 skip_group_check=True)
                last = nc.tensor.matmul(pair(ps[0], h), pair(d_A, 4 + h), pair(d_vn, h), start=False, stop=True,
                                        skip_group_check=True)
            last.then_inc(dn_o1, 1)
            wait_bank(pe, "dnz0")
            wait_bank(pe, "dnz1")
            pe_merge_gates(pe, 0, 0)
            pe.wait_ge(dn_out, 1)
            pe_turn(pe, "ya")
            pe.wait_ge(turn_low, turn_done("ya"))
            pe_merge_up(pe, 0, 0)
            pe_merge_gates(pe, 0, 1)
            pe_merge_up(pe, 0, 1)
            with pe.Fori(0, NBR - 1) as i:
                for half in range(2):
                    pe_merge_gates(pe, 1, half, i)
                    pe_merge_up(pe, 1, half, i)
            pe.wait_ge(mg_sig, 4 * NBR)
            for j in range(4):
                pe_plain(pe, f"out{j}", "T", {a: (mg_low, n) for a, _, n in MERGED} if j == 0 else None)
            pe_norm(pe, "f0")
            pe_ffn(pe, 0)
            pe_norm(pe, "mx0")
            pe_plain(pe, "mlain2", "TF", "mx0")
            pe_plain(pe, "mlain0", "T")
            pe_plain(pe, "mlain1", "T")
            pe_turn(pe, "mlc", {0: (ml_cs, TT), 1: (ml_cs, 2 * TT)})
            for j in range(4):
                t = TILE[f"uq{j}"]
                weights_here(pe, t)
                if j == 1:
                    pe.wait_ge(turn_low, turn_done("mlc"))
                for b in range(2):
                    if j >= 2:
                        pe.wait_ge(ml_qa, 2 * (j - 2) + b + 1)
                        pe.wait_ge(ml_qd, 2 * (j - 2) + b + 1)
                    for c in range(2):
                        last = by_feature(ps[2 * (j % 2) + b][:, S * c:S * c + S], slot(t, 3, 512), P * (2 * b + c),
                                          NT_, 3, 0, pe, None if j + b + c else "mlc")
                    last.then_inc(w_used if b else ml_q, 1)
            for name in ("mlain2", "mlain0", "mlain1"):
                wait_bank(pe, name)
            t = TILE["uk"]
            weights_here(pe, t)
            for c in range(8):
                last = by_feature(ps[4 + c // 2][:, S * (c % 2):S * (c % 2) + S], slot(t, 2, D), P * c, NT_, 2, 3)
            last.then_inc(w_used, 1)
            t = TILE["uv"]
            weights_here(pe, t)
            pe.wait_ge(ml_qa, 8)
            pe.wait_ge(ml_qd, 8)
            for n in range(4):
                last = by_token(ps[n][:, :], slot(t, 2, D), 512 * (n % 2), 512, NT_, 2, n // 2, 3)
            last.then_inc(w_used, 1)
            pe.wait_ge(ml_va, 2)
            pe.wait_ge(ml_vd, 2)
            pe.wait_ge(ml_ka, 4)
            pe.wait_ge(ml_kd, 4)
            pe.wait_ge(ml_krd, 1)
            pe.wait_ge(ml_zero, 1)
            pe_units(pe, MLA0, MLA_H)
            pe.wait_ge(at_read, MLA0 + MLA_H)
            pe_turn(pe, "mly")
            for j in range(4):
                pe_plain(pe, f"mlao{j}", "T", None if j else "mly")
            pe_norm(pe, "f1")
            pe_ffn(pe, 1)
            def position_part(m):
                for j in range(CMP_L // 2):
                    last = nc.tensor.matmul(ps[5][:, m:m + 1], w1s[:, m, j, :], poss[:, m, j:j + 1], start=j == 0,
                                            stop=j == CMP_L // 2 - 1)
                last.then_inc(ns_posed, 1)

            pe.wait_ge(ns_tbl, 32)
            pe.wait_ge(ns_w1, 48)
            tbl = nt_["tbl"][0:BIAS_ROWS, 0:NSA_H]
            nc.tensor.matmul(ps[6][0:NSA_H, :], tbl, nt_["hot"][0:BIAS_ROWS, :], start=True, stop=True)\
                .then_inc(ns_line, 1)
            pe.wait_ge(ff_h, 2 * FT)
            position_part(0)
            pe_norm(pe, "f2")
            pe.wait_ge(ns_pos, 1)
            pe_ffn(pe, 2)
            pe.wait_ge(ff_h, 3 * FT)
            position_part(1)
            pe_norm(pe, "mx1")
            pe.wait_ge(ns_pos, 2)
            pe_plain(pe, "nkc", "F", "mx1")
            for name in ("nvc", "nq0", "ng", "nq1", "nq2", "nq3"):
                pe_plain(pe, name, "N" if name == "ng" else "F")
            wait_bank(pe, "ng")
            for t in range(TT):
                last = nc.tensor.transpose(ps[6][:, 48 * t:48 * t + 48], n_gt[:, P * t:P * t + P],
                                           ident[0:48, 0:48])
            last.then_inc(ns_gt, 1)
            wait_bank(pe, "nkc")
            wait_bank(pe, "nvc")
            for m in range(2):
                for j in range(CMP_L // 2):
                    blocks = xx[m][:, :, 2 * j:2 * j + CMP_ST * (NCMP - 1) + 1:CMP_ST]
                    last = nc.tensor.matmul(ps[1][:, 64 * m:64 * m + NSA_G * NCMP], w1s[:, m, j, :], blocks,
                                            start=j == 0, stop=j == CMP_L // 2 - 1)
            last.then_inc(ns_hid, 1)
            pe_plain(pe, "nks", "F")
            pe.wait_ge(ns_hc, 2)
            nc.tensor.matmul(ps[2][0:64, 0:NSA_G * NCMP], w2s[:, 0, :], n_hid[0][:, 0:NSA_G * NCMP], start=True,
                             stop=True).then_inc(ns_kc, 1)
            for r in range(NSA_R):
                for g in range(NSA_G):
                    last = nc.tensor.matmul(ps[3][32 * r:32 * r + NCMP, 64 * g:64 * g + 64],
                                            n_hid[1][:, NCMP * g:NCMP * g + NCMP], w2s[:, 1, :], start=True, stop=True)
            last.then_inc(ns_vc, 1)
            pe_plain(pe, "nvs", "T")
            pe.wait_ge(ns_kcd, 1)
            pe.wait_ge(ns_linec, 1)
            for name in ("nq2", "nq3"):
                wait_bank(pe, name)
            for t in range(TT):
                for c in range(NSA_H // 2):
                    at = 256 * t + 32 * c
                    last = nc.tensor.matmul(r3(ps[7][:, at:at + 32], 2)[:, :, 0:NCMP],
                                            ns["q"][:, S * c + P * t:S * c + P * t + P],
                                            kc2[:, c // (NSA_R // 2)], start=True, stop=True)
            last.then_inc(ns_cs, 1)
            pe_plain(pe, "nkw", "F")
            for t in range(TT):
                pe.wait_ge(ns_ce, t + 1)
                if t == 0:
                    pe.wait_ge(ns_pos, 1)
                for g in range(NSA_G):
                    last = nc.tensor.transpose(pair(ps[t], g), xs[:, 0, 512 * t + P * g:512 * t + P * g + P], ident)
                last.then_inc(ns_ct, 1)
            pe.wait_ge(ns_vcd, 1)
            for t in range(TT):
                pe.wait_ge(ns_ctc, t + 1)
                for half in range(2):
                    for gg in range(2):
                        g = 2 * half + gg
                        last = nc.tensor.matmul(ps[(2, 3, 6, 7)[2 * t + half]][:, 256 * gg:256 * gg + 256],
                                                sct[:, 512 * t + P * g:512 * t + P * g + P], vcd[:, g, :], start=True,
                                                stop=True)
                    last.then_inc(ns_co, 1)
            pe_plain(pe, "nvw", "T")
            for name in ("nks", "nvs", "nkw", "nvw"):
                wait_bank(pe, name)
            pe.wait_ge(ns_cy, 4)
            pe_units(pe, NSA0, 2 * NSA_H)
            pe.wait_ge(at_read, NSA0 + 2 * NSA_H)
            pe_turn(pe, "nsy")
            for j in range(4):
                pe_plain(pe, f"nsao{j}", "T", None if j else "nsy")
            pe_norm(pe, "f3")
            pe_ffn(pe, 3)


def kernel(**inputs):
    import concourse.bacc as bacc
    from concourse.bass_utils import run_bass_kernel_spmd as run

    arrays = lay_out({k: np.asarray(v) for k, v in inputs.items()})
    nc = bacc.Bacc("TRN2", target_bir_lowering=False, num_devices=1)
    A = {k: nc.dram_tensor(f"in_{k}", v.shape, F32, kind="ExternalInput").ap() for k, v in arrays.items()}
    out = nc.dram_tensor("out", (P, TT, D), F32, kind="ExternalOutput").ap()
    build(nc, A, out)
    r = run(nc, [{f"in_{k}": v for k, v in arrays.items()}], core_ids=[0])
    y = r.results[0]["out"]
    return np.ascontiguousarray(np.asarray(y).transpose(1, 0, 2)).reshape(1, S, D)
```
